# Optimizing a Trainium2 kernel written in Bass

```python
import jax, jax.numpy as jnp
from jax import lax
import numpy as np

D_MODEL = 1024
BATCH = 1
SEQ = 1024
DEPTH = 1
DEC_BATCH = 1
DEC_SEQ = 64
PAST_LEN = 128

CHUNK = 64
N_MEM = 256
N_BRANCHES = 3
A_HEADS = 6
A_KV_HEADS = 2
HEAD_DIM = 128
ROT_DIM = HEAD_DIM // 4
IDX_HEADS = 8
IDX_DIM = 64
IDX_ROT_DIM = IDX_DIM // 4
TOPK_MAX = 256
Q_BLOCK = 128
B_HEADS = 6
B_KEY_DIM = 128
B_VAL_DIM = 128
C_HEADS = 4
C_HEAD_DIM = 128

A_WIDTH = A_HEADS * HEAD_DIM
B_WIDTH = B_HEADS * B_VAL_DIM
C_WIDTH = C_HEADS * C_HEAD_DIM
D_FF = 4 * D_MODEL
ROPE_THETA = 500000.0
EPS = 1e-6

IN_WIDTHS = (
    A_HEADS * HEAD_DIM,
    A_KV_HEADS * HEAD_DIM,
    A_KV_HEADS * HEAD_DIM,
    IDX_HEADS * IDX_DIM,
    IDX_DIM,
    IDX_HEADS,
    B_HEADS * B_KEY_DIM,
    B_HEADS * B_KEY_DIM,
    B_HEADS * B_VAL_DIM,
    B_HEADS * B_VAL_DIM,
    C_WIDTH,
    N_BRANCHES * D_MODEL,
)
IN_WIDTH = sum(IN_WIDTHS)

kernel_name = "dsa_hgrn2_memory_gated_streaming_encoder_step"

def rms_norm(x, gain):
    xf = x.astype(jnp.float32)
    y = xf * lax.rsqrt(jnp.mean(xf * xf, axis=-1, keepdims=True) + EPS)
    return (y * gain.astype(jnp.float32)).astype(x.dtype)

def partial_rope(x, pos, rot_dim):
    half = rot_dim // 2
    inv_freq = ROPE_THETA ** (-jnp.arange(half, dtype=jnp.float32) / half)
    ang = pos.astype(jnp.float32)[:, None] * inv_freq[None, :]
    cos = jnp.cos(ang)[:, None, :]
    sin = jnp.sin(ang)[:, None, :]
    xr = x[..., :rot_dim].astype(jnp.float32)
    x1, x2 = xr[..., :half], xr[..., half:]
    rot = jnp.concatenate([x1 * cos - x2 * sin, x2 * cos + x1 * sin], axis=-1)
    return jnp.concatenate([rot.astype(x.dtype), x[..., rot_dim:]], axis=-1)

def split_projection(h, w_in, pos):
    bsz, t = h.shape[:2]
    points = [int(s) for s in np.cumsum(IN_WIDTHS)[:-1]]
    a_q, a_k, a_v, i_q, i_k, i_w, b_q, b_f, b_i, b_g, c_q, gates = jnp.split(h @ w_in, points, axis=-1)
    a_q = partial_rope(a_q.reshape(bsz, t, A_HEADS, HEAD_DIM), pos, ROT_DIM)
    a_k = partial_rope(a_k.reshape(bsz, t, A_KV_HEADS, HEAD_DIM), pos, ROT_DIM)
    a_v = a_v.reshape(bsz, t, A_KV_HEADS, HEAD_DIM)
    i_q = partial_rope(i_q.reshape(bsz, t, IDX_HEADS, IDX_DIM), pos, IDX_ROT_DIM)
    i_k = partial_rope(i_k.reshape(bsz, t, 1, IDX_DIM), pos, IDX_ROT_DIM)[:, :, 0]
    c_q = c_q.reshape(bsz, t, C_HEADS, C_HEAD_DIM)
    return a_q, a_k, a_v, i_q, i_k, i_w, b_q, b_f, b_i, b_g, c_q, gates

def dsa_block(q, iq, iw, limit, k, v, ik, topk):
    n_keys = k.shape[1]
    key_ok = jnp.arange(n_keys, dtype=jnp.int32)[None, :] < limit[:, None]
    dots = jnp.einsum('bqhd,bsd->bqhs', iq, ik).astype(jnp.float32) * (IDX_DIM ** -0.5)
    score = jnp.einsum('bqhs,bqh->bqs', jax.nn.relu(dots), iw.astype(jnp.float32)) * (IDX_HEADS ** -0.5)
    score = jnp.where(key_ok[None], score, -jnp.inf)
    _, sel = lax.top_k(score, topk)
    valid = sel < limit[None, :, None]
    take = jax.vmap(lambda arr, ix: arr[ix])
    k_sel = take(k, sel)
    v_sel = take(v, sel)
    bsz, nq = q.shape[:2]
    qg = q.reshape(bsz, nq, A_KV_HEADS, A_HEADS // A_KV_HEADS, HEAD_DIM)
    s = jnp.einsum('bqkgd,bqnkd->bqkgn', qg, k_sel).astype(jnp.float32) * (HEAD_DIM ** -0.5)
    s = jnp.where(valid[:, :, None, None, :], s, -jnp.inf)
    p = jax.nn.softmax(s, axis=-1).astype(v.dtype)
    o = jnp.einsum('bqkgn,bqnkd->bqkgd', p, v_sel)
    return o.reshape(bsz, nq, A_WIDTH)

def dsa_prompt(q, iq, iw, k, v, ik):
    bsz, t = q.shape[:2]
    topk = min(TOPK_MAX, t // 4)
    nblk = t // Q_BLOCK
    pos = jnp.arange(t, dtype=jnp.int32)
    limit = (pos // CHUNK + 1) * CHUNK

    def blocks(a):
        return jnp.moveaxis(a.reshape(bsz, nblk, Q_BLOCK, *a.shape[2:]), 1, 0)

    xs = (blocks(q), blocks(iq), blocks(iw), limit.reshape(nblk, Q_BLOCK))
    out = lax.map(lambda blk: dsa_block(blk[0], blk[1], blk[2], blk[3], k, v, ik, topk), xs)
    return jnp.moveaxis(out, 0, 1).reshape(bsz, t, A_WIDTH)

def hgrn2_gates(b_q, b_f, b_i, lower_bound):
    bsz, t = b_q.shape[:2]
    shp = (bsz, t, B_HEADS, B_KEY_DIM)
    f = lower_bound + (1.0 - lower_bound) * jax.nn.sigmoid(b_f.astype(jnp.float32))
    q = jax.nn.silu(b_q.astype(jnp.float32)).reshape(shp)
    k = (1.0 - f).reshape(shp)
    log_f = jnp.log(f).reshape(shp)
    v = b_i.astype(jnp.float32).reshape(bsz, t, B_HEADS, B_VAL_DIM)
    return q, k, v, log_f

def hgrn2_chunk(state, q, k, v, log_f):
    c = q.shape[1]
    b = jnp.cumsum(log_f, axis=1)
    causal = jnp.tril(jnp.ones((c, c), dtype=bool))[None, :, :, None, None]
    decay = jnp.exp(jnp.where(causal, b[:, :, None] - b[:, None, :], -jnp.inf))
    scores = jnp.einsum('btshd,bshd->bhts', q[:, :, None] * decay, k)
    o = jnp.einsum('bhts,bshv->bthv', scores, v) + jnp.einsum('bthd,bhdv->bthv', q * jnp.exp(b), state)
    b_end = b[:, -1]
    new_state = jnp.exp(b_end)[..., None] * state + jnp.einsum(
        'bshd,bshv->bhdv', k * jnp.exp(b_end[:, None] - b), v)
    return new_state, o

def hgrn2_prompt(q, k, v, log_f):
    bsz, t = q.shape[:2]
    n = t // CHUNK

    def chunks(a):
        return jnp.moveaxis(a.reshape(bsz, n, CHUNK, *a.shape[2:]), 1, 0)

    s0 = jnp.zeros((bsz, B_HEADS, B_KEY_DIM, B_VAL_DIM), jnp.float32)
    s_final, o = lax.scan(lambda s, xs: hgrn2_chunk(s, xs[0], xs[1], xs[2], xs[3]), s0,
                          (chunks(q), chunks(k), chunks(v), chunks(log_f)))
    return s_final, jnp.moveaxis(o, 0, 1).reshape(bsz, t, B_HEADS, B_VAL_DIM)

def hgrn2_readout(o, b_g, gain):
    o = rms_norm(o, gain)
    return (o.reshape(*o.shape[:2], B_WIDTH) * jax.nn.silu(b_g.astype(jnp.float32))).astype(b_g.dtype)

def memory_kv(mem, gain, w_mem_kv):
    bsz, n = mem.shape[:2]
    mk, mv = jnp.split(rms_norm(mem, gain) @ w_mem_kv, 2, axis=-1)
    return mk.reshape(bsz, n, C_HEADS, C_HEAD_DIM), mv.reshape(bsz, n, C_HEADS, C_HEAD_DIM)

def memory_attend(q, mem_k, mem_v):
    s = jnp.einsum('bthd,bnhd->bhtn', q, mem_k.astype(q.dtype)).astype(jnp.float32) * (C_HEAD_DIM ** -0.5)
    p = jax.nn.softmax(s, axis=-1).astype(q.dtype)
    o = jnp.einsum('bhtn,bnhd->bthd', p, mem_v.astype(q.dtype))
    return o.reshape(*q.shape[:2], C_WIDTH)

def merge_and_ffn(x, y_a, y_b, y_c, gates, lp):
    g_a, g_b, g_c = jnp.split(jax.nn.sigmoid(gates), N_BRANCHES, axis=-1)
    merged = g_a * (y_a @ lp['w_out_a']) + g_b * (y_b @ lp['w_out_b']) + g_c * (y_c @ lp['w_out_c'])
    x = x + rms_norm(merged @ lp['w_out'], lp['post_mix_gain'])
    u = jax.nn.relu(rms_norm(x, lp['pre_ffn_gain']) @ lp['w_up'])
    return x + rms_norm((u * u) @ lp['w_down'], lp['post_ffn_gain'])

def layer_prompt(x, mem, pos, lower_bound, lp):
    h = rms_norm(x, lp['pre_mix_gain'])
    a_q, a_k, a_v, i_q, i_k, i_w, b_q, b_f, b_i, b_g, c_q, gates = split_projection(h, lp['w_in'], pos)
    y_a = dsa_prompt(a_q, i_q, i_w, a_k, a_v, i_k)
    q, k, v, log_f = hgrn2_gates(b_q, b_f, b_i, lower_bound)
    s_new, o = hgrn2_prompt(q, k, v, log_f)
    y_b = hgrn2_readout(o, b_g, lp['hgrn_norm_gain'])
    mem_k, mem_v = memory_kv(mem, lp['mem_norm_gain'], lp['w_mem_kv'])
    y_c = memory_attend(c_q, mem_k, mem_v)
    x = merge_and_ffn(x, y_a, y_b, y_c, gates, lp)
    return x, (a_k, a_v, i_k, s_new, mem_k, mem_v)

def layer_sample(x, pos, c_k, c_v, c_ik, s_h, c_mk, c_mv, lower_bound, lp):
    h = rms_norm(x, lp['pre_mix_gain'])
    a_q, a_k, a_v, i_q, i_k, i_w, b_q, b_f, b_i, b_g, c_q, gates = split_projection(h, lp['w_in'], pos)
    k_all = jnp.concatenate([c_k.astype(a_k.dtype), a_k], axis=1)
    v_all = jnp.concatenate([c_v.astype(a_v.dtype), a_v], axis=1)
    ik_all = jnp.concatenate([c_ik.astype(i_k.dtype), i_k], axis=1)
    n_keys = k_all.shape[1]
    limit = jnp.full((x.shape[1],), n_keys, dtype=jnp.int32)
    y_a = dsa_block(a_q, i_q, i_w, limit, k_all, v_all, ik_all, min(TOPK_MAX, n_keys // 4))
    q, k, v, log_f = hgrn2_gates(b_q, b_f, b_i, lower_bound)
    s_new, o = hgrn2_chunk(s_h.astype(jnp.float32), q, k, v, log_f)
    y_b = hgrn2_readout(o, b_g, lp['hgrn_norm_gain'])
    y_c = memory_attend(c_q, c_mk, c_mv)
    x = merge_and_ffn(x, y_a, y_b, y_c, gates, lp)
    return x, (a_k, a_v, i_k, s_new)

def setup_inputs(seed: int = 0) -> dict:
    key = jax.random.key(seed)
    ks = jax.random.split(key, 24)

    def nrm(k, shape, scale=1.0):
        return jax.random.normal(k, shape, jnp.float32) * scale

    def gain(k, shape):
        return 1.0 + 0.05 * jax.random.normal(k, shape, jnp.float32)

    return {
        'x_prompt': nrm(ks[0], (BATCH, SEQ, D_MODEL)),
        'x_sample': nrm(ks[1], (DEC_BATCH, DEC_SEQ, D_MODEL)),
        'cache_k': nrm(ks[2], (DEPTH, DEC_BATCH, PAST_LEN, A_KV_HEADS, HEAD_DIM)),
        'cache_v': nrm(ks[3], (DEPTH, DEC_BATCH, PAST_LEN, A_KV_HEADS, HEAD_DIM)),
        'cache_idx_k': nrm(ks[4], (DEPTH, DEC_BATCH, PAST_LEN, IDX_DIM)),
        'state_hgrn': nrm(ks[5], (DEPTH, DEC_BATCH, B_HEADS, B_KEY_DIM, B_VAL_DIM)),
        'cache_mem_k': nrm(ks[6], (DEPTH, DEC_BATCH, N_MEM, C_HEADS, C_HEAD_DIM)),
        'cache_mem_v': nrm(ks[7], (DEPTH, DEC_BATCH, N_MEM, C_HEADS, C_HEAD_DIM)),
        'mem_prompt': nrm(ks[8], (BATCH, N_MEM, D_MODEL)),
        'w_in': nrm(ks[9], (DEPTH, D_MODEL, IN_WIDTH), D_MODEL ** -0.5),
        'w_mem_kv': nrm(ks[10], (DEPTH, D_MODEL, 2 * C_WIDTH), D_MODEL ** -0.5),
        'mem_norm_gain': gain(ks[11], (DEPTH, D_MODEL)),
        'hgrn_lb_logits': nrm(ks[12], (DEPTH + 1, B_HEADS * B_KEY_DIM), 0.5),
        'hgrn_norm_gain': gain(ks[13], (DEPTH, B_HEADS, B_VAL_DIM)),
        'w_out_a': nrm(ks[14], (DEPTH, A_WIDTH, D_MODEL), A_WIDTH ** -0.5),
        'w_out_b': nrm(ks[15], (DEPTH, B_WIDTH, D_MODEL), B_WIDTH ** -0.5),
        'w_out_c': nrm(ks[16], (DEPTH, C_WIDTH, D_MODEL), C_WIDTH ** -0.5),
        'w_out': nrm(ks[17], (DEPTH, D_MODEL, D_MODEL), D_MODEL ** -0.5),
        'pre_mix_gain': gain(ks[18], (DEPTH, D_MODEL)),
        'post_mix_gain': gain(ks[19], (DEPTH, D_MODEL)),
        'pre_ffn_gain': gain(ks[20], (DEPTH, D_MODEL)),
        'post_ffn_gain': gain(ks[21], (DEPTH, D_MODEL)),
        'w_up': nrm(ks[22], (DEPTH, D_MODEL, D_FF), D_MODEL ** -0.5),
        'w_down': nrm(ks[23], (DEPTH, D_FF, D_MODEL), D_FF ** -0.5),
    }

def reference(x_prompt, x_sample, cache_k, cache_v, cache_idx_k, state_hgrn, cache_mem_k, cache_mem_v,
              mem_prompt, w_in, w_mem_kv, mem_norm_gain, hgrn_lb_logits, hgrn_norm_gain, w_out_a, w_out_b,
              w_out_c, w_out, pre_mix_gain, post_mix_gain, pre_ffn_gain, post_ffn_gain, w_up, w_down):
    lower_bounds = jnp.cumsum(jax.nn.softmax(hgrn_lb_logits.astype(jnp.float32), axis=0), axis=0)
    pos_p = jnp.arange(x_prompt.shape[1], dtype=jnp.int32)
    pos_s = cache_k.shape[2] + jnp.arange(x_sample.shape[1], dtype=jnp.int32)
    xp, xs = x_prompt, x_sample
    outs_p, outs_s = [], []
    for l in range(DEPTH):
        lp = {
            'w_in': w_in[l], 'w_mem_kv': w_mem_kv[l], 'mem_norm_gain': mem_norm_gain[l],
            'hgrn_norm_gain': hgrn_norm_gain[l], 'w_out_a': w_out_a[l], 'w_out_b': w_out_b[l],
            'w_out_c': w_out_c[l], 'w_out': w_out[l], 'pre_mix_gain': pre_mix_gain[l],
            'post_mix_gain': post_mix_gain[l], 'pre_ffn_gain': pre_ffn_gain[l],
            'post_ffn_gain': post_ffn_gain[l], 'w_up': w_up[l], 'w_down': w_down[l],
        }
        xp, st_p = layer_prompt(xp, mem_prompt, pos_p, lower_bounds[l], lp)
        xs, st_s = layer_sample(xs, pos_s, cache_k[l], cache_v[l], cache_idx_k[l], state_hgrn[l],
                                cache_mem_k[l], cache_mem_v[l], lower_bounds[l], lp)
        outs_p.append(st_p)
        outs_s.append(st_s)
    new_k_p, new_v_p, new_ik_p, new_s_p, new_mk_p, new_mv_p = [jnp.stack(a) for a in zip(*outs_p)]
    new_k_s, new_v_s, new_ik_s, new_s_s = [jnp.stack(a) for a in zip(*outs_s)]
    return (xp, xs, new_k_p, new_v_p, new_ik_p, new_s_p, new_mk_p, new_mv_p,
            new_k_s, new_v_s, new_ik_s, new_s_s)


_drawn_inputs = setup_inputs


def setup_inputs(seed=0):
    import zlib

    import numpy as np

    out = dict(_drawn_inputs(seed))
    spreads = {}
    factors = {}
    for name, (base, spread) in spreads.items():
        noise = np.random.default_rng([zlib.crc32(name.encode()), seed]).standard_normal(out[name].shape)
        drawn = base * np.exp(spread * noise) if base else spread * noise
        out[name] = __import__('jax').numpy.asarray(drawn.astype(out[name].dtype))
    for name, factor in factors.items():
        out[name] = (out[name] * factor).astype(out[name].dtype)
    return out
```

```python
from contextlib import ExitStack

import numpy as np
import concourse.bass as bass
from concourse import mybir

P = 128
D_MODEL, SEQ, DEC, PAST, N_MEM = 1024, 1024, 64, 128, 256
HD, IDX_D = 128, 64
A_HEADS, A_KV, IDX_HEADS, B_HEADS, C_HEADS = 6, 2, 8, 6, 4
GROUP = A_HEADS // A_KV
A_W, KV_W, IDX_W = A_HEADS * HD, A_KV * HD, IDX_HEADS * IDX_D
B_W, C_W = B_HEADS * HD, C_HEADS * HD
D_FF = 4 * D_MODEL
EPS, NEG, MASKED = 1e-6, -3.0e38, 1.0e30
TOPK_P, TOPK_S = min(256, SEQ // 4), min(256, (PAST + DEC) // 4)

T_ALL = SEQ + DEC
T_PAD = -(-T_ALL // P) * P
N_TILE = T_PAD // P
TILE_P = SEQ // P
KT = D_MODEL // P
GROUPS = [(0, 384), (384, 384), (768, T_ALL - 768)]
SLAB = 2048
SCALE = float(HD) ** -0.5
IDX_SCALE = float(IDX_D) ** -0.5 * float(IDX_HEADS) ** -0.5

OFF_Q = 0
OFF_K = OFF_Q + A_W
OFF_V = OFF_K + KV_W
OFF_IQ = OFF_V + KV_W
OFF_IK = OFF_IQ + IDX_W
OFF_IW = OFF_IK + IDX_D
OFF_BQ = OFF_IW + IDX_HEADS
OFF_BF = OFF_BQ + B_W
OFF_BI = OFF_BF + B_W
OFF_BG = OFF_BI + B_W
OFF_CQ = OFF_BG + B_W
OFF_G = OFF_CQ + C_W
IDX_KW = IDX_D + IDX_HEADS

F32, F32R, I32 = mybir.dt.float32, mybir.dt.float32r, mybir.dt.int32
ALU, ACT, AX = mybir.AluOpType, mybir.ActivationFunctionType, mybir.AxisListType

LEVELS = [1, 2, 4, 8, 16, 32, 64]
OFF_COS, OFF_SIN = 0, 16
OFF_ICOS, OFF_ISIN = 32, 40
ROPE_W = 48


class Shared:
    pass


class IndexBuffers:
    pass


class SlabPlan:

    def __init__(self, kind, w, cols, units, func, rope=None, mem=False):
        self.kind, self.w, self.cols, self.units = kind, w, cols, units
        self.func, self.rope, self.mem = func, rope, mem


def rows(i):
    return P if i < TILE_P else DEC


def n_keys(i):
    return (i + 1) * P if i < TILE_P else PAST + DEC


BIAS_OFF = [sum(n_keys(j) for j in range(i)) for i in range(N_TILE + 1)]


def bcast(ap, n):
    return ap.unsqueeze(2).to_broadcast([ap.shape[0], ap.shape[1], n])


def bcast_mid(ap, n):
    return ap.unsqueeze(1).to_broadcast([ap.shape[0], n, ap.shape[1]])


def build(nc, io):
    with ExitStack() as ctx:
        g = Shared()
        g.nc, g.io = nc, io
        g.sb = lambda name, shape, dt=F32: ctx.enter_context(nc.sbuf_tensor(name, shape, dt))
        g.sem = lambda name: ctx.enter_context(nc.semaphore(name))
        g.ps = ctx.enter_context(nc.psum_tensor("ps", [P, 8, 512], F32))
        dram = lambda name, shape: nc.dram_tensor(name, shape, F32, kind="Internal").ap()
        g.d_q = dram("d_q", (T_ALL, A_W))
        g.d_iq = dram("d_iq", (T_ALL, IDX_W))
        g.d_ik = dram("d_ik", (T_ALL, IDX_KW))
        g.d_bq = dram("d_bq", (B_W, T_ALL))
        g.d_bf = dram("d_bf", (B_W, T_ALL))
        g.d_bi = dram("d_bi", (T_ALL, B_W))
        g.d_bg = dram("d_bg", (T_ALL, B_W))
        g.d_cq = dram("d_cq", (C_W, T_ALL))
        g.d_gate = dram("d_gate", (3 * D_MODEL, T_ALL))
        g.d_y = dram("d_y", (A_W + B_W + C_W, T_ALL))
        g.d_x2 = dram("d_x2", (T_ALL, D_MODEL))

        g.ident = g.sb("ident", [P, P])
        g.gains = g.sb("gains", [P, 3, KT])
        ring_semaphores(g)
        with ExitStack() as mid:
            g.bias = mid.enter_context(nc.sbuf_tensor("bias", [P, BIAS_OFF[N_TILE]], F32))
            with ExitStack() as first:
                weight_ring(g, first, "w1")
                g.h_hi = first.enter_context(nc.sbuf_tensor("h_hi", [P, KT, T_PAD], F32R))
                g.h_lo = first.enter_context(nc.sbuf_tensor("h_lo", [P, KT, T_PAD], F32R))
                with ExitStack() as c0:
                    g.m_hi = c0.enter_context(nc.sbuf_tensor("m_hi", [P, KT, N_MEM], F32R))
                    g.m_lo = c0.enter_context(nc.sbuf_tensor("m_lo", [P, KT, N_MEM], F32R))
                    block_norm(g)
                    block_project(g, "b1", plan_first(g), False)
                block_project(g, "b2", plan_second(g), True)
            block_branches(g)
        with ExitStack() as last:
            weight_ring(g, last, "w2")
            g.big = last.enter_context(nc.sbuf_tensor("big", [P, N_TILE * D_MODEL], F32))
            g.merged = g.big[:, 0:KT * T_ALL].rearrange("p (k t) -> p k t", k=KT)
            block_gate_merge(g)
            g.h_hi = last.enter_context(nc.sbuf_tensor("f_hi", [P, KT, T_PAD], F32R))
            g.h_lo = last.enter_context(nc.sbuf_tensor("f_lo", [P, KT, T_PAD], F32R))
            block_out(g)
            block_ffn(g)
            block_final(g)



def weight_ring(g, ctx, tag):
    sb = lambda name, dt: ctx.enter_context(g.nc.sbuf_tensor(f"{tag}_{name}", [P, 2, SLAB], dt))
    g.w_raw, g.w_hi, g.w_lo = sb("raw", F32), sb("hi", F32R), sb("lo", F32R)


def ring_semaphores(g):
    g.slab = 0
    g.arrived = [g.sem(f"arrived{i}") for i in range(N_TILE + N_MEM // P)]
    g.w_loaded = [g.sem("w_loaded0"), g.sem("w_loaded1")]
    g.w_rounded = g.sem("w_rounded")
    g.w_split = g.sem("w_split")
    g.w_used = g.sem("w_used")


def load_slab(g, sp, n, src, k):
    if n >= 2:
        sp.wait_ge(g.w_split, n - 1)
    cols = src.shape[2]
    dst = g.w_raw[:, n % 2, 0:k * cols].rearrange("p (k c) -> p k c", k=k)
    sp.dma_start(dst, src).then_inc(g.w_loaded[n % 2], 16)


def split_slab(g, pool, n, size):
    s = n % 2
    pool.wait_ge(g.w_loaded[s], 16 * (n // 2 + 1))
    if n >= 2:
        pool.wait_ge(g.w_used, n - 1)
    raw, hi, lo = g.w_raw[:, s, 0:size], g.w_hi[:, s, 0:size], g.w_lo[:, s, 0:size]
    g.nc.gpsimd.tensor_copy(hi, raw).then_inc(g.w_rounded, 1)
    pool.wait_ge(g.w_rounded, n + 1)
    g.nc.gpsimd.tensor_tensor(lo, raw, hi.bitcast(F32), ALU.subtract).then_inc(g.w_split, 1)


def slab_view(g, n, k, cols):
    s = n % 2
    return [w[:, s, 0:k * cols].rearrange("p (k c) -> p k c", k=k) for w in (g.w_hi, g.w_lo)]


def three_products(pe, out, left, right, k):
    for kk in range(k):
        for n, (a, b) in enumerate(((0, 0), (0, 1), (1, 0))):
            last = pe.matmul(out, left(a, kk), right(b, kk),
                             start=(kk == 0 and n == 0), stop=(kk == k - 1 and n == 2))
    return last


def w_cols(w, c0, n):
    return w[:, c0:c0 + n].rearrange("(k p) c -> p k c", p=P)



def block_norm(g):
    nc, io = g.nc, g.io
    NT = N_TILE + N_MEM // P
    with ExitStack() as ctx:
        xs = ctx.enter_context(nc.sbuf_tensor("n_x", [P, NT, D_MODEL], F32))
        junk = ctx.enter_context(nc.sbuf_tensor("n_junk", [P, D_MODEL], F32))
        ss = ctx.enter_context(nc.sbuf_tensor("n_ss", [P, NT], F32))
        rs = ctx.enter_context(nc.sbuf_tensor("n_rs", [P, NT], F32))
        x_in = g.arrived
        c_in, zeroed, squared, mean, root = (g.sem("n_const"), g.sem("n_zero"), g.sem("n_sq"),
                                             g.sem("n_mean"), g.sem("n_root"))
        scaled, turned, hi_done, lo_done = g.sem("n_scaled"), g.sem("n_turned"), g.sem("n_hi"), g.sem("n_lo")
        srcs = [io["x_prompt"][0, i * P:(i + 1) * P, :] for i in range(TILE_P)] + [io["x_sample"][0]]
        srcs += [io["mem_prompt"][0, i * P:(i + 1) * P, :] for i in range(N_MEM // P)]
        units = []
        for k in range(KT):
            for c0, n in GROUPS:
                units.append((k, 0, [c0 // P + j for j in range(-(-n // P))], c0, n))
            units.append((k, 1, [N_TILE + j for j in range(N_MEM // P)], 0, N_MEM))

        with nc.Block() as block:
            @block.sync
            def _(sp):
                sp.dma_start(g.ident[:], io["c_ident"]).then_inc(c_in, 16)
                for j, name in enumerate(("pre_mix_gain", "mem_norm_gain", "pre_ffn_gain")):
                    sp.dma_start(g.gains[:, j, :], io[name][0].rearrange("(k p) -> p k", p=P),
                                 allow_slow_non_contiguous=True).then_inc(c_in, 16)
                for i, src in enumerate(srcs):
                    sp.dma_start(xs[0:src.shape[0], i, :], src).then_inc(x_in[i], 16)

            @block.scalar
            def _(act):
                act.wait_ge(zeroed, 1)
                for i, src in enumerate(srcs):
                    r = src.shape[0]
                    act.wait_ge(x_in[i], 16)
                    if i:
                        act.wait_ge(squared, i)
                    nc.scalar.activation(junk[0:r, :], xs[0:r, i, :], ACT.Square,
                                         accum_out=ss[0:r, i:i + 1]).then_inc(squared, 1)
                act.wait_ge(mean, 1)
                nc.scalar.activation(rs[:, :], ss[:, :], ACT.Sqrt).then_inc(root, 1)
                act.wait_ge(c_in, 64)
                for u, (k, which, tiles, c0, n) in enumerate(units):
                    act.wait_ge(turned, u + 1)
                    dst = (g.h_hi, g.m_hi)[which][:, k, c0:c0 + n]
                    nc.scalar.activation(dst, g.ps[:, u % 8, 0:n], ACT.Copy,
                                         scale=g.gains[:, which, k:k + 1]).then_inc(hi_done, 1)

            @block.vector
            def _(dve):
                nc.vector.memset(ss[:], 1.0).then_inc(zeroed, 1)
                for t in (g.h_hi, g.h_lo):
                    nc.vector.memset(t[:, :, T_ALL:T_PAD].bitcast(F32), 0.0)
                dve.wait_ge(squared, NT)
                nc.vector.tensor_scalar(ss[:], ss[:], 1.0 / D_MODEL, EPS, ALU.mult, ALU.add).then_inc(mean, 1)
                dve.wait_ge(root, 1)
                nc.vector.reciprocal(rs[:], rs[:]).then_inc(mean, 1)
                dve.wait_ge(mean, 2)
                for i, src in enumerate(srcs):
                    r = src.shape[0]
                    nc.vector.tensor_scalar(xs[0:r, i, :], xs[0:r, i, :], rs[0:r, i:i + 1], None,
                                            ALU.mult).then_inc(scaled, 1)
                for u, (k, which, tiles, c0, n) in enumerate(units):
                    dve.wait_ge(hi_done, u + 1)
                    hi = (g.h_hi, g.m_hi)[which][:, k, c0:c0 + n]
                    lo = (g.h_lo, g.m_lo)[which][:, k, c0:c0 + n]
                    nc.vector.scalar_tensor_tensor(out=lo, in0=g.ps[:, u % 8, 0:n],
                                                   scalar=g.gains[:, which, k:k + 1], in1=hi.bitcast(F32),
                                                   op0=ALU.mult, op1=ALU.subtract).then_inc(lo_done, 1)

            @block.tensor
            def _(pe):
                pe.wait_ge(c_in, 64)
                pe.wait_ge(scaled, NT)
                for u, (k, which, tiles, c0, n) in enumerate(units):
                    if u >= 8:
                        pe.wait_ge(lo_done, u - 7)
                    for j, i in enumerate(tiles):
                        r = srcs[i].shape[0]
                        last = pe.transpose(g.ps[:, u % 8, j * P:j * P + r], xs[0:r, i, k * P:(k + 1) * P],
                                            g.ident[0:r, 0:r])
                    last.then_inc(turned, 1)



def token_units(dests):
    return [(i, rows(i), dests(i)) for i in range(N_TILE)]


def row_slice(i):
    return slice(i * P, i * P + rows(i))


def feature_units(d, f0):
    return [(ft, c0, n, d[f0 + ft * P:f0 + (ft + 1) * P, c0:c0 + n]) for ft in range(2) for c0, n in GROUPS]


def kv_dest(io, prompt, sample, i):
    return io[prompt][0, 0, i * P:(i + 1) * P] if i < TILE_P else io[sample][0, 0]


def plan_first(g):
    io, plan = g.io, []
    w = io["w_in"][0]
    for j in range(2):
        plan.append(SlabPlan("t", w_cols(w, OFF_IQ + j * 256, 256), 256,
                              token_units(lambda i: [(g.d_iq[row_slice(i), j * 256:(j + 1) * 256], 0, 256)]),
                              ACT.Copy, rope=(4, IDX_D, 8, OFF_ICOS, OFF_ISIN)))
    plan.append(SlabPlan("t", w_cols(w, OFF_IK, IDX_KW), IDX_KW,
                          token_units(lambda i: [(g.d_ik[row_slice(i), :], 0, IDX_KW),
                                                 (kv_dest(io, "new_idx_k_prompt", "new_idx_k_sample", i), 0, IDX_D)]),
                          ACT.Copy, rope=(1, IDX_D, 8, OFF_ICOS, OFF_ISIN)))
    for j in range(4):
        out = io["new_mem_k_prompt"] if j < 2 else io["new_mem_v_prompt"]
        out = out[0, 0].rearrange("n h d -> n (h d)")
        c0 = (j % 2) * 256
        units = [(i, P, [(out[i * P:(i + 1) * P, c0:c0 + 256], 0, 256)]) for i in range(N_MEM // P)]
        plan.append(SlabPlan("t", w_cols(io["w_mem_kv"][0], j * 256, 256), 256, units, ACT.Copy, mem=True))
    return plan


def plan_second(g):
    io, plan = g.io, []
    w = io["w_in"][0]
    rope = (2, HD, 16, OFF_COS, OFF_SIN)

    def flat(name_p, name_s, i):
        return kv_dest(io, name_p, name_s, i).rearrange("t h d -> t (h d)")

    plan.append(SlabPlan("t", w_cols(w, OFF_K, 256), 256,
                          token_units(lambda i: [(flat("new_k_prompt", "new_k_sample", i), 0, 256)]),
                          ACT.Copy, rope=rope))
    plan.append(SlabPlan("t", w_cols(w, OFF_V, 256), 256,
                          token_units(lambda i: [(flat("new_v_prompt", "new_v_sample", i), 0, 256)]), ACT.Copy))

    def to_rows(d, off, n, func, rope=None):
        for j in range(n):
            plan.append(SlabPlan("t", w_cols(w, off + j * 256, 256), 256,
                                  token_units(lambda i: [(d[row_slice(i), j * 256:(j + 1) * 256], 0, 256)]),
                                  func, rope=rope))

    def to_features(d, off, n, func):
        for j in range(n):
            plan.append(SlabPlan("f", w_cols(w, off + j * 256, 256), 256, feature_units(d, j * 256), func))

    to_rows(g.d_q, OFF_Q, 3, ACT.Copy, rope=rope)
    to_rows(g.d_bi, OFF_BI, 3, ACT.Copy)
    to_features(g.d_cq, OFF_CQ, 2, ACT.Copy)
    to_rows(g.d_bg, OFF_BG, 3, ACT.Silu)
    to_features(g.d_bq, OFF_BQ, 3, ACT.Silu)
    to_features(g.d_bf, OFF_BF, 3, ACT.Sigmoid)
    to_features(g.d_gate, OFF_G, 12, ACT.Sigmoid)
    return plan


def block_project(g, tag, plan, with_index):
    nc, io = g.nc, g.io
    n0 = g.slab
    g.slab += len(plan)
    NB, NS = 4, 8
    order = []
    for s, sl in enumerate(plan):
        order += [(s, u) for u in sl.units]
    first = [sum(len(q.units) for q in plan[:s]) for s in range(len(plan) + 1)]
    roped = []
    for s, u in order:
        roped.append((roped[-1] if roped else 0) + (plan[s].rope is not None))
    n_out = []
    per = [0] * NS
    for n, (s, u) in enumerate(order):
        per[n % NS] += len(u[2]) if plan[s].kind == "t" else 1
        n_out.append(per[n % NS])
    with ExitStack() as ctx:
        stage = ctx.enter_context(nc.sbuf_tensor(f"{tag}_stage", [P, NS, 384], F32))
        cs = ctx.enter_context(nc.sbuf_tensor(f"{tag}_cs", [P, N_TILE, ROPE_W], F32))
        rt = ctx.enter_context(nc.sbuf_tensor(f"{tag}_rt", [P, 4, 32], F32))
        cs_in, full, staged = g.sem(f"{tag}_cs_in"), g.sem(f"{tag}_full"), g.sem(f"{tag}_staged")
        rope_part, rope_done = g.sem(f"{tag}_rope_part"), g.sem(f"{tag}_roped")
        stored = [g.sem(f"{tag}_stored{j}") for j in range(NS)]
        ix = index_setup(g, ctx) if with_index else None

        with nc.Block() as block:
            @block.sync
            def _(sp):
                sp.dma_start(cs[:], io["c_rope"]).then_inc(cs_in, 16)
                for s in range(2):
                    load_slab(g, sp, n0 + s, plan[s].w, KT)
                if ix:
                    index_loads(g, ix, sp)
                for s, sl in enumerate(plan):
                    for n in range(first[s], first[s + 1]):
                        u = order[n][1]
                        if sl.rope:
                            sp.wait_ge(rope_done, roped[n])
                        else:
                            sp.wait_ge(staged, n + 1)
                        if sl.kind == "t":
                            for dst, c0, c in u[2]:
                                sp.dma_start(dst, stage[0:u[1], n % NS, c0:c0 + c]).then_inc(stored[n % NS], 16)
                        else:
                            sp.dma_start(u[3], stage[:, n % NS, 0:u[2]]).then_inc(stored[n % NS], 16)
                    if s + 2 < len(plan):
                        load_slab(g, sp, n0 + s + 2, plan[s + 2].w, KT)
                for j in range(NS):
                    sp.wait_ge(stored[j], 16 * per[j])

            @block.gpsimd
            def _(pool):
                pool.wait_ge(cs_in, 16)
                split_slab(g, pool, n0, KT * plan[0].cols)
                parts = 0
                for s, sl in enumerate(plan):
                    if s + 1 < len(plan):
                        split_slab(g, pool, n0 + s + 1, KT * plan[s + 1].cols)
                    if not sl.rope:
                        continue
                    heads, width, half, co, so = sl.rope
                    for n in range(first[s], first[s + 1]):
                        i, r, _ = order[n][1]
                        x = stage[0:r, n % NS, 0:heads * width].rearrange("p (h d) -> p h d", h=heads)
                        x1, x2 = x[:, :, 0:half], x[:, :, half:2 * half]
                        cos = bcast_mid(cs[0:r, i, co:co + half], heads)
                        sin = bcast_mid(cs[0:r, i, so:so + half], heads)
                        t = [rt[0:r, j, 0:heads * half].rearrange("p (h d) -> p h d", h=heads) for j in range(4)]
                        pool.wait_ge(staged, n + 1)
                        if parts:
                            pool.wait_ge(rope_done, parts)
                        for j, (a, b) in enumerate(((x1, cos), (x2, sin), (x2, cos), (x1, sin))):
                            last = nc.gpsimd.tensor_tensor(t[j], a, b, ALU.mult)
                        parts += 1
                        last.then_inc(rope_part, 1)
                        pool.wait_ge(rope_part, parts)
                        nc.gpsimd.tensor_tensor(x1, t[0], t[1], ALU.subtract)
                        nc.gpsimd.tensor_tensor(x2, t[2], t[3], ALU.add).then_inc(rope_done, 1)

            @block.scalar
            def _(act):
                for s, sl in enumerate(plan):
                    for n in range(first[s], first[s + 1]):
                        u = order[n][1]
                        act.wait_ge(full, n + 1)
                        if n >= NS:
                            act.wait_ge(stored[n % NS], 16 * n_out[n - NS])
                        r, c = (u[1], sl.cols) if sl.kind == "t" else (P, u[2])
                        nc.scalar.activation(stage[0:r, n % NS, 0:c], g.ps[0:r, n % NB, 0:c],
                                             sl.func).then_inc(staged, 1)
                    if ix:
                        index_act(g, ix, act, s)

            @block.tensor
            def _(pe):
                if ix:
                    index_turn(g, ix, pe)
                for s, sl in enumerate(plan):
                    w = slab_view(g, n0 + s, KT, sl.cols)
                    x = (g.m_hi, g.m_lo) if sl.mem else (g.h_hi, g.h_lo)
                    pe.wait_ge(g.w_split, n0 + s + 1)
                    for n in range(first[s], first[s + 1]):
                        u = order[n][1]
                        if n >= NB:
                            pe.wait_ge(staged, n - NB + 1)
                        if sl.kind == "t":
                            c = slice(u[0] * P, (u[0] + 1) * P)
                            last = three_products(pe, g.ps[:, n % NB, 0:sl.cols],
                                                  lambda a, k: x[a][:, k, c], lambda b, k: w[b][:, k, :], KT)
                        else:
                            f, c = slice(u[0] * P, (u[0] + 1) * P), slice(u[1], u[1] + u[2])
                            last = three_products(pe, g.ps[:, n % NB, 0:u[2]],
                                                  lambda a, k: w[a][:, k, f], lambda b, k: x[b][:, k, c], KT)
                        last.then_inc(full, 1)
                    pe.drain().then_inc(g.w_used, 1)
                    if ix:
                        index_scores(g, ix, pe, s)

            if ix:
                @block.vector
                def _(dve):
                    index_select(g, ix, dve)



SCORED = list(range(2, N_TILE))
SCORED_AFTER = {0: [2, 3], 1: [4, 5], 2: [6, 7], 3: [8]}
IX_BANKS = 4


def index_setup(g, ctx):
    nc = g.nc
    sb = lambda name, shape: ctx.enter_context(nc.sbuf_tensor(name, shape, F32))
    ix = IndexBuffers()
    ix.qT = sb("ix_qT", [P, IDX_W // P, T_ALL])
    ix.kT = sb("ix_kT", [P, SEQ + PAST + DEC])
    ix.w = sb("ix_w", [P, N_TILE, IDX_HEADS])
    ix.relu = sb("ix_relu", [P, 3, 512])
    ix.work = sb("ix_work", [P, 3, 1024])
    ix.m8 = sb("ix_m8", [P, 8])
    ix.cnt = sb("ix_cnt", [P, 1])
    ix.in_, ix.turned, ix.kept, ix.scored = g.sem("ix_in"), g.sem("ix_turned"), g.sem("ix_kept"), g.sem("ix_scored")
    ix.relued, ix.added, ix.step = g.sem("ix_relued"), g.sem("ix_added"), g.sem("ix_step")
    ix.q_rows = g.bias[:, 0:N_TILE * IDX_W].rearrange("p (i c) -> p i c", i=N_TILE)
    ix.k_rows = ix.work[:].rearrange("p a b -> p (a b)")[:, 0:(N_TILE + 1) * P].rearrange("p (i c) -> p i c", c=P)
    ix.k_tiles = [(j, P, j * P) for j in range(TILE_P)] + [(N_TILE, P, SEQ), (TILE_P, DEC, SEQ + PAST)]
    ix.units = [(i, h, c, min(512, n_keys(i) - c)) for i in SCORED
                for c in range(0, n_keys(i), 512) for h in range(IDX_HEADS)]
    ix.turns = [("q", i) for i in range(N_TILE)] + [("k", j) for j in range(len(ix.k_tiles))]
    ix.n_in = 0
    return ix


def index_loads(g, ix, sp):
    def load(dst, src):
        sp.dma_start(dst, src, allow_slow_non_contiguous=True).then_inc(ix.in_, 16)
        ix.n_in += 16
    for i in range(N_TILE):
        r = rows(i)
        load(ix.q_rows[0:r, i, :], g.d_iq[row_slice(i), :])
        load(ix.w[0:r, i, :], g.d_ik[row_slice(i), IDX_D:IDX_KW])
        for c in range(0, P, IDX_D):
            load(ix.k_rows[0:r, i, c:c + IDX_D], g.d_ik[row_slice(i), 0:IDX_D])
    for c in range(0, P, IDX_D):
        load(ix.k_rows[:, N_TILE, c:c + IDX_D], g.io["cache_idx_k"][0, 0])


def index_turn(g, ix, pe):
    pe.wait_ge(ix.in_, ix.n_in)
    for n, (kind, j) in enumerate(ix.turns):
        bank = g.ps[:, 4 + n % IX_BANKS, :]
        if n >= IX_BANKS:
            pe.wait_ge(ix.kept, n - IX_BANKS + 1)
        if kind == "q":
            r = rows(j)
            for f in range(IDX_W // P):
                last = pe.transpose(bank[:, f * P:f * P + r], ix.q_rows[0:r, j, f * P:(f + 1) * P],
                                    g.ident[0:r, 0:r])
        else:
            src, r, _ = ix.k_tiles[j]
            last = pe.transpose(bank[:, 0:r], ix.k_rows[0:r, src, :], g.ident[0:r, 0:r])
        last.then_inc(ix.turned, 1)


def index_scores(g, ix, pe, s):
    for n, (i, h, c, w) in enumerate(ix.units):
        if i not in SCORED_AFTER.get(s, []):
            continue
        if n == 0:
            pe.wait_ge(ix.kept, len(ix.turns))
        if n >= IX_BANKS:
            pe.wait_ge(ix.relued, n - IX_BANKS + 1)
        half = slice((h % 2) * IDX_D, (h % 2) * IDX_D + IDX_D)
        k0 = (0 if i < TILE_P else SEQ) + c
        pe.matmul(g.ps[0:rows(i), 4 + n % IX_BANKS, 0:w], ix.qT[half, h // 2, row_slice(i)],
                  ix.kT[half, k0:k0 + w], start=True, stop=True).then_inc(ix.scored, 1)


def index_act(g, ix, act, s):
    for n, (i, h, c, w) in enumerate(ix.units):
        if i not in SCORED_AFTER.get(s, []):
            continue
        act.wait_ge(ix.scored, n + 1)
        if n >= 3:
            act.wait_ge(ix.added, n - 2)
        g.nc.scalar.activation(ix.relu[0:rows(i), n % 3, 0:w], g.ps[0:rows(i), 4 + n % IX_BANKS, 0:w],
                               ACT.Relu, scale=IDX_SCALE).then_inc(ix.relued, 1)


def index_select(g, ix, dve):
    v = g.nc.vector
    for n, (kind, j) in enumerate(ix.turns):
        bank = g.ps[:, 4 + n % IX_BANKS, :]
        dve.wait_ge(ix.turned, n + 1)
        if kind == "q":
            r = rows(j)
            src = bank.rearrange("p (f t) -> p f t", t=P)[:, :, 0:r]
            v.tensor_copy(ix.qT[:, :, j * P:j * P + r], src).then_inc(ix.kept, 1)
        else:
            _, r, c0 = ix.k_tiles[j]
            v.tensor_copy(ix.kT[:, c0:c0 + r], bank[:, 0:r]).then_inc(ix.kept, 1)
    for n, (i, h, c, w) in enumerate(ix.units):
        r, sc = rows(i), g.bias[0:rows(i), BIAS_OFF[i] + c:BIAS_OFF[i] + c + w]
        dve.wait_ge(ix.relued, n + 1)
        relu, weight = ix.relu[0:r, n % 3, 0:w], ix.w[0:r, i, h:h + 1]
        if h == 0:
            v.tensor_scalar(sc, relu, weight, None, ALU.mult).then_inc(ix.added, 1)
        else:
            dve.wait_ge(ix.added, n)
            v.scalar_tensor_tensor(out=sc, in0=relu, scalar=weight, in1=sc,
                                   op0=ALU.mult, op1=ALU.add).then_inc(ix.added, 1)
    dve.wait_ge(ix.added, len(ix.units))

    steps = [0]

    def link(ins):
        steps[0] += 1
        ins.then_inc(ix.step, 1)
        dve.wait_ge(ix.step, steps[0])

    for i in range(N_TILE):
        n, r = n_keys(i), rows(i)
        sc = g.bias[0:r, BIAS_OFF[i]:BIAS_OFF[i + 1]]
        if i < 2:
            link(v.memset(sc, 0.0))
            link(v.memset(sc[0:64, n - 64:n], -MASKED))
            continue
        if i < TILE_P:
            link(v.memset(sc[0:64, n - 64:n], NEG))
        topk = TOPK_P if i < TILE_P else TOPK_S
        left, eq, cum = (ix.work[0:r, j, 0:n] for j in range(3))
        m8, cnt = ix.m8[0:r, :], ix.cnt[0:r, :]
        for it in range(topk // 8):
            link(v.max(m8, sc if it == 0 else left))
            if it < topk // 8 - 1:
                link(v.match_replace(left, m8, sc if it == 0 else left, NEG))
        bar = m8[:, 7:8]
        link(v.tensor_scalar(left, sc, bar, 0.0, ALU.is_gt, ALU.add, accum_out=cnt))
        link(v.tensor_scalar(cnt, cnt, -1.0, float(topk), ALU.mult, ALU.add))
        link(v.tensor_scalar(eq, sc, bar, None, ALU.is_equal))
        link(v.tensor_tensor_scan(cum, eq, eq, 0.0, ALU.add, ALU.max))
        link(v.scalar_tensor_tensor(out=eq, in0=cum, scalar=cnt, in1=eq, op0=ALU.is_le, op1=ALU.mult))
        link(v.tensor_tensor(left, left, eq, ALU.add))
        link(v.tensor_scalar(sc, left, -1.0, MASKED, ALU.add, ALU.mult))



N_HEAD = N_TILE * A_HEADS
H3 = B_HEADS // 2
YB0, YC0 = A_W, A_W + B_W


def stages(i):
    return [h for h in LEVELS if 2 * h <= rows(i)] + ["q", "k"]


STEP0 = [sum(len(stages(j)) for j in range(i)) for i in range(N_TILE + 1)]


def v_tiles(i):
    if i < TILE_P:
        return [(j, P) for j in range(i + 1)]
    return [(TILE_P, P), (TILE_P + 1, DEC)]


def block_branches(g):
    nc, io = g.nc, g.io
    V, S, G = nc.vector, nc.scalar, nc.gpsimd
    with ExitStack() as ctx:
        sb = lambda name, shape, dt=F32: ctx.enter_context(nc.sbuf_tensor("br_" + name, shape, dt))
        kT = sb("kT", [P, A_KV, SEQ + PAST + DEC])
        val = sb("val", [P, N_TILE + 1, KV_W])
        mkT = sb("mkT", [P, 2, C_HEADS, N_MEM])
        mval = sb("mval", [P, 2, N_MEM // P, C_W])
        pT = sb("pT", [P, TILE_P, A_HEADS, P])
        nat = pT[:].rearrange("p a b c -> p (a b c)")
        k_nat = nat[:, 0:(N_TILE + 1) * KV_W].rearrange("p (j c) -> p j c", c=KV_W)
        m_nat = nat[:, (N_TILE + 1) * KV_W:(N_TILE + 1) * KV_W + 4 * C_W].rearrange("p (m j c) -> p m j c", m=2, j=2)
        q_nat, qT = sb("q_nat", [P, 2, A_W]), sb("qT", [P, 2, A_HEADS, P])
        prob = sb("prob", [P, 3, 1024])
        top, ntop, den = sb("top", [P, 8]), sb("ntop", [P, 8]), sb("den", [P, 8])
        part = sb("part", [P, 1])
        cq = sb("cq", [P, 2, C_HEADS, P])
        cp, cpT = sb("cp", [P, C_HEADS, N_MEM]), sb("cpT", [P, C_HEADS, 2, P])
        ctop, cden = sb("ctop", [P, C_HEADS]), sb("cden", [P, C_HEADS])
        ysb = sb("ysb", [P, 3, 512])
        sig, bq = sb("sig", [P, 2, B_W]), sb("bq", [P, 2, B_W])
        bv, bg = sb("bv", [P, 2, B_W]), sb("bg", [P, 2, B_W])
        kk, cum = sb("kk", [P, B_W]), sb("cum", [P, B_W])
        dif, ex, wk = sb("dif", [P, 2, B_W]), sb("ex", [P, 2, B_W]), sb("wk", [P, 2, B_W])
        exn, kp = sb("exn", [P, B_W]), sb("kp", [P, B_W])
        smat, kdT = sb("smat", [P, B_HEADS, P]), sb("kdT", [P, B_W])
        osb, sq = sb("osb", [P, B_W]), sb("sq", [P, B_W])
        ybT = sb("ybT", [P, B_HEADS, P])
        ms = sb("ms", [P, B_HEADS])
        eb = sb("eb", [P, B_HEADS])
        state = [sb("stateP", [P, B_HEADS, HD]), sb("stateS", [P, B_HEADS, HD])]
        lgt, lb, oml = sb("lgt", [P, 2, B_HEADS]), sb("lb", [P, B_HEADS]), sb("oml", [P, B_HEADS])
        lmx = sb("lmx", [P, B_HEADS])
        masks, grow, zero = sb("masks", [P, len(LEVELS), P], I32), sb("grow", [P, B_W]), sb("zero", [P, P])

        sem = lambda name: g.sem("br_" + name)
        s_set, s_step, s_act, s_zero = sem("set"), sem("step"), sem("lb_exp"), sem("zero")
        s_lb = sem("lb")
        s_in = [sem("in0"), sem("in1")]
        t_done, t_kept = sem("t_done"), sem("t_kept")
        s_done, s_masked, ntop_ok, e_done, p_done, p_turned = (sem("s_done"), sem("s_masked"), sem("ntop"),
                                                               sem("exp"), sem("p_done"), sem("p_turned"))
        c_done, c_top, c_exp, c_norm, c_turned = sem("c_done"), sem("c_top"), sem("c_exp"), sem("c_norm"), sem("c_turned")
        o_done, o_kept = sem("o_done"), sem("o_kept")
        y_out = [sem(f"y_out{j}") for j in range(3)]
        yb_out, st_out = sem("yb_out"), sem("st_out")
        f_part, f_done, l_done, d_done, x_done, w_done = (sem("f_part"), sem("f_done"), sem("l_done"),
                                                                  sem("d_done"), sem("x_done"), sem("w_done"))
        hp_done, hp_free, s_cleared = sem("hp_done"), sem("hp_free"), sem("s_cleared")
        sq_done, ms_done, rs_part, rs_done, y_part, y_done, gg_done = (sem("sq"), sem("ms"), sem("rs_part"), sem("rs"),
                                                                       sem("y_part"), sem("y_done"), sem("gg"))

        k_rows = [(j, P, j * P) for j in range(TILE_P)] + [(TILE_P, P, SEQ), (TILE_P + 1, DEC, SEQ + PAST)]
        N_SET = 16 * (2 + 4 + 4 + 4)

        def due(i, s):
            return [pos for pos in (2 * s, 2 * s + 1) if s >= 0 and pos < len(stages(i))]

        qturned, prob_turned, tc = {0: len(k_rows) + 4 + 2}, {}, len(k_rows) + 4 + 2
        hu_step, hu_idx, hu_st, hu_y, hc = {}, {}, {}, {}, 0
        for n in range(N_HEAD + 2):
            i, slot = divmod(n, A_HEADS)
            if n >= 2:
                tc += -(-len(v_tiles((n - 2) // A_HEADS)) // 4)
                prob_turned[n - 2] = tc
            if slot == 2 and i + 1 < N_TILE:
                tc += 2
                qturned[i + 1] = tc
            if slot == 3:
                tc += 2
            if slot == 1 and i >= 1:
                hc += 2
                hu_y[i - 1] = hc
            if i < N_TILE:
                for pos in due(i, slot - 1):
                    hc += 2
                    hu_step[i, pos] = hu_idx[STEP0[i] + pos] = hc
                if slot == 5:
                    hc += 2
                    hu_st[i] = hc

        def dcount(i, pos):
            st = stages(i)
            return STEP0[i] - i + pos + 1 - (1 if pos >= st.index("q") else 0)

        with nc.Block() as block:
            @block.sync
            def _(sp):
                def setup(dst, src):
                    sp.dma_start(dst, src, allow_slow_non_contiguous=True).then_inc(s_set, 16)

                kp_, vp_ = (io[n][0, 0].rearrange("(j p) h d -> p j (h d)", p=P)
                            for n in ("new_k_prompt", "new_v_prompt"))
                setup(k_nat[:, 0:TILE_P, :], kp_)
                setup(val[:, 0:TILE_P, :], vp_)
                for dst, name, new in ((k_nat, "cache_k", "new_k_sample"), (val, "cache_v", "new_v_sample")):
                    setup(dst[:, TILE_P, :], io[name][0, 0].rearrange("t h d -> t (h d)"))
                    setup(dst[0:DEC, TILE_P + 1, :], io[new][0, 0].rearrange("t h d -> t (h d)"))
                for m, names in enumerate((("new_mem_k_prompt", "new_mem_v_prompt"), ("cache_mem_k", "cache_mem_v"))):
                    for dst, name in zip((m_nat, mval), names):
                        setup(dst[:, m, :, :], io[name][0, 0].rearrange("(j p) h d -> p j (h d)", p=P))
                setup(lgt[:], io["hgrn_lb_logits"].rearrange("r (h p) -> p r h", p=P))
                setup(masks[:], io["c_masks"])
                setup(grow[:], io["hgrn_norm_gain"][0].rearrange("h d -> (h d)").partition_broadcast(P))
                setup(state[1][:], io["state_hgrn"][0, 0].rearrange("h d v -> d h v"))

                def loads(i):
                    r, c, j = rows(i), row_slice(i), i % 2
                    w = B_HEADS * r
                    heads = lambda t: t[:, j, 0:w].rearrange("p (h t) -> p h t", h=B_HEADS)
                    feat = lambda d: d[:, c].rearrange("(h p) t -> p h t", p=P)
                    for dst, src in ((q_nat[0:r, j, :], g.d_q[c, :]), (cq[:, j, :, 0:r], feat(g.d_cq)),
                                     (heads(sig), feat(g.d_bf)), (heads(bq), feat(g.d_bq)),
                                     (bv[0:r, j, :], g.d_bi[c, :]), (bg[0:r, j, :], g.d_bg[c, :])):
                        sp.dma_start(dst, src).then_inc(s_in[j], 16)

                def store_y(n, i, row0, heads):
                    r = rows(i)
                    sp.wait_ge(o_kept, n + 1)
                    src = ysb[:, n % 3, 0:heads * r].rearrange("p (h t) -> p h t", h=heads)
                    dst = g.d_y[row0:row0 + heads * HD, row_slice(i)].rearrange("(h p) t -> p h t", p=P)
                    sp.dma_start(dst, src).then_inc(y_out[n % 3], 16)

                loads(0)
                loads(1)
                for i in range(N_TILE):
                    r = rows(i)
                    store_y(3 * i, i, YC0, C_HEADS)
                    store_y(3 * i + 1, i, 0, GROUP)
                    store_y(3 * i + 2, i, GROUP * HD, GROUP)
                    sp.wait_ge(hp_free, hu_y[i])
                    sp.dma_start(g.d_y[YB0:YC0, row_slice(i)].rearrange("(h p) t -> p h t", p=P),
                                 ybT[:, :, 0:r]).then_inc(yb_out, 16)
                    if i + 2 < N_TILE:
                        loads(i + 2)
                for j, (name, i) in enumerate((("new_hgrn_prompt", TILE_P - 1), ("new_hgrn_sample", N_TILE - 1))):
                    sp.wait_ge(hp_free, hu_st[i])
                    sp.dma_start(io[name][0, 0].rearrange("h d v -> d h v"), state[j][:]).then_inc(st_out, 16)
                for j in range(3):
                    sp.wait_ge(y_out[j], 16 * N_TILE)
                sp.wait_ge(yb_out, 16 * N_TILE)
                sp.wait_ge(st_out, 32)

            @block.tensor
            def _(pe):
                tu, su, hu, ou = [0], [0], [0], [0]

                def turn(parts):
                    n = tu[0]
                    if n >= 2:
                        pe.wait_ge(t_kept, n - 1)
                    for c, x in parts:
                        kb, m = x.shape
                        last = pe.transpose(g.ps[0:m, 2 + n % 2, c:c + kb], x, g.ident[0:kb, 0:kb])
                    last.then_inc(t_done, 1)
                    tu[0] += 1
                    return last

                def half_unit(make):
                    n = hu[0]
                    if n >= 2:
                        pe.wait_ge(hp_free, n - 1)
                    for h in range(H3):
                        last = make(g.ps[:, 5 + n % 2, h * P:(h + 1) * P], (n % 2) * H3 + h)
                    last.then_inc(hp_done, 1)
                    hu[0] += 1
                    return last

                def q_turn(i):
                    r = rows(i)
                    pe.wait_ge(s_in[i % 2], 96 * (i // 2 + 1))
                    for h0, h1 in ((0, 4), (4, A_HEADS)):
                        turn([((h - h0) * P, q_nat[0:r, i % 2, h * HD:(h + 1) * HD]) for h in range(h0, h1)])

                def scores(n):
                    i, h = divmod(n, A_HEADS)
                    r, k0 = rows(i), 0 if i < TILE_P else SEQ
                    if h == 0:
                        pe.wait_ge(t_kept, qturned[i])
                    for c in range(0, n_keys(i), 512):
                        w = min(512, n_keys(i) - c)
                        if su[0] >= 2:
                            pe.wait_ge(s_masked, su[0] - 1)
                        pe.matmul(g.ps[0:r, su[0] % 2, 0:w], qT[:, i % 2, h, 0:r],
                                  kT[:, h // GROUP, k0 + c:k0 + c + w], start=True, stop=True).then_inc(s_done, 1)
                        su[0] += 1

                def prob_turn(n):
                    i, h = divmod(n, A_HEADS)
                    r, vt = rows(i), v_tiles(i)
                    pe.wait_ge(p_done, n + 1)
                    for b0 in range(0, len(vt), 4):
                        turn([((b - b0) * P, prob[0:r, n % 3, b * P:b * P + vt[b][1]])
                              for b in range(b0, min(b0 + 4, len(vt)))])
                    if h % GROUP == GROUP - 1:
                        kv = h // GROUP
                        pe.wait_ge(t_kept, tu[0])
                        out = g.ps[:, 4, 0:GROUP * r]
                        if ou[0] >= 1:
                            pe.wait_ge(o_kept, ou[0])
                        for b, (vj, kb) in enumerate(vt):
                            last = pe.matmul(out, val[0:kb, vj, kv * HD:(kv + 1) * HD],
                                             pT[0:kb, b, kv * GROUP:(kv + 1) * GROUP, 0:r],
                                             start=(b == 0), stop=(b == len(vt) - 1))
                        last.then_inc(o_done, 1)
                        ou[0] += 1

                def mem_scores(i):
                    r, m = rows(i), 0 if i < TILE_P else 1
                    pe.wait_ge(s_in[i % 2], 96 * (i // 2 + 1))
                    for pair in range(2):
                        if 2 * i + pair >= 1:
                            pe.wait_ge(c_exp, 2 * i + pair)
                        for e in range(2):
                            last = pe.matmul(g.ps[0:r, 7, e * N_MEM:(e + 1) * N_MEM], cq[:, i % 2, 2 * pair + e, 0:r],
                                             mkT[:, m, 2 * pair + e, :], start=True, stop=True)
                        last.then_inc(c_done, 1)

                def mem_out(i):
                    r, m = rows(i), 0 if i < TILE_P else 1
                    pe.wait_ge(c_norm, i + 1)
                    for pair in range(2):
                        turn([((2 * e + b) * P, cp[0:r, 2 * pair + e, b * P:(b + 1) * P])
                              for e in range(2) for b in range(2)])
                    pe.wait_ge(t_kept, tu[0])
                    if ou[0] >= 1:
                        pe.wait_ge(o_kept, ou[0])
                    for h in range(C_HEADS):
                        for b in range(2):
                            last = pe.matmul(g.ps[:, 4, h * r:(h + 1) * r], mval[:, m, b, h * HD:(h + 1) * HD],
                                             cpT[:, h, b, 0:r], start=(b == 0), stop=(b == 1))
                    last.then_inc(o_done, 1)
                    ou[0] += 1

                def recur_step(i, pos):
                    t, idx, kind = rows(i), STEP0[i] + pos, stages(i)[pos]
                    st, par = state[i // TILE_P], (STEP0[i] + pos) % 2
                    w = lambda h: wk[:, par, h * t:(h + 1) * t]
                    pe.wait_ge(w_done, idx + 1)
                    if kind == "q":
                        pe.wait_ge(hp_free, hu[0])
                        def make(out, h):
                            last = pe.matmul(out[0:t], smat[0:t, h, 0:t], bv[0:t, i % 2, h * HD:(h + 1) * HD],
                                             start=True, stop=(i == 0))
                            if i:
                                last = pe.matmul(out[0:t], w(h), st[:, h, :], start=False, stop=True)
                            return last
                    elif kind == "k":
                        make = lambda out, h: pe.transpose(out[0:t], w(h), g.ident[:])
                    elif kind == 1:
                        make = lambda out, h: pe.matmul(out[0:t, 0:t], kp[:, h * t:(h + 1) * t], w(h), start=True, stop=True)
                    else:
                        make = lambda out, h: pe.matmul(out[0:t, 0:t], w(h), w(h), start=True, stop=True)
                    half_unit(make)
                    half_unit(make)

                def recur_state(i):
                    t = rows(i)
                    pe.wait_ge(hp_free, hu[0])
                    make = lambda out, h: pe.matmul(out, kdT[0:t, h * HD:(h + 1) * HD],
                                                    bv[0:t, i % 2, h * HD:(h + 1) * HD], start=True, stop=True)
                    half_unit(make)
                    half_unit(make)

                def recur_out(i):
                    t = rows(i)
                    pe.wait_ge(y_done, i + 1)
                    make = lambda out, h: pe.transpose(out[:, 0:t], osb[0:t, h * HD:(h + 1) * HD], g.ident[0:t, 0:t])
                    half_unit(make)
                    half_unit(make)

                pe.wait_ge(s_set, N_SET)
                for j, kb, _ in k_rows:
                    turn([(kv * P, k_nat[0:kb, j, kv * HD:(kv + 1) * HD]) for kv in range(A_KV)])
                for m in range(2):
                    for j in range(N_MEM // P):
                        turn([(h * P, m_nat[:, m, j, h * HD:(h + 1) * HD]) for h in range(C_HEADS)])
                q_turn(0)
                for n in range(N_HEAD + 2):
                    i, slot = divmod(n, A_HEADS)
                    if n < N_HEAD:
                        scores(n)
                    if slot == 1 and i < N_TILE:
                        mem_scores(i)
                    if n >= 2:
                        prob_turn(n - 2)
                    if slot == 2 and i + 1 < N_TILE:
                        q_turn(i + 1)
                    if slot == 3:
                        mem_out(i)
                    if slot == 1 and i >= 1:
                        recur_out(i - 1)
                    if i < N_TILE:
                        for pos in due(i, slot - 1):
                            recur_step(i, pos)
                        if slot == 5:
                            recur_state(i)

            @block.scalar
            def _(act):
                tu = [0]

                def keep(copies):
                    act.wait_ge(t_done, tu[0] + 1)
                    for dst, src in copies(g.ps[:, 2 + tu[0] % 2, :]):
                        last = S.activation(dst, src, ACT.Copy)
                    last.then_inc(t_kept, 1)
                    tu[0] += 1

                def q_keep(i):
                    r = rows(i)
                    for h0, h1 in ((0, 4), (4, A_HEADS)):
                        keep(lambda b: [(qT[:, i % 2, h0:h1, 0:r],
                                         b.rearrange("p (h t) -> p h t", t=P)[:, 0:h1 - h0, 0:r])])

                def prob_keep(n):
                    i, h = divmod(n, A_HEADS)
                    r, vt, kv = rows(i), v_tiles(i), h // GROUP
                    if i >= 1:
                        act.wait_ge(o_done, 3 * (i - 1) + 2 + kv)
                    for b0 in range(0, len(vt), 4):
                        bl = range(b0, min(b0 + 4, len(vt)))
                        if all(vt[b][1] == P for b in bl):
                            keep(lambda bank: [(pT[:, b0:b0 + len(bl), h, 0:r],
                                                bank.rearrange("p (b t) -> p b t", t=P)[:, 0:len(bl), 0:r])])
                        else:
                            keep(lambda bank: [(pT[0:vt[b][1], b, h, 0:r],
                                                bank[0:vt[b][1], (b - b0) * P:(b - b0) * P + r]) for b in bl])

                def recur_exp(i, pos):
                    t, idx, kind = rows(i), STEP0[i] + pos, stages(i)[pos]
                    w = B_HEADS * t
                    if kind != "q":
                        act.wait_ge(d_done, dcount(i, pos))
                    if idx >= 2:
                        act.wait_ge(w_done, idx - 1)
                    dst = ex[:, idx % 2, 0:w]
                    if kind == "q":
                        c3 = cum[:, 0:w].rearrange("p (h t) -> p h t", h=B_HEADS)
                        if i >= 1:
                            act.wait_ge(hp_free, hu_st[i - 1])
                        S.activation(eb[:, :], c3[:, :, t - 1], ACT.Exp)
                        S.activation(dst, cum[:, 0:w], ACT.Exp).then_inc(x_done, 1)
                    elif kind == 1:
                        S.activation(exn[:, 0:w], dif[:, idx % 2, 0:w], ACT.Exp, scale=-1.0)
                        S.activation(dst, dif[:, idx % 2, 0:w], ACT.Exp).then_inc(x_done, 1)
                    else:
                        S.activation(dst, dif[:, idx % 2, 0:w], ACT.Exp).then_inc(x_done, 1)

                act.wait_ge(s_lb, 1)
                S.activation(lgt[:], lgt[:], ACT.Exp).then_inc(s_act, 1)
                for j, kb, c0 in k_rows:
                    keep(lambda b: [(kT[:, :, c0:c0 + kb], b.rearrange("p (h t) -> p h t", t=P)[:, 0:A_KV, 0:kb])])
                for m in range(2):
                    for j in range(N_MEM // P):
                        keep(lambda b: [(mkT[:, m, :, j * P:(j + 1) * P], b.rearrange("p (h t) -> p h t", t=P))])
                q_keep(0)
                for n in range(N_HEAD + 2):
                    i, slot = divmod(n, A_HEADS)
                    if n < N_HEAD:
                        r, w = rows(i), n_keys(i)
                        act.wait_ge(ntop_ok, n + 1)
                        if n >= 8:
                            act.wait_ge(p_done, n - 7)
                        S.activation(prob[0:r, n % 3, 0:w], prob[0:r, n % 3, 0:w], ACT.Exp, bias=ntop[0:r, n % 8:n % 8 + 1],
                                     scale=1.0, accum_out=den[0:r, n % 8:n % 8 + 1]).then_inc(e_done, 1)
                    if slot == 1 and i < N_TILE:
                        r = rows(i)
                        for pair in range(2):
                            act.wait_ge(c_top, 2 * i + pair + 1)
                            for h in (2 * pair, 2 * pair + 1):
                                last = S.activation(cp[0:r, h, :], g.ps[0:r, 7, (h % 2) * N_MEM:(h % 2 + 1) * N_MEM],
                                                    ACT.Exp, bias=ctop[0:r, h:h + 1], scale=SCALE,
                                                    accum_out=cden[0:r, h:h + 1])
                            last.then_inc(c_exp, 1)
                    if n >= 2:
                        prob_keep(n - 2)
                    if slot == 2 and i + 1 < N_TILE:
                        q_keep(i + 1)
                    if slot == 3:
                        r = rows(i)
                        if i >= 1:
                            act.wait_ge(o_done, 3 * (i - 1) + 1)
                        for pair in range(2):
                            keep(lambda b: [(cpT[:, 2 * pair:2 * pair + 2, :, 0:r],
                                             b.rearrange("p (h b t) -> p h b t", h=2, b=2)[:, :, :, 0:r])])
                    if i < N_TILE:
                        t = rows(i)
                        if slot == 0:
                            act.wait_ge(f_done, i + 1)
                            if i >= 1:
                                act.wait_ge(x_done, STEP0[i])
                            S.activation(sig[:, i % 2, 0:B_HEADS * t], sig[:, i % 2, 0:B_HEADS * t],
                                         ACT.Ln).then_inc(l_done, 1)
                        for pos in due(i, slot):
                            recur_exp(i, pos)
                        if slot == 5:
                            act.wait_ge(hp_free, hu_step[i, stages(i).index("q")])
                            S.activation(sq[0:t, :], osb[0:t, :], ACT.Square).then_inc(sq_done, 1)
                            act.wait_ge(ms_done, 2 * i + 2)
                            S.activation(ms[0:t, :], ms[0:t, :], ACT.Ln).then_inc(rs_part, 1)
                            act.wait_ge(rs_part, i + 1)
                            S.activation(ms[0:t, :], ms[0:t, :], ACT.Exp, scale=-0.5).then_inc(rs_done, 1)

            @block.gpsimd
            def _(pool):
                pool.wait_ge(s_lb, 2)
                pool.wait_ge(s_set, N_SET)
                G.memset(zero[:], 0.0).then_inc(s_zero, 1)
                for n in range(N_TILE * A_HEADS):
                    i, slot = divmod(n, A_HEADS)
                    t = rows(i)
                    w = B_HEADS * t
                    j = i % 2
                    if slot == 0:
                        pool.wait_ge(s_in[j], 96 * (i // 2 + 1))
                        if i >= 1:
                            pool.wait_ge(w_done, STEP0[i])
                        for h in range(B_HEADS):
                            x = sig[:, j, h * t:(h + 1) * t]
                            last = G.tensor_scalar(x, x, oml[:, h:h + 1], lb[:, h:h + 1], ALU.mult, ALU.add)
                        last.then_inc(f_part, 1)
                        pool.wait_ge(f_part, i + 1)
                        G.tensor_scalar(kk[:, 0:w], sig[:, j, 0:w], -1.0, 1.0, ALU.mult, ALU.add).then_inc(f_done, 1)
                        if i >= 1:
                            pool.wait_ge(hp_done, hu_idx[STEP0[i] - 1])
                        G.memset(smat[:], 0.0).then_inc(s_cleared, 1)
                        G.tensor_tensor(bg[0:t, j, :], bg[0:t, j, :], grow[0:t, :], ALU.mult).then_inc(gg_done, 1)
                    for pos in due(i, slot):
                        idx, kind = STEP0[i] + pos, stages(i)[pos]
                        e, o = ex[:, idx % 2, 0:w], wk[:, idx % 2, 0:w]
                        q = bq[:, j, 0:w]
                        pool.wait_ge(x_done, idx + 1)
                        pool.wait_ge(f_done, i + 1)
                        if idx >= 2:
                            pool.wait_ge(hp_done, hu_idx[idx - 2])
                        if kind == 1:
                            G.tensor_tensor(kp[:, 0:w], kk[:, 0:w], exn[:, 0:w], ALU.mult)
                            G.tensor_tensor(o, q, e, ALU.mult).then_inc(w_done, 1)
                        elif kind == "q":
                            G.tensor_tensor(o, q, e, ALU.mult).then_inc(w_done, 1)
                        elif kind == "k":
                            G.tensor_tensor(o, kk[:, 0:w], e, ALU.mult).then_inc(w_done, 1)
                        else:
                            blk = lambda x: x.rearrange("p (b t) -> p b t", t=2 * kind)
                            G.tensor_tensor(blk(o)[:, :, 0:kind], blk(kk[:, 0:w])[:, :, 0:kind],
                                            blk(e)[:, :, 0:kind], ALU.mult)
                            G.tensor_tensor(blk(o)[:, :, kind:], blk(q)[:, :, kind:],
                                            blk(e)[:, :, kind:], ALU.mult).then_inc(w_done, 1)
                    if slot == 5:
                        pool.wait_ge(rs_done, i + 1)
                        pool.wait_ge(gg_done, i + 1)
                        o3 = osb[0:t, :].rearrange("p (h d) -> p h d", h=B_HEADS)
                        G.tensor_tensor(o3, o3, bcast(ms[0:t, :], HD), ALU.mult).then_inc(y_part, 1)
                        pool.wait_ge(y_part, i + 1)
                        G.tensor_tensor(osb[0:t, :], osb[0:t, :], bg[0:t, j, :], ALU.mult).then_inc(y_done, 1)

            @block.vector
            def _(dve):
                su, hu, ou = [0], [0], [0]
                steps = [0]

                def link(ins):
                    steps[0] += 1
                    ins.then_inc(s_step, 1)
                    dve.wait_ge(s_step, steps[0])

                def half_unit():
                    n = hu[0]
                    dve.wait_ge(hp_done, n + 1)
                    hu[0] += 1
                    return g.ps[:, 5 + n % 2, 0:H3 * P].rearrange("p (h t) -> p h t", h=H3), (n % 2) * H3

                def mask_scores(n):
                    i, h = divmod(n, A_HEADS)
                    r, w = rows(i), n_keys(i)
                    if n >= 3:
                        dve.wait_ge(t_done, prob_turned[n - 3])
                    if n >= 8:
                        dve.wait_ge(e_done, n - 7)
                    tp = top[0:r, n % 8:n % 8 + 1]
                    for c in range(0, w, 512):
                        cw = min(512, w - c)
                        dve.wait_ge(s_done, su[0] + 1)
                        acc = part[0:r, :] if c + cw < w else tp
                        ins = V.tensor_tensor_reduce(prob[0:r, n % 3, c:c + cw], g.ps[0:r, su[0] % 2, 0:cw],
                                                     g.bias[0:r, BIAS_OFF[i] + c:BIAS_OFF[i] + c + cw], SCALE,
                                                     NEG if c == 0 else part[0:r, :], ALU.add, ALU.max, acc)
                        ins.then_inc(s_masked, 1)
                        su[0] += 1
                        dve.wait_ge(s_masked, su[0])
                    V.tensor_scalar(ntop[0:r, n % 8:n % 8 + 1], tp, -1.0, None, ALU.mult).then_inc(ntop_ok, 1)

                def normalise(n):
                    i = n // A_HEADS
                    r, w, d = rows(i), n_keys(i), den[0:rows(i), n % 8:n % 8 + 1]
                    dve.wait_ge(e_done, n + 1)
                    link(V.reciprocal(d, d))
                    V.tensor_scalar(prob[0:r, n % 3, 0:w], prob[0:r, n % 3, 0:w], d, None, ALU.mult).then_inc(p_done, 1)

                def keep_out(w):
                    n = ou[0]
                    dve.wait_ge(o_done, n + 1)
                    if n >= 3:
                        dve.wait_ge(y_out[n % 3], 16 * (n // 3))
                    V.tensor_copy(ysb[:, n % 3, 0:w], g.ps[:, 4, 0:w]).then_inc(o_kept, 1)
                    ou[0] += 1

                def recur_diff(i, pos):
                    t, idx, kind = rows(i), STEP0[i] + pos, stages(i)[pos]
                    w = B_HEADS * t
                    if kind == "q":
                        return
                    if idx >= 2:
                        dve.wait_ge(x_done, idx - 1)
                    b, d = cum[:, 0:w], dif[:, idx % 2, 0:w]
                    if kind == "k":
                        b3, d3 = (x.rearrange("p (h t) -> p h t", h=B_HEADS) for x in (b, d))
                        V.tensor_tensor(d3, b3[:, :, t - 1:t].to_broadcast([P, B_HEADS, t]), b3,
                                        ALU.subtract).then_inc(d_done, 1)
                        return
                    b3, d3 = (x.rearrange("p (b t) -> p b t", t=2 * kind) for x in (b, d))
                    nb = w // (2 * kind)
                    ref = b3[:, :, kind - 1:kind]
                    if kind == 1:
                        V.tensor_tensor(d3, b3, ref.to_broadcast([P, nb, 2]), ALU.subtract).then_inc(d_done, 1)
                    else:
                        ref = ref.to_broadcast([P, nb, kind])
                        V.tensor_tensor(d3[:, :, 0:kind], ref, b3[:, :, 0:kind], ALU.subtract)
                        V.tensor_tensor(d3[:, :, kind:], b3[:, :, kind:], ref, ALU.subtract).then_inc(d_done, 1)

                def recur_keep(i, pos):
                    t, kind = rows(i), stages(i)[pos]
                    if pos == 0:
                        dve.wait_ge(s_cleared, i + 1)
                    if kind == "q" and i >= 1:
                        dve.wait_ge(y_done, i)
                        dve.wait_ge(hp_free, hu[0])
                    for _ in range(2):
                        bank, h0 = half_unit()
                        if kind == "q":
                            dst = osb[0:t, h0 * HD:(h0 + H3) * HD].rearrange("p (h d) -> p h d", h=H3)
                            last = V.tensor_copy(dst, bank[0:t])
                        elif kind == "k":
                            dst = kdT[0:t, h0 * HD:(h0 + H3) * HD].rearrange("p (h d) -> p h d", h=H3)
                            last = V.tensor_copy(dst, bank[0:t])
                        else:
                            m = bcast_mid(masks[0:t, LEVELS.index(kind), 0:t], H3)
                            last = V.copy_predicated(smat[0:t, h0:h0 + H3, 0:t], m, bank[0:t, :, 0:t])
                        last.then_inc(hp_free, 1)

                dve.wait_ge(s_set, N_SET)
                link(V.tensor_tensor(lmx[:], lgt[:, 0, :], lgt[:, 1, :], ALU.max))
                for r in range(2):
                    last = V.tensor_tensor(lgt[:, r, :], lgt[:, r, :], lmx[:], ALU.subtract)
                last.then_inc(s_lb, 1)
                dve.wait_ge(s_act, 1)
                link(V.tensor_tensor(lmx[:], lgt[:, 0, :], lgt[:, 1, :], ALU.add))
                link(V.reciprocal(lmx[:], lmx[:]))
                link(V.tensor_tensor(lb[:], lgt[:, 0, :], lmx[:], ALU.mult))
                V.tensor_scalar(oml[:], lb[:], -1.0, 1.0, ALU.mult, ALU.add).then_inc(s_lb, 1)
                dve.wait_ge(s_zero, 1)
                for n in range(N_HEAD + 2):
                    i, slot = divmod(n, A_HEADS)
                    if n < N_HEAD:
                        mask_scores(n)
                    if slot == 1 and i < N_TILE:
                        r = rows(i)
                        for pair in range(2):
                            dve.wait_ge(c_done, 2 * i + pair + 1)
                            hs = slice(2 * pair, 2 * pair + 2)
                            link(V.tensor_reduce(ctop[0:r, hs], g.ps[0:r, 7, :].rearrange("p (h m) -> p h m", h=2),
                                                 AX.X, ALU.max))
                            V.tensor_scalar(ctop[0:r, hs], ctop[0:r, hs], -SCALE, None, ALU.mult).then_inc(c_top, 1)
                    if 1 <= n <= N_HEAD:
                        normalise(n - 1)
                    if slot == 2 and i < N_TILE:
                        r = rows(i)
                        dve.wait_ge(c_exp, 2 * i + 2)
                        link(V.reciprocal(cden[0:r, :], cden[0:r, :]))
                        V.tensor_tensor(cp[0:r], cp[0:r], bcast(cden[0:r, :], N_MEM), ALU.mult).then_inc(c_norm, 1)
                    if n >= 2 and (n - 2) % GROUP == GROUP - 1:
                        keep_out(GROUP * rows((n - 2) // A_HEADS))
                    if slot == 3:
                        keep_out(C_HEADS * rows(i))
                    if slot == 1 and i >= 1:
                        t = rows(i - 1)
                        if i >= 2:
                            dve.wait_ge(yb_out, 16 * (i - 1))
                        for _ in range(2):
                            bank, h0 = half_unit()
                            V.tensor_copy(ybT[:, h0:h0 + H3, 0:t], bank[:, :, 0:t]).then_inc(hp_free, 1)
                    if i < N_TILE:
                        t = rows(i)
                        if slot == 0:
                            dve.wait_ge(l_done, i + 1)
                            if i >= 1:
                                dve.wait_ge(x_done, STEP0[i])
                            for h in range(B_HEADS):
                                last = V.tensor_tensor_scan(cum[:, h * t:(h + 1) * t], sig[:, i % 2, h * t:(h + 1) * t],
                                                            zero[:, 0:t], 0.0, ALU.add, ALU.add)
                            link(last)
                        for pos in due(i, slot):
                            recur_diff(i, pos)
                        for pos in due(i, slot - 1):
                            recur_keep(i, pos)
                        if slot == 5:
                            st = state[i // TILE_P]
                            for _ in range(2):
                                bank, h0 = half_unit()
                                for h in range(H3):
                                    if i == 0:
                                        last = V.tensor_copy(st[:, h0 + h, :], bank[:, h, :])
                                    else:
                                        last = V.scalar_tensor_tensor(
                                            out=st[:, h0 + h, :], in0=st[:, h0 + h, :], scalar=eb[:, h0 + h:h0 + h + 1],
                                            in1=bank[:, h, :], op0=ALU.mult, op1=ALU.add)
                                last.then_inc(hp_free, 1)
                            dve.wait_ge(sq_done, i + 1)
                            V.tensor_reduce(ms[0:t, :], sq[0:t, :].rearrange("p (h d) -> p h d", h=B_HEADS),
                                            AX.X, ALU.add).then_inc(ms_done, 1)
                            dve.wait_ge(ms_done, 2 * i + 1)
                            V.tensor_scalar(ms[0:t, :], ms[0:t, :], 1.0 / HD, EPS, ALU.mult, ALU.add).then_inc(ms_done, 1)



BRANCHES = [("w_out_a", 0, A_HEADS), ("w_out_b", YB0, B_HEADS), ("w_out_c", YC0, C_HEADS)]


def block_gate_merge(g):
    nc, io = g.nc, g.io
    n0 = g.slab
    slabs = [(b, j) for b in range(3) for j in range(D_MODEL // 256)]
    g.slab += len(slabs)
    units = [(s, b, 2 * j + ft, c0, n) for s, (b, j) in enumerate(slabs) for ft in range(2) for c0, n in GROUPS]
    per_branch = len(units) // 3
    pieces = [(b, k) for b in range(3) for k in range(BRANCHES[b][2])]
    NB, NG = 4, 4
    with ExitStack() as ctx:
        sb = lambda name, shape, dt=F32: ctx.enter_context(nc.sbuf_tensor("gm_" + name, shape, dt))
        y_hi, y_lo = sb("y_hi", [P, 2, A_HEADS, T_ALL], F32R), sb("y_lo", [P, 2, A_HEADS, T_ALL], F32R)
        y_raw, gate, tmp = sb("y_raw", [P, 2, T_ALL]), sb("gate", [P, NG, 384]), sb("tmp", [P, 384])
        sem = lambda name: g.sem("gm_" + name)
        y_in, hi_done, lo_done = [sem("y_in0"), sem("y_in1")], sem("hi"), sem("lo")
        gate_in = [sem(f"gate_in{j}") for j in range(NG)]
        full, gated, summed = sem("full"), sem("gated"), sem("summed")

        with nc.Block() as block:
            @block.sync
            def _(sp):
                def load_piece(m):
                    b, k = pieces[m]
                    if m >= 2:
                        sp.wait_ge(lo_done, m - 1)
                    sp.dma_start(y_raw[:, m % 2, :], g.d_y[BRANCHES[b][1] + k * P:BRANCHES[b][1] + (k + 1) * P, :]
                                 ).then_inc(y_in[m % 2], 16)

                def load_weights(s):
                    b, j = slabs[s]
                    load_slab(g, sp, n0 + s, w_cols(io[BRANCHES[b][0]][0], j * 256, 256), BRANCHES[b][2])

                load_weights(0)
                load_weights(1)
                m = 0
                for b in range(3):
                    while m < len(pieces) and pieces[m][0] <= min(b + 1, 2) and (b > 0 or pieces[m][0] == 0):
                        load_piece(m)
                        m += 1
                        if b == 0:
                            continue
                        break
                    for u in range(b * per_branch, (b + 1) * per_branch):
                        s, _, f, c0, n = units[u]
                        if u >= NG:
                            sp.wait_ge(gated, u - NG + 1)
                        row = b * D_MODEL + f * P
                        sp.dma_start(gate[:, u % NG, 0:n], g.d_gate[row:row + P, c0:c0 + n]).then_inc(gate_in[u % NG], 16)
                        if u % 4 == 3 and m < len(pieces) and pieces[m][0] == b + 1:
                            load_piece(m)
                            m += 1
                        if u % 6 == 5 and s + 2 < len(slabs):
                            load_weights(s + 2)
                assert m == len(pieces)

            @block.gpsimd
            def _(pool):
                for s, (b, j) in enumerate(slabs):
                    split_slab(g, pool, n0 + s, BRANCHES[b][2] * 256)

            @block.scalar
            def _(act):
                for m, (b, k) in enumerate(pieces):
                    act.wait_ge(y_in[m % 2], 16 * (m // 2 + 1))
                    if b == 2:
                        act.wait_ge(full, per_branch)
                    nc.scalar.activation(y_hi[:, b % 2, k, :], y_raw[:, m % 2, :], ACT.Copy).then_inc(hi_done, 1)

            @block.tensor
            def _(pe):
                for u, (s, b, f, c0, n) in enumerate(units):
                    kt = BRANCHES[b][2]
                    if u % per_branch == 0:
                        pe.wait_ge(lo_done, sum(BRANCHES[q][2] for q in range(b + 1)))
                    if u % 6 == 0:
                        pe.wait_ge(g.w_split, n0 + s + 1)
                    if u >= NB:
                        pe.wait_ge(gated, u - NB + 1)
                    w, y = slab_view(g, n0 + s, kt, 256), (y_hi, y_lo)
                    fs, cs = slice((f % 2) * P, (f % 2 + 1) * P), slice(c0, c0 + n)
                    three_products(pe, g.ps[:, u % NB, 0:n], lambda a, k: w[a][:, k, fs],
                                   lambda a, k: y[a][:, b % 2, k, cs], kt).then_inc(full, 1)
                    if u % 6 == 5:
                        pe.drain().then_inc(g.w_used, 1)

            @block.vector
            def _(dve):
                def split(m):
                    b, k = pieces[m]
                    dve.wait_ge(hi_done, m + 1)
                    nc.vector.tensor_tensor(y_lo[:, b % 2, k, :], y_raw[:, m % 2, :],
                                            y_hi[:, b % 2, k, :].bitcast(F32), ALU.subtract).then_inc(lo_done, 1)

                m = 0
                while pieces[m][0] == 0:
                    split(m)
                    m += 1
                for u, (s, b, f, c0, n) in enumerate(units):
                    dve.wait_ge(full, u + 1)
                    dve.wait_ge(gate_in[u % NG], 16 * (u // NG + 1))
                    dst, ps, gt = g.merged[:, f, c0:c0 + n], g.ps[:, u % NB, 0:n], gate[:, u % NG, 0:n]
                    if b == 0:
                        nc.vector.tensor_tensor(dst, ps, gt, ALU.mult).then_inc(gated, 1)
                    else:
                        if u > per_branch:
                            dve.wait_ge(summed, u - per_branch)
                        nc.vector.tensor_tensor(tmp[:, 0:n], ps, gt, ALU.mult).then_inc(gated, 1)
                        dve.wait_ge(gated, u + 1)
                        nc.vector.tensor_tensor(dst, dst, tmp[:, 0:n], ALU.add).then_inc(summed, 1)
                    if u % 4 == 3 and m < len(pieces) and pieces[m][0] == b + 1:
                        split(m)
                        m += 1



def token_srcs(io):
    return [io["x_prompt"][0, i * P:(i + 1) * P, :] for i in range(TILE_P)] + [io["x_sample"][0]]


def block_out(g):
    nc, io = g.nc, g.io
    n0 = g.slab
    NSL = D_MODEL // 256
    g.slab += NSL
    NB = 4
    units = [(s, i) for s in range(NSL) for i in range(N_TILE)]
    spare = lambda k: g.big[:, k * D_MODEL:(k + 1) * D_MODEL]
    gain, junk, xin, x2 = spare(0), spare(1), [spare(2), spare(3)], [spare(4), spare(5)]
    with ExitStack() as ctx:
        sb = lambda name, shape: ctx.enter_context(nc.sbuf_tensor("out_" + name, shape, F32))
        o_all = sb("o_all", [P, N_TILE, D_MODEL])
        ss, s2 = sb("ss", [P, N_TILE]), sb("s2", [P, N_TILE])
        sem = lambda name: g.sem("out_" + name)
        hi_done, lo_done, full, kept = sem("hi"), sem("lo"), sem("full"), sem("kept")
        gain_in, x_in, x2_out = sem("gain_in"), [sem("x_in0"), sem("x_in1")], [sem("x2_out0"), sem("x2_out1")]
        sq1, v1, r1, q1, n1, x2_done, sq2, v2, r2, q2, n2 = (sem(n) for n in (
            "sq1", "v1", "r1", "q1", "n1", "x2_done", "sq2", "v2", "r2", "q2", "n2"))
        t_done, t_hi, t_lo, zeroed = sem("t_done"), sem("t_hi"), sem("t_lo"), sem("zeroed")
        srcs = token_srcs(io)
        turns = [(k, c0, n) for k in range(KT) for c0, n in GROUPS]

        with nc.Block() as block:
            def store(sp, i):
                sp.wait_ge(x2_done, i + 1)
                sp.dma_start(g.d_x2[row_slice(i), :], x2[i % 2][0:rows(i), :]).then_inc(x2_out[i % 2], 16)

            @block.sync
            def _(sp):
                for s in range(NSL):
                    load_slab(g, sp, n0 + s, w_cols(io["w_out"][0], s * 256, 256), KT)
                sp.wait_ge(lo_done, KT)
                sp.dma_start(gain, io["post_mix_gain"][0].partition_broadcast(P)).then_inc(gain_in, 16)
                for i in range(N_TILE):
                    r = rows(i)
                    if i >= 2:
                        sp.wait_ge(x2_done, i - 1)
                    sp.dma_start(xin[i % 2][0:r, :], srcs[i]).then_inc(x_in[i % 2], 16)
                    if i >= 1:
                        store(sp, i - 1)
                store(sp, N_TILE - 1)
                sp.wait_ge(x2_out[0], 16 * ((N_TILE + 1) // 2))
                sp.wait_ge(x2_out[1], 16 * (N_TILE // 2))

            @block.gpsimd
            def _(pool):
                for s in range(NSL):
                    split_slab(g, pool, n0 + s, SLAB)

            @block.scalar
            def _(act):
                for k in range(KT):
                    nc.scalar.activation(g.h_hi[:, k, 0:T_ALL], g.merged[:, k, :], ACT.Copy).then_inc(hi_done, 1)
                for u, (s, i) in enumerate(units):
                    act.wait_ge(full, u + 1)
                    nc.scalar.activation(o_all[0:rows(i), i, s * 256:(s + 1) * 256], g.ps[0:rows(i), u % NB, 0:256],
                                         ACT.Copy).then_inc(kept, 1)
                    if s == NSL - 1:
                        r = rows(i)
                        if i == 0:
                            act.wait_ge(lo_done, KT)
                        act.wait_ge(kept, u + 1)
                        if i:
                            act.wait_ge(sq2, i)
                        nc.scalar.activation(junk[0:r, :], o_all[0:r, i, :], ACT.Square,
                                             accum_out=ss[0:r, i:i + 1]).then_inc(sq1, 1)
                        act.wait_ge(v1, i + 1)
                        nc.scalar.activation(ss[0:r, i:i + 1], ss[0:r, i:i + 1], ACT.Sqrt).then_inc(r1, 1)
                        act.wait_ge(x2_done, i + 1)
                        nc.scalar.activation(junk[0:r, :], x2[i % 2][0:r, :], ACT.Square,
                                             accum_out=s2[0:r, i:i + 1]).then_inc(sq2, 1)
                        act.wait_ge(v2, i + 1)
                        nc.scalar.activation(s2[0:r, i:i + 1], s2[0:r, i:i + 1], ACT.Sqrt).then_inc(r2, 1)
                for u, (k, c0, n) in enumerate(turns):
                    act.wait_ge(t_done, u + 1)
                    nc.scalar.activation(g.h_hi[:, k, c0:c0 + n], g.ps[:, u % 8, 0:n], ACT.Copy,
                                         scale=g.gains[:, 2, k:k + 1]).then_inc(t_hi, 1)

            @block.tensor
            def _(pe):
                pe.wait_ge(lo_done, KT)
                pe.wait_ge(zeroed, 2)
                x = (g.h_hi, g.h_lo)
                for u, (s, i) in enumerate(units):
                    if i == 0:
                        pe.wait_ge(g.w_split, n0 + s + 1)
                    if u >= NB:
                        pe.wait_ge(kept, u - NB + 1)
                    w, c = slab_view(g, n0 + s, KT, 256), slice(i * P, (i + 1) * P)
                    three_products(pe, g.ps[:, u % NB, 0:256], lambda a, k: x[a][:, k, c],
                                   lambda b, k: w[b][:, k, :], KT).then_inc(full, 1)
                    if i == N_TILE - 1:
                        pe.drain().then_inc(g.w_used, 1)
                pe.wait_ge(n2, N_TILE)
                for u, (k, c0, n) in enumerate(turns):
                    if u >= 8:
                        pe.wait_ge(t_lo, u - 7)
                    for j in range(-(-n // P)):
                        i = c0 // P + j
                        r = rows(i)
                        last = pe.transpose(g.ps[:, u % 8, j * P:j * P + r], o_all[0:r, i, k * P:(k + 1) * P],
                                            g.ident[0:r, 0:r])
                    last.then_inc(t_done, 1)

            @block.vector
            def _(dve):
                V = nc.vector
                for t in (g.h_hi, g.h_lo):
                    V.memset(t[:, :, T_ALL:T_PAD].bitcast(F32), 0.0).then_inc(zeroed, 1)
                for k in range(KT):
                    dve.wait_ge(hi_done, k + 1)
                    V.tensor_tensor(g.h_lo[:, k, 0:T_ALL], g.merged[:, k, :], g.h_hi[:, k, 0:T_ALL].bitcast(F32),
                                    ALU.subtract).then_inc(lo_done, 1)
                dve.wait_ge(gain_in, 16)
                for i in range(N_TILE):
                    r = rows(i)
                    o, a, b = o_all[0:r, i, :], ss[0:r, i:i + 1], s2[0:r, i:i + 1]
                    x_new = x2[i % 2][0:r, :]
                    dve.wait_ge(sq1, i + 1)
                    V.tensor_scalar(a, a, 1.0 / D_MODEL, EPS, ALU.mult, ALU.add).then_inc(v1, 1)
                    dve.wait_ge(r1, i + 1)
                    V.reciprocal(a, a).then_inc(q1, 1)
                    dve.wait_ge(q1, i + 1)
                    V.scalar_tensor_tensor(out=o, in0=o, scalar=a, in1=gain[0:r, :],
                                           op0=ALU.mult, op1=ALU.mult).then_inc(n1, 1)
                    dve.wait_ge(n1, i + 1)
                    dve.wait_ge(x_in[i % 2], 16 * (i // 2 + 1))
                    if i >= 2:
                        dve.wait_ge(x2_out[i % 2], 16 * (i // 2))
                    V.tensor_tensor(x_new, o, xin[i % 2][0:r, :], ALU.add).then_inc(x2_done, 1)
                    dve.wait_ge(sq2, i + 1)
                    V.tensor_scalar(b, b, 1.0 / D_MODEL, EPS, ALU.mult, ALU.add).then_inc(v2, 1)
                    dve.wait_ge(r2, i + 1)
                    V.reciprocal(b, b).then_inc(q2, 1)
                    dve.wait_ge(q2, i + 1)
                    V.tensor_scalar(o, x_new, b, None, ALU.mult).then_inc(n2, 1)
                for u, (k, c0, n) in enumerate(turns):
                    dve.wait_ge(t_hi, u + 1)
                    V.scalar_tensor_tensor(out=g.h_lo[:, k, c0:c0 + n], in0=g.ps[:, u % 8, 0:n],
                                           scalar=g.gains[:, 2, k:k + 1], in1=g.h_hi[:, k, c0:c0 + n].bitcast(F32),
                                           op0=ALU.mult, op1=ALU.subtract).then_inc(t_lo, 1)



FF_G = 512
FK = FF_G // P


def block_ffn(g):
    nc, io = g.nc, g.io
    n0 = g.slab
    N_GRP = D_FF // FF_G
    g.slab += 4 * N_GRP
    assert n0 % 2 == 0
    w_up, w_down = io["w_up"][0], io["w_down"][0]
    acc = g.big[:].rearrange("p (i c) -> p i c", c=D_MODEL)
    ups = [(f, c0, n) for f in range(FK) for c0, n in GROUPS]
    downs = [(half, i) for half in range(2) for i in range(N_TILE)]
    NU, ND = len(ups), len(downs)
    B_UP, B_DN = 4, 3
    LEAD = 4
    with ExitStack() as ctx:
        sb = lambda name, shape, dt=F32: ctx.enter_context(nc.sbuf_tensor("ff_" + name, shape, dt))
        u_hi, u_lo = sb("u_hi", [P, FK, T_PAD], F32R), sb("u_lo", [P, FK, T_PAD], F32R)
        relu, sq, tick = sb("relu", [P, 2, 384]), sb("sq", [P, 2, 384]), sb("tick", [P, 2])
        sem = lambda name: g.sem("ff_" + name)
        (up_full, up_free, squared, sq_made, u_ready, dn_full, acc_done, group_done, zeroed) = (sem(n) for n in (
            "up_full", "up_free", "squared", "sq_made", "u_ready", "dn_full", "acc_done", "group_done", "zeroed"))

        with nc.Block() as block:
            @block.sync
            def _(sp):
                with sp.Fori(0, N_GRP) as i:
                    for s in range(4):
                        n = n0 + 4 * i + s
                        slot = s % 2
                        sp.wait_ge(g.w_split, n - 1)
                        if s < 2:
                            src = w_up[:, bass.ds(i * FF_G + s * 256, 256)].rearrange("(k p) c -> p k c", p=P)
                            k = KT
                        else:
                            src = w_down[bass.ds(i * FF_G, FF_G), (s - 2) * 512:(s - 1) * 512].rearrange(
                                "(k p) c -> p k c", p=P)
                            k = FK
                        sp.dma_start(g.w_raw[:, slot, :].rearrange("p (k c) -> p k c", k=k), src
                                     ).then_inc(g.w_loaded[slot], 16)

            @block.gpsimd
            def _(pool):
                G = nc.gpsimd
                G.memset(tick[:], 0.0).then_inc(zeroed, 1)
                G.memset(u_hi[:, :, T_ALL:T_PAD].bitcast(F32), 0.0).then_inc(zeroed, 1)
                G.memset(u_lo[:, :, T_ALL:T_PAD].bitcast(F32), 0.0).then_inc(zeroed, 1)
                pool.wait_ge(zeroed, 3)
                with pool.Fori(0, N_GRP) as i:
                    for s in range(4):
                        n, slot = n0 + 4 * i + s, s % 2
                        pool.wait_ge(g.w_loaded[slot], 16 * (n0 // 2 + 2 * i + s // 2 + 1))
                        pool.wait_ge(g.w_used, n - 1)
                        G.tensor_tensor(tick[:, 0:1], tick[:, 1:2], tick[:, 1:2], ALU.mult)
                        G.tensor_copy(g.w_hi[:, slot, :], g.w_raw[:, slot, :]).then_inc(g.w_rounded, 1)
                        pool.wait_ge(g.w_rounded, n + 1)
                        G.tensor_tensor(g.w_lo[:, slot, :], g.w_raw[:, slot, :], g.w_hi[:, slot, :].bitcast(F32),
                                        ALU.subtract).then_inc(g.w_split, 1)

            @block.scalar
            def _(act):
                S = nc.scalar
                with act.Fori(0, N_GRP) as i:
                    for u, (f, c0, n) in enumerate(ups):
                        act.wait_ge(up_full, i * NU + u + 1)
                        act.wait_ge(u_ready, i * NU + u - 1 + LEAD)
                        S.activation(relu[:, u % 2, 0:n], g.ps[:, u % B_UP, 0:n], ACT.Relu).then_inc(up_free, 1)
                        act.wait_ge(up_free, i * NU + u + 1 + LEAD)
                        if u == 0:
                            act.wait_ge(group_done, i + 1)
                        S.activation(u_hi[:, f, c0:c0 + n], relu[:, u % 2, 0:n], ACT.Square).then_inc(squared, 1)

            @block.vector
            def _(dve):
                V = nc.vector
                for half, t in downs:
                    V.memset(acc[:, t, half * 512:(half + 1) * 512], 0.0).then_inc(acc_done, 1)
                V.memset(sq[:, 0, 0:1], 0.0).then_inc(u_ready, LEAD)
                V.memset(sq[:, 0, 1:2], 0.0).then_inc(up_free, LEAD)
                V.memset(sq[:, 0, 2:3], 0.0).then_inc(group_done, 1)
                dve.wait_ge(group_done, 1)
                with dve.Fori(0, N_GRP) as i:
                    for u, (f, c0, n) in enumerate(ups):
                        dve.wait_ge(up_free, i * NU + u + 1 + LEAD)
                        V.tensor_tensor(sq[:, u % 2, 0:n], relu[:, u % 2, 0:n], relu[:, u % 2, 0:n],
                                        ALU.mult).then_inc(sq_made, 1)
                        dve.wait_ge(sq_made, i * NU + u + 1)
                        dve.wait_ge(squared, i * NU + u + 1)
                        V.tensor_tensor(u_lo[:, f, c0:c0 + n], sq[:, u % 2, 0:n], u_hi[:, f, c0:c0 + n].bitcast(F32),
                                        ALU.subtract).then_inc(u_ready, 1)
                    for d, (half, t) in enumerate(downs):
                        dst = acc[:, t, half * 512:(half + 1) * 512]
                        dve.wait_ge(dn_full, i * ND + d + 1)
                        dve.wait_ge(acc_done, i * ND + d + 1)
                        V.tensor_tensor(dst, dst, g.ps[:, 4 + d % B_DN, :], ALU.add).then_inc(acc_done, 1)

            @block.tensor
            def _(pe):
                pe.wait_ge(zeroed, 3)
                x, uu = (g.h_hi, g.h_lo), (u_hi, u_lo)
                with pe.Fori(0, N_GRP) as i:
                    for u, (f, c0, n) in enumerate(ups):
                        if u % 6 == 0:
                            pe.wait_ge(g.w_split, n0 + 4 * i + u // 6 + 1)
                        pe.wait_ge(up_free, i * NU + u - B_UP + 1 + LEAD)
                        w = slab_view(g, u // 6, KT, 256)
                        fs, cs = slice((f % 2) * P, (f % 2 + 1) * P), slice(c0, c0 + n)
                        three_products(pe, g.ps[:, u % B_UP, 0:n], lambda a, k: w[a][:, k, fs],
                                       lambda b, k: x[b][:, k, cs], KT).then_inc(up_full, 1)
                        if u % 6 == 5:
                            pe.drain().then_inc(g.w_used, 1)
                    pe.wait_ge(u_ready, i * NU + NU + LEAD)
                    for d, (half, t) in enumerate(downs):
                        if t == 0:
                            pe.wait_ge(g.w_split, n0 + 4 * i + 3 + half)
                        pe.wait_ge(acc_done, i * ND + d - B_DN + 1 + ND)
                        w, c = slab_view(g, half, FK, 512), slice(t * P, (t + 1) * P)
                        three_products(pe, g.ps[:, 4 + d % B_DN, :], lambda a, k: uu[a][:, k, c],
                                       lambda b, k: w[b][:, k, :], FK).then_inc(dn_full, 1)
                        if t == N_TILE - 1:
                            pe.drain().then_inc(g.w_used, 1)
                    pe.drain().then_inc(group_done, 1)



def block_final(g):
    nc, io = g.nc, g.io
    acc = g.big[:].rearrange("p (i c) -> p i c", c=D_MODEL)
    with ExitStack() as ctx:
        sb = lambda name, shape: ctx.enter_context(nc.sbuf_tensor("fin_" + name, shape, F32))
        gain, junk, x2, ss = sb("gain", [P, D_MODEL]), sb("junk", [P, D_MODEL]), sb("x2", [P, N_TILE, D_MODEL]), sb("ss", [P, N_TILE])
        sem = lambda name: g.sem("fin_" + name)
        gain_in, x_in = sem("gain_in"), g.arrived
        sq, v, r_, q, n_, done, out, zeroed = (sem(n) for n in ("sq", "v", "r", "q", "n", "done", "out", "zeroed"))
        outs = [io["y_prompt"][0, i * P:(i + 1) * P, :] for i in range(TILE_P)] + [io["y_sample"][0]]
        with nc.Block() as block:
            @block.sync
            def _(sp):
                sp.dma_start(gain[:], io["post_ffn_gain"][0].partition_broadcast(P)).then_inc(gain_in, 16)
                for i in range(N_TILE):
                    sp.dma_start(x2[0:rows(i), i, :], g.d_x2[row_slice(i), :]).then_inc(x_in[i], 16)
                for i in range(N_TILE):
                    sp.wait_ge(done, i + 1)
                    sp.dma_start(outs[i], x2[0:rows(i), i, :]).then_inc(out, 16)
                sp.wait_ge(out, 16 * N_TILE)

            @block.scalar
            def _(act):
                act.wait_ge(zeroed, 1)
                for i in range(N_TILE):
                    r = rows(i)
                    if i:
                        act.wait_ge(sq, i)
                    nc.scalar.activation(junk[0:r, :], acc[0:r, i, :], ACT.Square,
                                         accum_out=ss[0:r, i:i + 1]).then_inc(sq, 1)
                act.wait_ge(v, 1)
                nc.scalar.activation(ss[:], ss[:], ACT.Sqrt).then_inc(r_, 1)

            @block.vector
            def _(dve):
                V = nc.vector
                V.memset(ss[:], 1.0).then_inc(zeroed, 1)
                dve.wait_ge(sq, N_TILE)
                V.tensor_scalar(ss[:], ss[:], 1.0 / D_MODEL, EPS, ALU.mult, ALU.add).then_inc(v, 1)
                dve.wait_ge(r_, 1)
                V.reciprocal(ss[:], ss[:]).then_inc(q, 1)
                dve.wait_ge(q, 1)
                dve.wait_ge(gain_in, 16)
                for i in range(N_TILE):
                    r = rows(i)
                    a = acc[0:r, i, :]
                    V.scalar_tensor_tensor(out=a, in0=a, scalar=ss[0:r, i:i + 1], in1=gain[0:r, :],
                                           op0=ALU.mult, op1=ALU.mult).then_inc(n_, 1)
                    dve.wait_ge(n_, i + 1)
                    dve.wait_ge(x_in[i], 32)
                    V.tensor_tensor(x2[0:r, i, :], a, x2[0:r, i, :], ALU.add).then_inc(done, 1)



_INS = ["x_prompt", "x_sample", "cache_k", "cache_v", "cache_idx_k", "state_hgrn", "cache_mem_k", "cache_mem_v",
        "mem_prompt", "w_in", "w_mem_kv", "mem_norm_gain", "hgrn_lb_logits", "hgrn_norm_gain", "w_out_a", "w_out_b",
        "w_out_c", "w_out", "pre_mix_gain", "post_mix_gain", "pre_ffn_gain", "post_ffn_gain", "w_up", "w_down"]
_OUTS = [("y_prompt", (1, SEQ, D_MODEL)), ("y_sample", (1, DEC, D_MODEL)),
         ("new_k_prompt", (1, 1, SEQ, A_KV, HD)), ("new_v_prompt", (1, 1, SEQ, A_KV, HD)),
         ("new_idx_k_prompt", (1, 1, SEQ, IDX_D)), ("new_hgrn_prompt", (1, 1, B_HEADS, HD, HD)),
         ("new_mem_k_prompt", (1, 1, N_MEM, C_HEADS, HD)), ("new_mem_v_prompt", (1, 1, N_MEM, C_HEADS, HD)),
         ("new_k_sample", (1, 1, DEC, A_KV, HD)), ("new_v_sample", (1, 1, DEC, A_KV, HD)),
         ("new_idx_k_sample", (1, 1, DEC, IDX_D)), ("new_hgrn_sample", (1, 1, B_HEADS, HD, HD))]


def _constants():
    pos = np.concatenate([np.arange(SEQ), PAST + np.arange(DEC)]).astype(np.float32)
    rope = np.zeros((N_TILE * P, ROPE_W), np.float32)
    for half, c, s in ((HD // 8, OFF_COS, OFF_SIN), (IDX_D // 8, OFF_ICOS, OFF_ISIN)):
        freq = np.float32(500000.0) ** (-np.arange(half, dtype=np.float32) / np.float32(half))
        ang = pos[:, None] * freq[None, :].astype(np.float32)
        rope[:T_ALL, c:c + half], rope[:T_ALL, s:s + half] = np.cos(ang), np.sin(ang)
    s, t = np.arange(P)[:, None], np.arange(P)[None, :]
    masks = []
    for h in LEVELS:
        same = s // (2 * h) == t // (2 * h)
        masks.append(same & (s <= t) if h == 1 else same & (s % (2 * h) < h) & (t % (2 * h) >= h))
    return {"c_ident": np.eye(P, dtype=np.float32),
            "c_rope": np.ascontiguousarray(rope.reshape(N_TILE, P, ROPE_W).transpose(1, 0, 2)),
            "c_masks": np.ascontiguousarray(np.stack(masks, 1).astype(np.int32))}


def kernel(**inputs):
    import numpy as _np
    import concourse.bacc as _bacc
    from concourse import mybir as _mybir
    from concourse.bass_utils import run_bass_kernel_spmd as _run

    nc = _bacc.Bacc("TRN2", target_bir_lowering=False, num_devices=1)
    arrays = {f"in_{n}": _np.ascontiguousarray(inputs[n]) for n in _INS}
    arrays.update({f"in_{n}": a for n, a in _constants().items()})
    io = {n[3:]: nc.dram_tensor(n, a.shape, _mybir.dt.from_np(a.dtype), kind="ExternalInput").ap()
          for n, a in arrays.items()}
    for name, shape in _OUTS:
        io[name] = nc.dram_tensor(f"out_{name}", shape, _mybir.dt.float32, kind="ExternalOutput").ap()
    build(nc, io)
    r = _run(nc, [arrays], core_ids=[0])
    return tuple(r.results[0][f"out_{name}"] for name, _ in _OUTS)
```

```python
from contextlib import ExitStack

import numpy as np
import concourse.bass as bass
from concourse import mybir

P = 128
D_MODEL, SEQ, DEC, PAST, N_MEM = 1024, 1024, 64, 128, 256
HD, IDX_D = 128, 64
A_HEADS, A_KV, IDX_HEADS, B_HEADS, C_HEADS = 6, 2, 8, 6, 4
GROUP = A_HEADS // A_KV
A_W, KV_W, IDX_W = A_HEADS * HD, A_KV * HD, IDX_HEADS * IDX_D
B_W, C_W = B_HEADS * HD, C_HEADS * HD
D_FF = 4 * D_MODEL
EPS, NEG, MASKED = 1e-6, -3.0e38, 1.0e30
TOPK_P, TOPK_S = min(256, SEQ // 4), min(256, (PAST + DEC) // 4)

T_ALL = SEQ + DEC
T_PAD = -(-T_ALL // P) * P
N_TILE = T_PAD // P
TILE_P = SEQ // P
KT = D_MODEL // P
GROUPS = [(0, 384), (384, 384), (768, T_ALL - 768)]
SLAB = 2048
SCALE = float(HD) ** -0.5
IDX_SCALE = float(IDX_D) ** -0.5 * float(IDX_HEADS) ** -0.5

OFF_Q = 0
OFF_K = OFF_Q + A_W
OFF_V = OFF_K + KV_W
OFF_IQ = OFF_V + KV_W
OFF_IK = OFF_IQ + IDX_W
OFF_IW = OFF_IK + IDX_D
OFF_BQ = OFF_IW + IDX_HEADS
OFF_BF = OFF_BQ + B_W
OFF_BI = OFF_BF + B_W
OFF_BG = OFF_BI + B_W
OFF_CQ = OFF_BG + B_W
OFF_G = OFF_CQ + C_W
IDX_KW = IDX_D + IDX_HEADS

F32, F32R, I32 = mybir.dt.float32, mybir.dt.float32r, mybir.dt.int32
ALU, ACT, AX = mybir.AluOpType, mybir.ActivationFunctionType, mybir.AxisListType

LEVELS = [1, 2, 4, 8, 16, 32, 64]
OFF_COS, OFF_SIN = 0, 16
OFF_ICOS, OFF_ISIN = 32, 40
ROPE_W = 48


class Shared:
    pass


class IndexBuffers:
    pass


class ForgetBuffers:
    pass


class SlabPlan:

    def __init__(self, kind, w, cols, units, func, rope=None, mem=False):
        self.kind, self.w, self.cols, self.units = kind, w, cols, units
        self.func, self.rope, self.mem = func, rope, mem


def rows(i):
    return P if i < TILE_P else DEC


def n_keys(i):
    return (i + 1) * P if i < TILE_P else PAST + DEC


BIAS_OFF = [sum(n_keys(j) for j in range(i)) for i in range(N_TILE + 1)]


def bcast(ap, n):
    return ap.unsqueeze(2).to_broadcast([ap.shape[0], ap.shape[1], n])


def bcast_mid(ap, n):
    return ap.unsqueeze(1).to_broadcast([ap.shape[0], n, ap.shape[1]])


def build(nc, io):
    with ExitStack() as ctx:
        g = Shared()
        g.nc, g.io = nc, io
        g.sb = lambda name, shape, dt=F32: ctx.enter_context(nc.sbuf_tensor(name, shape, dt))
        g.sem = lambda name: ctx.enter_context(nc.semaphore(name))
        g.ps = ctx.enter_context(nc.psum_tensor("ps", [P, 8, 512], F32))
        dram = lambda name, shape: nc.dram_tensor(name, shape, F32, kind="Internal").ap()
        g.d_q = dram("d_q", (T_ALL, A_W))
        g.d_iq = dram("d_iq", (T_ALL, IDX_W))
        g.d_ik = dram("d_ik", (T_ALL, IDX_KW))
        g.d_bq = dram("d_bq", (B_W, T_ALL))
        g.d_cum = dram("d_cum", (B_W, T_ALL))
        g.d_kk = dram("d_kk", (B_W, T_ALL))
        g.d_bi = dram("d_bi", (T_ALL, B_W))
        g.d_bg = dram("d_bg", (T_ALL, B_W))
        g.d_cq = dram("d_cq", (C_W, T_ALL))
        g.d_gate = dram("d_gate", (3 * D_MODEL, T_ALL))
        g.d_y = dram("d_y", (A_W + B_W + C_W, T_ALL))
        g.d_x2 = dram("d_x2", (T_ALL, D_MODEL))

        g.ident = g.sb("ident", [P, P])
        g.gains = g.sb("gains", [P, 3, KT])
        ring_semaphores(g)
        with ExitStack() as mid:
            g.bias = mid.enter_context(nc.sbuf_tensor("bias", [P, BIAS_OFF[N_TILE]], F32))
            with ExitStack() as first:
                weight_ring(g, first, "w1")
                g.h_hi = first.enter_context(nc.sbuf_tensor("h_hi", [P, KT, T_PAD], F32R))
                g.h_lo = first.enter_context(nc.sbuf_tensor("h_lo", [P, KT, T_PAD], F32R))
                with ExitStack() as c0:
                    g.m_hi = c0.enter_context(nc.sbuf_tensor("m_hi", [P, KT, N_MEM], F32R))
                    g.m_lo = c0.enter_context(nc.sbuf_tensor("m_lo", [P, KT, N_MEM], F32R))
                    plans = plan_first(g), plan_second(g)
                    block_norm(g, plans[0][:2])
                    block_project(g, "b1", plans[0], False, plans[1][:2])
                block_project(g, "b2", plans[1], True, [])
            block_branches(g)
        with ExitStack() as last:
            weight_ring(g, last, "w2")
            g.big = last.enter_context(nc.sbuf_tensor("big", [P, N_TILE * D_MODEL], F32))
            g.merged = g.big[:, 0:KT * T_ALL].rearrange("p (k t) -> p k t", k=KT)
            block_gate_merge(g)
            g.h_hi = last.enter_context(nc.sbuf_tensor("f_hi", [P, KT, T_PAD], F32R))
            g.h_lo = last.enter_context(nc.sbuf_tensor("f_lo", [P, KT, T_PAD], F32R))
            block_out(g)
            block_ffn(g)
            block_final(g)



def weight_ring(g, ctx, tag):
    sb = lambda name, dt: ctx.enter_context(g.nc.sbuf_tensor(f"{tag}_{name}", [P, 2, SLAB], dt))
    g.w_raw, g.w_hi, g.w_lo = sb("raw", F32), sb("hi", F32R), sb("lo", F32R)


def ring_semaphores(g):
    g.slab = 0
    g.arrived = [g.sem(f"arrived{i}") for i in range(N_TILE + N_MEM // P)]
    g.w_loaded = [g.sem("w_loaded0"), g.sem("w_loaded1")]
    g.w_rounded = g.sem("w_rounded")
    g.w_split = g.sem("w_split")
    g.w_used = g.sem("w_used")


def load_slab(g, sp, n, src, k):
    if n >= 2:
        sp.wait_ge(g.w_split, n - 1)
    cols = src.shape[2]
    dst = g.w_raw[:, n % 2, 0:k * cols].rearrange("p (k c) -> p k c", k=k)
    sp.dma_start(dst, src).then_inc(g.w_loaded[n % 2], 16)


def round_slab(g, act, n, size):
    s = n % 2
    act.wait_ge(g.w_loaded[s], 16 * (n // 2 + 1))
    if n >= 2:
        act.wait_ge(g.w_used, n - 1)
    g.nc.scalar.activation(g.w_hi[:, s, 0:size], g.w_raw[:, s, 0:size], ACT.Copy).then_inc(g.w_rounded, 1)


def split_slab(g, pool, n, size):
    s = n % 2
    pool.wait_ge(g.w_rounded, n + 1)
    g.nc.gpsimd.tensor_tensor(g.w_lo[:, s, 0:size], g.w_raw[:, s, 0:size], g.w_hi[:, s, 0:size].bitcast(F32),
                              ALU.subtract).then_inc(g.w_split, 1)


def slab_view(g, n, k, cols):
    s = n % 2
    return [w[:, s, 0:k * cols].rearrange("p (k c) -> p k c", k=k) for w in (g.w_hi, g.w_lo)]


def three_products(pe, out, left, right, k):
    for kk in range(k):
        for n, (a, b) in enumerate(((0, 0), (0, 1), (1, 0))):
            last = pe.matmul(out, left(a, kk), right(b, kk),
                             start=(kk == 0 and n == 0), stop=(kk == k - 1 and n == 2))
    return last


def w_cols(w, c0, n):
    return w[:, c0:c0 + n].rearrange("(k p) c -> p k c", p=P)



def block_norm(g, ahead):
    nc, io = g.nc, g.io
    NT = N_TILE + N_MEM // P
    with ExitStack() as ctx:
        xs = ctx.enter_context(nc.sbuf_tensor("n_x", [P, NT, D_MODEL], F32))
        junk = ctx.enter_context(nc.sbuf_tensor("n_junk", [P, D_MODEL], F32))
        ss = ctx.enter_context(nc.sbuf_tensor("n_ss", [P, NT], F32))
        rs = ctx.enter_context(nc.sbuf_tensor("n_rs", [P, NT], F32))
        x_in = g.arrived
        c_in, zeroed, squared, mean, root = (g.sem("n_const"), g.sem("n_zero"), g.sem("n_sq"),
                                             g.sem("n_mean"), g.sem("n_root"))
        scaled, turned, hi_done, lo_done = g.sem("n_scaled"), g.sem("n_turned"), g.sem("n_hi"), g.sem("n_lo")
        srcs = [io["x_prompt"][0, i * P:(i + 1) * P, :] for i in range(TILE_P)] + [io["x_sample"][0]]
        srcs += [io["mem_prompt"][0, i * P:(i + 1) * P, :] for i in range(N_MEM // P)]
        units = []
        for k in range(KT):
            for c0, n in GROUPS:
                units.append((k, 0, [c0 // P + j for j in range(-(-n // P))], c0, n))
            units.append((k, 1, [N_TILE + j for j in range(N_MEM // P)], 0, N_MEM))

        with nc.Block() as block:
            @block.sync
            def _(sp):
                sp.dma_start(g.ident[:], io["c_ident"]).then_inc(c_in, 16)
                for j, name in enumerate(("pre_mix_gain", "mem_norm_gain", "pre_ffn_gain")):
                    sp.dma_start(g.gains[:, j, :], io[name][0].rearrange("(k p) -> p k", p=P),
                                 allow_slow_non_contiguous=True).then_inc(c_in, 16)
                for i, src in enumerate(srcs):
                    sp.dma_start(xs[0:src.shape[0], i, :], src).then_inc(x_in[i], 16)
                for n in range(2):
                    load_slab(g, sp, n, ahead[n].w, KT)

            @block.gpsimd
            def _(pool):
                split_slab(g, pool, 0, KT * ahead[0].cols)

            @block.scalar
            def _(act):
                act.wait_ge(zeroed, 1)
                for i, src in enumerate(srcs):
                    r = src.shape[0]
                    act.wait_ge(x_in[i], 16)
                    if i:
                        act.wait_ge(squared, i)
                    nc.scalar.activation(junk[0:r, :], xs[0:r, i, :], ACT.Square,
                                         accum_out=ss[0:r, i:i + 1]).then_inc(squared, 1)
                act.wait_ge(mean, 1)
                nc.scalar.activation(rs[:, :], ss[:, :], ACT.Sqrt).then_inc(root, 1)
                act.wait_ge(c_in, 64)
                for u, (k, which, tiles, c0, n) in enumerate(units):
                    if u == len(units) // 2:
                        round_slab(g, act, 0, KT * ahead[0].cols)
                    act.wait_ge(turned, u + 1)
                    dst = (g.h_hi, g.m_hi)[which][:, k, c0:c0 + n]
                    nc.scalar.activation(dst, g.ps[:, u % 8, 0:n], ACT.Copy,
                                         scale=g.gains[:, which, k:k + 1]).then_inc(hi_done, 1)

            @block.vector
            def _(dve):
                nc.vector.memset(ss[:], 1.0).then_inc(zeroed, 1)
                for t in (g.h_hi, g.h_lo):
                    nc.vector.memset(t[:, :, T_ALL:T_PAD].bitcast(F32), 0.0)
                dve.wait_ge(squared, NT)
                nc.vector.tensor_scalar(ss[:], ss[:], 1.0 / D_MODEL, EPS, ALU.mult, ALU.add).then_inc(mean, 1)
                dve.wait_ge(root, 1)
                nc.vector.reciprocal(rs[:], rs[:]).then_inc(mean, 1)
                dve.wait_ge(mean, 2)
                for i, src in enumerate(srcs):
                    r = src.shape[0]
                    nc.vector.tensor_scalar(xs[0:r, i, :], xs[0:r, i, :], rs[0:r, i:i + 1], None,
                                            ALU.mult).then_inc(scaled, 1)
                for u, (k, which, tiles, c0, n) in enumerate(units):
                    dve.wait_ge(hi_done, u + 1)
                    hi = (g.h_hi, g.m_hi)[which][:, k, c0:c0 + n]
                    lo = (g.h_lo, g.m_lo)[which][:, k, c0:c0 + n]
                    nc.vector.scalar_tensor_tensor(out=lo, in0=g.ps[:, u % 8, 0:n],
                                                   scalar=g.gains[:, which, k:k + 1], in1=hi.bitcast(F32),
                                                   op0=ALU.mult, op1=ALU.subtract).then_inc(lo_done, 1)

            @block.tensor
            def _(pe):
                pe.wait_ge(c_in, 64)
                pe.wait_ge(scaled, NT)
                for u, (k, which, tiles, c0, n) in enumerate(units):
                    if u >= 8:
                        pe.wait_ge(lo_done, u - 7)
                    for j, i in enumerate(tiles):
                        r = srcs[i].shape[0]
                        last = pe.transpose(g.ps[:, u % 8, j * P:j * P + r], xs[0:r, i, k * P:(k + 1) * P],
                                            g.ident[0:r, 0:r])
                    last.then_inc(turned, 1)



def token_units(dests):
    return [(i, rows(i), dests(i)) for i in range(N_TILE)]


def row_slice(i):
    return slice(i * P, i * P + rows(i))


def feature_units(d, f0):
    return [(ft, c0, n, d[f0 + ft * P:f0 + (ft + 1) * P, c0:c0 + n]) for ft in range(2) for c0, n in GROUPS]


def kv_dest(io, prompt, sample, i):
    return io[prompt][0, 0, i * P:(i + 1) * P] if i < TILE_P else io[sample][0, 0]


def plan_first(g):
    io, plan = g.io, []
    w = io["w_in"][0]
    for j in range(2):
        plan.append(SlabPlan("t", w_cols(w, OFF_IQ + j * 256, 256), 256,
                              token_units(lambda i: [(g.d_iq[row_slice(i), j * 256:(j + 1) * 256], 0, 256)]),
                              ACT.Copy, rope=(4, IDX_D, 8, OFF_ICOS, OFF_ISIN)))
    plan.append(SlabPlan("t", w_cols(w, OFF_IK, IDX_KW), IDX_KW,
                          token_units(lambda i: [(g.d_ik[row_slice(i), :], 0, IDX_KW),
                                                 (kv_dest(io, "new_idx_k_prompt", "new_idx_k_sample", i), 0, IDX_D)]),
                          ACT.Copy, rope=(1, IDX_D, 8, OFF_ICOS, OFF_ISIN)))
    for j in range(4):
        out = io["new_mem_k_prompt"] if j < 2 else io["new_mem_v_prompt"]
        out = out[0, 0].rearrange("n h d -> n (h d)")
        c0 = (j % 2) * 256
        units = [(i, P, [(out[i * P:(i + 1) * P, c0:c0 + 256], 0, 256)]) for i in range(N_MEM // P)]
        plan.append(SlabPlan("t", w_cols(io["w_mem_kv"][0], j * 256, 256), 256, units, ACT.Copy, mem=True))
    return plan


def plan_second(g):
    io, plan = g.io, []
    w = io["w_in"][0]
    rope = (2, HD, 16, OFF_COS, OFF_SIN)

    def flat(name_p, name_s, i):
        return kv_dest(io, name_p, name_s, i).rearrange("t h d -> t (h d)")

    plan.append(SlabPlan("t", w_cols(w, OFF_K, 256), 256,
                          token_units(lambda i: [(flat("new_k_prompt", "new_k_sample", i), 0, 256)]),
                          ACT.Copy, rope=rope))
    plan.append(SlabPlan("t", w_cols(w, OFF_V, 256), 256,
                          token_units(lambda i: [(flat("new_v_prompt", "new_v_sample", i), 0, 256)]), ACT.Copy))

    def to_rows(d, off, n, func, rope=None):
        for j in range(n):
            plan.append(SlabPlan("t", w_cols(w, off + j * 256, 256), 256,
                                  token_units(lambda i: [(d[row_slice(i), j * 256:(j + 1) * 256], 0, 256)]),
                                  func, rope=rope))

    def to_features(d, off, n, func):
        for j in range(n):
            plan.append(SlabPlan("f", w_cols(w, off + j * 256, 256), 256, feature_units(d, j * 256), func))

    to_rows(g.d_q, OFF_Q, 3, ACT.Copy, rope=rope)
    to_rows(g.d_bi, OFF_BI, 3, ACT.Copy)
    to_features(g.d_cq, OFF_CQ, 2, ACT.Copy)
    to_rows(g.d_bg, OFF_BG, 3, ACT.Silu)
    to_features(g.d_bq, OFF_BQ, 3, ACT.Silu)
    to_features(g.d_gate, OFF_G, 12, ACT.Sigmoid)
    for j in range(3):
        plan.append(SlabPlan("decay", w_cols(w, OFF_BF + j * 256, 256), 256,
                             [(ft, c0, n, 2 * j + ft) for ft in range(2) for c0, n in GROUPS], ACT.Sigmoid))
    return plan


def block_project(g, tag, plan, with_index, ahead):
    nc, io = g.nc, g.io
    n0 = g.slab
    g.slab += len(plan)
    NB, NS = 4, 8
    coming = plan + ahead
    order = []
    for s, sl in enumerate(plan):
        order += [(s, u) for u in sl.units]
    first = [sum(len(q.units) for q in plan[:s]) for s in range(len(plan) + 1)]
    roped = []
    for s, u in order:
        roped.append((roped[-1] if roped else 0) + (plan[s].rope is not None))
    n_out = []
    per = [0] * NS
    for n, (s, u) in enumerate(order):
        per[n % NS] += {"t": lambda: len(u[2]), "f": lambda: 1, "decay": lambda: 2}[plan[s].kind]()
        n_out.append(per[n % NS])
    with ExitStack() as ctx:
        stage = ctx.enter_context(nc.sbuf_tensor(f"{tag}_stage", [P, NS, 384], F32))
        cs = ctx.enter_context(nc.sbuf_tensor(f"{tag}_cs", [P, N_TILE, ROPE_W], F32))
        rt = ctx.enter_context(nc.sbuf_tensor(f"{tag}_rt", [P, 4, 32], F32))
        cs_in, full, staged = g.sem(f"{tag}_cs_in"), g.sem(f"{tag}_full"), g.sem(f"{tag}_staged")
        rope_part, rope_done = g.sem(f"{tag}_rope_part"), g.sem(f"{tag}_roped")
        stored = [g.sem(f"{tag}_stored{j}") for j in range(NS)]
        ix = index_setup(g, ctx) if with_index else None
        fg = forget_setup(g, ctx, ix) if with_index else None
        decays = [n for n, (s, u) in enumerate(order) if plan[s].kind == "decay"]

        with nc.Block() as block:
            @block.sync
            def _(sp):
                sp.dma_start(cs[:], io["c_rope"]).then_inc(cs_in, 16)
                if ix:
                    sp.dma_start(fg.lgt[:], io["hgrn_lb_logits"].rearrange("r (h p) -> p r h", p=P),
                                 allow_slow_non_contiguous=True).then_inc(fg.set_, 16)
                    index_loads(g, ix, sp)
                for s, sl in enumerate(plan):
                    for n in range(first[s], first[s + 1]):
                        u = order[n][1]
                        if sl.kind == "decay":
                            ft, c0, w, h = u
                            sp.wait_ge(fg.summed, n - decays[0] + 1)
                            for dst, src in ((g.d_kk, fg.kk), (g.d_cum, fg.cum)):
                                sp.dma_start(dst[h * P:(h + 1) * P, c0:c0 + w],
                                             src[:, n % NS, 0:w]).then_inc(stored[n % NS], 16)
                            continue
                        if sl.rope:
                            sp.wait_ge(rope_done, roped[n])
                        else:
                            sp.wait_ge(staged, n + 1)
                        if sl.kind == "t":
                            for dst, c0, c in u[2]:
                                sp.dma_start(dst, stage[0:u[1], n % NS, c0:c0 + c]).then_inc(stored[n % NS], 16)
                        else:
                            sp.dma_start(u[3], stage[:, n % NS, 0:u[2]]).then_inc(stored[n % NS], 16)
                    if s + 2 < len(coming):
                        load_slab(g, sp, n0 + s + 2, coming[s + 2].w, KT)
                for j in range(NS):
                    sp.wait_ge(stored[j], 16 * per[j])

            @block.gpsimd
            def _(pool):
                pool.wait_ge(cs_in, 16)
                parts = 0
                for s, sl in enumerate(plan):
                    if s + 1 < len(coming):
                        split_slab(g, pool, n0 + s + 1, KT * coming[s + 1].cols)
                    if not sl.rope:
                        continue
                    heads, width, half, co, so = sl.rope
                    for n in range(first[s], first[s + 1]):
                        i, r, _ = order[n][1]
                        x = stage[0:r, n % NS, 0:heads * width].rearrange("p (h d) -> p h d", h=heads)
                        x1, x2 = x[:, :, 0:half], x[:, :, half:2 * half]
                        cos = bcast_mid(cs[0:r, i, co:co + half], heads)
                        sin = bcast_mid(cs[0:r, i, so:so + half], heads)
                        t = [rt[0:r, j, 0:heads * half].rearrange("p (h d) -> p h d", h=heads) for j in range(4)]
                        pool.wait_ge(staged, n + 1)
                        if parts:
                            pool.wait_ge(rope_done, parts)
                        for j, (a, b) in enumerate(((x1, cos), (x2, sin), (x2, cos), (x1, sin))):
                            last = nc.gpsimd.tensor_tensor(t[j], a, b, ALU.mult)
                        parts += 1
                        last.then_inc(rope_part, 1)
                        pool.wait_ge(rope_part, parts)
                        nc.gpsimd.tensor_tensor(x1, t[0], t[1], ALU.subtract)
                        nc.gpsimd.tensor_tensor(x2, t[2], t[3], ALU.add).then_inc(rope_done, 1)

            @block.scalar
            def _(act):
                if ix:
                    act.wait_ge(fg.lb_step, 1)
                    nc.scalar.activation(fg.lgt[:], fg.lgt[:], ACT.Exp).then_inc(fg.lb_exp, 1)
                for s, sl in enumerate(plan):
                    for n in range(first[s], first[s + 1]):
                        u = order[n][1]
                        if n == first[s] + (1 if s else 0) and s + 1 < len(coming):
                            round_slab(g, act, n0 + s + 1, KT * coming[s + 1].cols)
                        act.wait_ge(full, n + 1)
                        if n >= NS:
                            act.wait_ge(stored[n % NS], 16 * n_out[n - NS])
                        r, c = (u[1], sl.cols) if sl.kind == "t" else (P, u[2])
                        nc.scalar.activation(stage[0:r, n % NS, 0:c], g.ps[0:r, n % NB, 0:c],
                                             sl.func).then_inc(staged, 1)
                    if sl.kind == "decay":
                        for n in range(first[s], first[s + 1]):
                            x = stage[:, n % NS, 0:order[n][1][2]]
                            act.wait_ge(fg.made, n - decays[0] + 1)
                            nc.scalar.activation(x, x, ACT.Ln).then_inc(fg.logged, 1)
                    if ix:
                        index_act(g, ix, act, s)

            @block.tensor
            def _(pe):
                for s, sl in enumerate(plan):
                    w = slab_view(g, n0 + s, KT, sl.cols)
                    x = (g.m_hi, g.m_lo) if sl.mem else (g.h_hi, g.h_lo)
                    pe.wait_ge(g.w_split, n0 + s + 1)
                    for n in range(first[s], first[s + 1]):
                        u = order[n][1]
                        if n >= NB:
                            pe.wait_ge(staged, n - NB + 1)
                        if sl.kind == "t":
                            c = slice(u[0] * P, (u[0] + 1) * P)
                            last = three_products(pe, g.ps[:, n % NB, 0:sl.cols],
                                                  lambda a, k: x[a][:, k, c], lambda b, k: w[b][:, k, :], KT)
                        else:
                            f, c = slice(u[0] * P, (u[0] + 1) * P), slice(u[1], u[1] + u[2])
                            last = three_products(pe, g.ps[:, n % NB, 0:u[2]],
                                                  lambda a, k: w[a][:, k, f], lambda b, k: x[b][:, k, c], KT)
                        last.then_inc(full, 1)
                    pe.drain().then_inc(g.w_used, 1)
                    if ix and s == 0:
                        index_turn(g, ix, pe)
                    if ix:
                        index_scores(g, ix, pe, s)

            if ix:
                @block.vector
                def _(dve):
                    forget_bounds(g, fg, dve)
                    index_select(g, ix, dve)
                    for s, sl in enumerate(plan):
                        if sl.kind != "decay":
                            continue
                        for n in range(first[s], first[s + 1]):
                            ft, c0, w, h = order[n][1]
                            x = stage[:, n % NS, 0:w]
                            dve.wait_ge(staged, n + 1)
                            nc.vector.tensor_scalar(x, x, fg.oml[:, h:h + 1], fg.lb[:, h:h + 1],
                                                    ALU.mult, ALU.add).then_inc(fg.f_made, 1)
                            dve.wait_ge(fg.f_made, n - decays[0] + 2)
                            nc.vector.tensor_scalar(fg.kk[:, n % NS, 0:w], x, -1.0, 1.0,
                                                    ALU.mult, ALU.add).then_inc(fg.made, 1)
                        for n in range(first[s], first[s + 1]):
                            w = order[n][1][2]
                            dve.wait_ge(fg.logged, n - decays[0] + 1)
                            for c in range(0, w, P):
                                e = min(c + P, w)
                                last = nc.vector.tensor_tensor_scan(fg.cum[:, n % NS, c:e], stage[:, n % NS, c:e],
                                                                    fg.zero[:, 0:e - c], 0.0, ALU.add, ALU.add)
                            last.then_inc(fg.summed, 1)



def forget_setup(g, ctx, ix):
    sb = lambda name, shape: ctx.enter_context(g.nc.sbuf_tensor("fg_" + name, shape, F32))
    fg = ForgetBuffers()
    fg.lgt, fg.lb, fg.oml = sb("lgt", [P, 2, B_HEADS]), sb("lb", [P, B_HEADS]), sb("oml", [P, B_HEADS])
    fg.lmx, fg.zero = sb("lmx", [P, B_HEADS]), sb("zero", [P, P])
    fg.kk = ix.work[:].rearrange("p a b -> p (a b)").rearrange("p (j c) -> p j c", c=384)
    fg.cum = ix.qT[:].rearrange("p a b -> p (a b)")[:, 0:8 * 384].rearrange("p (j c) -> p j c", c=384)
    fg.set_, fg.lb_step, fg.lb_exp = g.sem("fg_set"), g.sem("fg_lb_step"), g.sem("fg_lb_exp")
    fg.f_made, fg.made, fg.logged, fg.summed = (g.sem("fg_f_made"), g.sem("fg_made"), g.sem("fg_logged"),
                                                g.sem("fg_summed"))
    return fg


def forget_bounds(g, fg, dve):
    V = g.nc.vector
    dve.wait_ge(fg.set_, 16)
    V.memset(fg.zero[:], 0.0)
    V.tensor_tensor(fg.lmx[:], fg.lgt[:, 0, :], fg.lgt[:, 1, :], ALU.max).then_inc(fg.f_made, 1)
    dve.wait_ge(fg.f_made, 1)
    for r in range(2):
        last = V.tensor_tensor(fg.lgt[:, r, :], fg.lgt[:, r, :], fg.lmx[:], ALU.subtract)
    last.then_inc(fg.lb_step, 1)
    dve.wait_ge(fg.lb_exp, 1)
    V.tensor_tensor(fg.lmx[:], fg.lgt[:, 0, :], fg.lgt[:, 1, :], ALU.add).then_inc(fg.lb_step, 1)
    dve.wait_ge(fg.lb_step, 2)
    V.reciprocal(fg.lmx[:], fg.lmx[:]).then_inc(fg.lb_step, 1)
    dve.wait_ge(fg.lb_step, 3)
    V.tensor_tensor(fg.lb[:], fg.lgt[:, 0, :], fg.lmx[:], ALU.mult).then_inc(fg.lb_step, 1)
    dve.wait_ge(fg.lb_step, 4)
    V.tensor_scalar(fg.oml[:], fg.lb[:], -1.0, 1.0, ALU.mult, ALU.add).then_inc(fg.lb_step, 1)
    dve.wait_ge(fg.lb_step, 5)



SCORED = list(range(2, N_TILE))
SCORED_AFTER = {1: [2, 3], 2: [4, 5], 3: [6, 7], 4: [8]}
IX_BANKS = 4


def index_setup(g, ctx):
    nc = g.nc
    sb = lambda name, shape: ctx.enter_context(nc.sbuf_tensor(name, shape, F32))
    ix = IndexBuffers()
    ix.qT = sb("ix_qT", [P, IDX_W // P, T_ALL])
    ix.kT = sb("ix_kT", [P, SEQ + PAST + DEC])
    ix.w = sb("ix_w", [P, N_TILE, IDX_HEADS])
    ix.relu = sb("ix_relu", [P, 3, 512])
    ix.work = sb("ix_work", [P, 3, 1024])
    ix.m8 = sb("ix_m8", [P, 8])
    ix.cnt = sb("ix_cnt", [P, 1])
    ix.in_, ix.turned, ix.kept, ix.scored = g.sem("ix_in"), g.sem("ix_turned"), g.sem("ix_kept"), g.sem("ix_scored")
    ix.relued, ix.added, ix.step = g.sem("ix_relued"), g.sem("ix_added"), g.sem("ix_step")
    ix.q_rows = g.bias[:, 0:N_TILE * IDX_W].rearrange("p (i c) -> p i c", i=N_TILE)
    ix.k_rows = ix.work[:].rearrange("p a b -> p (a b)")[:, 0:(N_TILE + 1) * P].rearrange("p (i c) -> p i c", c=P)
    ix.k_tiles = [(j, P, j * P) for j in range(TILE_P)] + [(N_TILE, P, SEQ), (TILE_P, DEC, SEQ + PAST)]
    ix.units = [(i, h, c, min(512, n_keys(i) - c)) for i in SCORED
                for c in range(0, n_keys(i), 512) for h in range(IDX_HEADS)]
    ix.turns = [("q", i) for i in range(N_TILE)] + [("k", j) for j in range(len(ix.k_tiles))]
    ix.n_in = 0
    return ix


def index_loads(g, ix, sp):
    def load(dst, src):
        sp.dma_start(dst, src, allow_slow_non_contiguous=True).then_inc(ix.in_, 16)
        ix.n_in += 16
    for i in range(N_TILE):
        r = rows(i)
        load(ix.q_rows[0:r, i, :], g.d_iq[row_slice(i), :])
        load(ix.w[0:r, i, :], g.d_ik[row_slice(i), IDX_D:IDX_KW])
        for c in range(0, P, IDX_D):
            load(ix.k_rows[0:r, i, c:c + IDX_D], g.d_ik[row_slice(i), 0:IDX_D])
    for c in range(0, P, IDX_D):
        load(ix.k_rows[:, N_TILE, c:c + IDX_D], g.io["cache_idx_k"][0, 0])


def index_turn(g, ix, pe):
    pe.wait_ge(ix.in_, ix.n_in)
    for n, (kind, j) in enumerate(ix.turns):
        bank = g.ps[:, 4 + n % IX_BANKS, :]
        if n >= IX_BANKS:
            pe.wait_ge(ix.kept, n - IX_BANKS + 1)
        if kind == "q":
            r = rows(j)
            for f in range(IDX_W // P):
                last = pe.transpose(bank[:, f * P:f * P + r], ix.q_rows[0:r, j, f * P:(f + 1) * P],
                                    g.ident[0:r, 0:r])
        else:
            src, r, _ = ix.k_tiles[j]
            last = pe.transpose(bank[:, 0:r], ix.k_rows[0:r, src, :], g.ident[0:r, 0:r])
        last.then_inc(ix.turned, 1)


def index_scores(g, ix, pe, s):
    for n, (i, h, c, w) in enumerate(ix.units):
        if i not in SCORED_AFTER.get(s, []):
            continue
        if n == 0:
            pe.wait_ge(ix.kept, len(ix.turns))
        if n >= IX_BANKS:
            pe.wait_ge(ix.relued, n - IX_BANKS + 1)
        half = slice((h % 2) * IDX_D, (h % 2) * IDX_D + IDX_D)
        k0 = (0 if i < TILE_P else SEQ) + c
        pe.matmul(g.ps[0:rows(i), 4 + n % IX_BANKS, 0:w], ix.qT[half, h // 2, row_slice(i)],
                  ix.kT[half, k0:k0 + w], start=True, stop=True).then_inc(ix.scored, 1)


def index_act(g, ix, act, s):
    for n, (i, h, c, w) in enumerate(ix.units):
        if i not in SCORED_AFTER.get(s, []):
            continue
        act.wait_ge(ix.scored, n + 1)
        if n >= 3:
            act.wait_ge(ix.added, n - 2)
        g.nc.scalar.activation(ix.relu[0:rows(i), n % 3, 0:w], g.ps[0:rows(i), 4 + n % IX_BANKS, 0:w],
                               ACT.Relu, scale=IDX_SCALE).then_inc(ix.relued, 1)


def index_select(g, ix, dve):
    v = g.nc.vector
    for n, (kind, j) in enumerate(ix.turns):
        bank = g.ps[:, 4 + n % IX_BANKS, :]
        dve.wait_ge(ix.turned, n + 1)
        if kind == "q":
            r = rows(j)
            src = bank.rearrange("p (f t) -> p f t", t=P)[:, :, 0:r]
            v.tensor_copy(ix.qT[:, :, j * P:j * P + r], src).then_inc(ix.kept, 1)
        else:
            _, r, c0 = ix.k_tiles[j]
            v.tensor_copy(ix.kT[:, c0:c0 + r], bank[:, 0:r]).then_inc(ix.kept, 1)
    for n, (i, h, c, w) in enumerate(ix.units):
        r, sc = rows(i), g.bias[0:rows(i), BIAS_OFF[i] + c:BIAS_OFF[i] + c + w]
        dve.wait_ge(ix.relued, n + 1)
        relu, weight = ix.relu[0:r, n % 3, 0:w], ix.w[0:r, i, h:h + 1]
        if h == 0:
            v.tensor_scalar(sc, relu, weight, None, ALU.mult).then_inc(ix.added, 1)
        else:
            dve.wait_ge(ix.added, n)
            v.scalar_tensor_tensor(out=sc, in0=relu, scalar=weight, in1=sc,
                                   op0=ALU.mult, op1=ALU.add).then_inc(ix.added, 1)
    dve.wait_ge(ix.added, len(ix.units))

    steps = [0]

    def link(ins):
        steps[0] += 1
        ins.then_inc(ix.step, 1)
        dve.wait_ge(ix.step, steps[0])

    for i in range(N_TILE):
        n, r = n_keys(i), rows(i)
        sc = g.bias[0:r, BIAS_OFF[i]:BIAS_OFF[i + 1]]
        if i < 2:
            link(v.memset(sc, 0.0))
            link(v.memset(sc[0:64, n - 64:n], -MASKED))
            continue
        if i < TILE_P:
            link(v.memset(sc[0:64, n - 64:n], NEG))
        topk = TOPK_P if i < TILE_P else TOPK_S
        left, eq, cum = (ix.work[0:r, j, 0:n] for j in range(3))
        m8, cnt = ix.m8[0:r, :], ix.cnt[0:r, :]
        for it in range(topk // 8):
            link(v.max(m8, sc if it == 0 else left))
            if it < topk // 8 - 1:
                link(v.match_replace(left, m8, sc if it == 0 else left, NEG))
        bar = m8[:, 7:8]
        link(v.tensor_scalar(left, sc, bar, 0.0, ALU.is_gt, ALU.add, accum_out=cnt))
        link(v.tensor_scalar(cnt, cnt, -1.0, float(topk), ALU.mult, ALU.add))
        link(v.tensor_scalar(eq, sc, bar, None, ALU.is_equal))
        link(v.tensor_tensor_scan(cum, eq, eq, 0.0, ALU.add, ALU.max))
        link(v.scalar_tensor_tensor(out=eq, in0=cum, scalar=cnt, in1=eq, op0=ALU.is_le, op1=ALU.mult))
        link(v.tensor_tensor(left, left, eq, ALU.add))
        link(v.tensor_scalar(sc, left, -1.0, MASKED, ALU.add, ALU.mult))



N_HEAD = N_TILE * A_HEADS
N_SLOT = N_HEAD + 3
H3 = B_HEADS // 2
YB0, YC0 = A_W, A_W + B_W


def stages(i):
    return [h for h in LEVELS if 2 * h <= rows(i)] + ["q", "k"]


STEP0 = [sum(len(stages(j)) for j in range(i)) for i in range(N_TILE + 1)]


def v_tiles(i):
    if i < TILE_P:
        return [(j, P) for j in range(i + 1)]
    return [(TILE_P, P), (TILE_P + 1, DEC)]


def block_branches(g):
    nc, io = g.nc, g.io
    V, S, G = nc.vector, nc.scalar, nc.gpsimd
    with ExitStack() as ctx:
        sb = lambda name, shape, dt=F32: ctx.enter_context(nc.sbuf_tensor("br_" + name, shape, dt))
        kT = sb("kT", [P, A_KV, SEQ + PAST + DEC])
        val = sb("val", [P, N_TILE + 1, KV_W])
        mkT = sb("mkT", [P, 2, C_HEADS, N_MEM])
        mval = sb("mval", [P, 2, N_MEM // P, C_W])
        pT = sb("pT", [P, TILE_P, A_HEADS, P])
        nat = pT[:].rearrange("p a b c -> p (a b c)")
        k_nat = nat[:, 0:(N_TILE + 1) * KV_W].rearrange("p (j c) -> p j c", c=KV_W)
        m_nat = nat[:, (N_TILE + 1) * KV_W:(N_TILE + 1) * KV_W + 4 * C_W].rearrange("p (m j c) -> p m j c", m=2, j=2)
        q_nat, qT = sb("q_nat", [P, 2, A_W]), sb("qT", [P, 2, A_HEADS, P])
        prob = sb("prob", [P, 3, 1024])
        top, ntop, den = sb("top", [P, 8]), sb("ntop", [P, 8]), sb("den", [P, 8])
        part = sb("part", [P, 1])
        cq = sb("cq", [P, 2, C_HEADS, P])
        cp, cpT = sb("cp", [P, C_HEADS, N_MEM]), sb("cpT", [P, C_HEADS, 2, P])
        ctop, cden = sb("ctop", [P, C_HEADS]), sb("cden", [P, C_HEADS])
        ysb = sb("ysb", [P, 3, 512])
        cum, bq = sb("cum", [P, 2, B_W]), sb("bq", [P, 2, B_W])
        bv, bg = sb("bv", [P, 2, B_W]), sb("bg", [P, 2, B_W])
        kk = sb("kk", [P, 2, B_W])
        dif, ex, wk = sb("dif", [P, 2, B_W]), sb("ex", [P, 2, B_W]), sb("wk", [P, 2, B_W])
        exn, kp = sb("exn", [P, B_W]), sb("kp", [P, B_W])
        smat, kdT = sb("smat", [P, B_HEADS, P]), sb("kdT", [P, B_W])
        osb, sq = sb("osb", [P, B_W]), sb("sq", [P, B_W])
        ybT = sb("ybT", [P, B_HEADS, P])
        ms, expo = sb("ms", [P, B_HEADS]), sb("expo", [P, B_HEADS])
        eb = sb("eb", [P, B_HEADS])
        state = [sb("stateP", [P, B_HEADS, HD]), sb("stateS", [P, B_HEADS, HD])]
        masks, grow = sb("masks", [P, len(LEVELS), P], I32), sb("grow", [P, B_W])

        sem = lambda name: g.sem("br_" + name)
        k_set, mk_set, s_set, s_step = sem("k_set"), sem("mk_set"), sem("set"), sem("step")
        s_in = [sem("in0"), sem("in1")]
        t_done, t_kept = sem("t_done"), sem("t_kept")
        s_done, s_masked, ntop_ok, e_done, p_done, p_turned = (sem("s_done"), sem("s_masked"), sem("ntop"),
                                                               sem("exp"), sem("p_done"), sem("p_turned"))
        c_done, c_top, c_exp, c_norm, c_turned = sem("c_done"), sem("c_top"), sem("c_exp"), sem("c_norm"), sem("c_turned")
        o_done, o_kept = sem("o_done"), sem("o_kept")
        y_out = [sem(f"y_out{j}") for j in range(3)]
        yb_out, st_out = sem("yb_out"), sem("st_out")
        d_done, x_done, w_done = sem("d_done"), sem("x_done"), sem("w_done")
        hp_done, hp_free, s_cleared = sem("hp_done"), sem("hp_free"), sem("s_cleared")
        sq_done, ms_done, rs_done, y_part, y_done, gg_done = (sem("sq"), sem("ms"), sem("rs"), sem("y_part"),
                                                              sem("y_done"), sem("gg"))

        k_rows = [(j, P, j * P) for j in range(TILE_P)] + [(TILE_P, P, SEQ), (TILE_P + 1, DEC, SEQ + PAST)]
        N_SET = 16 * (1 + 3 + 2 + 2)

        def due(i, s):
            return [pos for pos in (2 * s, 2 * s + 1) if s >= 0 and i < N_TILE and pos < len(stages(i))]

        qturned, prob_turned, mem_turned, tc = {0: len(k_rows) + 4 + 2}, {}, {}, len(k_rows) + 4 + 2
        hu_idx, hu_st, hu_y, hc = {}, {}, {}, 0
        for n in range(N_SLOT):
            i, slot = divmod(n, A_HEADS)
            if 2 <= n < N_HEAD + 2:
                tc += -(-len(v_tiles((n - 2) // A_HEADS)) // 4)
                prob_turned[n - 2] = tc
            if slot == 4 and i + 1 < N_TILE:
                tc += 2
                qturned[i + 1] = tc
            if slot == 3 and i < N_TILE:
                tc += 2
                mem_turned[i] = tc
            if slot == 0 and i >= 1:
                hc += 2
                hu_st[i - 1] = hc
            for pos in due(i, slot - 1):
                hc += 2
                hu_idx[STEP0[i] + pos] = hc
            if slot == 2 and i >= 1:
                hc += 2
                hu_y[i - 1] = hc

        N_IN = 16 * 7

        def dcount(i, pos):
            st = stages(i)
            return STEP0[i] - i + pos + 1 - (1 if pos >= st.index("q") else 0)

        with nc.Block() as block:
            @block.sync
            def _(sp):
                def setup(dst, src, s=s_set):
                    sp.dma_start(dst, src, allow_slow_non_contiguous=True).then_inc(s, 16)

                kp_, vp_ = (io[n][0, 0].rearrange("(j p) h d -> p j (h d)", p=P)
                            for n in ("new_k_prompt", "new_v_prompt"))
                setup(k_nat[:, 0:TILE_P, :], kp_, k_set)
                setup(k_nat[:, TILE_P, :], io["cache_k"][0, 0].rearrange("t h d -> t (h d)"), k_set)
                setup(k_nat[0:DEC, TILE_P + 1, :], io["new_k_sample"][0, 0].rearrange("t h d -> t (h d)"), k_set)

                def setup_rest():
                    mems = ("new_mem_k_prompt", "new_mem_v_prompt"), ("cache_mem_k", "cache_mem_v")
                    of_mem = lambda name: io[name][0, 0].rearrange("(j p) h d -> p j (h d)", p=P)
                    for m in range(2):
                        setup(m_nat[:, m, :, :], of_mem(mems[m][0]), mk_set)
                    setup(masks[:], io["c_masks"])
                    setup(val[:, 0:TILE_P, :], vp_)
                    setup(val[:, TILE_P, :], io["cache_v"][0, 0].rearrange("t h d -> t (h d)"))
                    setup(val[0:DEC, TILE_P + 1, :], io["new_v_sample"][0, 0].rearrange("t h d -> t (h d)"))
                    for m in range(2):
                        setup(mval[:, m, :, :], of_mem(mems[m][1]))
                    setup(grow[:], io["hgrn_norm_gain"][0].rearrange("h d -> (h d)").partition_broadcast(P))
                    setup(state[1][:], io["state_hgrn"][0, 0].rearrange("h d v -> d h v"))

                def loads(i):
                    r, c, j = rows(i), row_slice(i), i % 2
                    w = B_HEADS * r
                    heads = lambda t: t[:, j, 0:w].rearrange("p (h t) -> p h t", h=B_HEADS)
                    feat = lambda d: d[:, c].rearrange("(h p) t -> p h t", p=P)
                    for dst, src in ((q_nat[0:r, j, :], g.d_q[c, :]), (cq[:, j, :, 0:r], feat(g.d_cq)),
                                     (heads(cum), feat(g.d_cum)), (heads(kk), feat(g.d_kk)), (heads(bq), feat(g.d_bq)),
                                     (bv[0:r, j, :], g.d_bi[c, :]), (bg[0:r, j, :], g.d_bg[c, :])):
                        sp.dma_start(dst, src).then_inc(s_in[j], 16)

                def store_y(n, i, row0, heads):
                    r = rows(i)
                    sp.wait_ge(o_kept, n + 1)
                    src = ysb[:, n % 3, 0:heads * r].rearrange("p (h t) -> p h t", h=heads)
                    dst = g.d_y[row0:row0 + heads * HD, row_slice(i)].rearrange("(h p) t -> p h t", p=P)
                    sp.dma_start(dst, src).then_inc(y_out[n % 3], 16)

                loads(0)
                setup_rest()
                loads(1)
                for i in range(N_TILE):
                    r = rows(i)
                    store_y(3 * i, i, YC0, C_HEADS)
                    store_y(3 * i + 1, i, 0, GROUP)
                    store_y(3 * i + 2, i, GROUP * HD, GROUP)
                    sp.wait_ge(hp_free, hu_y[i])
                    sp.dma_start(g.d_y[YB0:YC0, row_slice(i)].rearrange("(h p) t -> p h t", p=P),
                                 ybT[:, :, 0:r]).then_inc(yb_out, 16)
                    if i + 2 < N_TILE:
                        loads(i + 2)
                for j, (name, i) in enumerate((("new_hgrn_prompt", TILE_P - 1), ("new_hgrn_sample", N_TILE - 1))):
                    sp.wait_ge(hp_free, hu_st[i])
                    sp.dma_start(io[name][0, 0].rearrange("h d v -> d h v"), state[j][:]).then_inc(st_out, 16)
                for j in range(3):
                    sp.wait_ge(y_out[j], 16 * N_TILE)
                sp.wait_ge(yb_out, 16 * N_TILE)
                sp.wait_ge(st_out, 32)

            @block.tensor
            def _(pe):
                tu, su, hu, ou = [0], [0], [0], [0]

                def turn(parts):
                    n = tu[0]
                    if n >= 2:
                        pe.wait_ge(t_kept, n - 1)
                    for c, x in parts:
                        kb, m = x.shape
                        last = pe.transpose(g.ps[0:m, 2 + n % 2, c:c + kb], x, g.ident[0:kb, 0:kb])
                    last.then_inc(t_done, 1)
                    tu[0] += 1
                    return last

                def half_unit(make):
                    n = hu[0]
                    if n >= 2:
                        pe.wait_ge(hp_free, n - 1)
                    for h in range(H3):
                        last = make(g.ps[:, 5 + n % 2, h * P:(h + 1) * P], (n % 2) * H3 + h)
                    last.then_inc(hp_done, 1)
                    hu[0] += 1
                    return last

                def q_turn(i):
                    r = rows(i)
                    pe.wait_ge(s_in[i % 2], N_IN * (i // 2 + 1))
                    for h0, h1 in ((0, 4), (4, A_HEADS)):
                        turn([((h - h0) * P, q_nat[0:r, i % 2, h * HD:(h + 1) * HD]) for h in range(h0, h1)])

                def scores(n):
                    i, h = divmod(n, A_HEADS)
                    r, k0 = rows(i), 0 if i < TILE_P else SEQ
                    if h == 0:
                        pe.wait_ge(t_kept, qturned[i])
                    for c in range(0, n_keys(i), 512):
                        w = min(512, n_keys(i) - c)
                        if su[0] >= 2:
                            pe.wait_ge(s_masked, su[0] - 1)
                        pe.matmul(g.ps[0:r, su[0] % 2, 0:w], qT[:, i % 2, h, 0:r],
                                  kT[:, h // GROUP, k0 + c:k0 + c + w], start=True, stop=True).then_inc(s_done, 1)
                        su[0] += 1

                def prob_turn(n):
                    i, h = divmod(n, A_HEADS)
                    r, vt = rows(i), v_tiles(i)
                    pe.wait_ge(p_done, n + 1)
                    for b0 in range(0, len(vt), 4):
                        turn([((b - b0) * P, prob[0:r, n % 3, b * P:b * P + vt[b][1]])
                              for b in range(b0, min(b0 + 4, len(vt)))])

                def prob_out(n):
                    i, h = divmod(n, A_HEADS)
                    r, vt = rows(i), v_tiles(i)
                    if h % GROUP == GROUP - 1:
                        kv = h // GROUP
                        pe.wait_ge(t_kept, prob_turned[n])
                        out = g.ps[:, 4, 0:GROUP * r]
                        if ou[0] >= 1:
                            pe.wait_ge(o_kept, ou[0])
                        for b, (vj, kb) in enumerate(vt):
                            last = pe.matmul(out, val[0:kb, vj, kv * HD:(kv + 1) * HD],
                                             pT[0:kb, b, kv * GROUP:(kv + 1) * GROUP, 0:r],
                                             start=(b == 0), stop=(b == len(vt) - 1))
                        last.then_inc(o_done, 1)
                        ou[0] += 1

                def mem_scores(i):
                    r, m = rows(i), 0 if i < TILE_P else 1
                    pe.wait_ge(s_in[i % 2], N_IN * (i // 2 + 1))
                    for pair in range(2):
                        if 2 * i + pair >= 1:
                            pe.wait_ge(c_exp, 2 * i + pair)
                        for e in range(2):
                            last = pe.matmul(g.ps[0:r, 7, e * N_MEM:(e + 1) * N_MEM], cq[:, i % 2, 2 * pair + e, 0:r],
                                             mkT[:, m, 2 * pair + e, :], start=True, stop=True)
                        last.then_inc(c_done, 1)

                def mem_turn(i):
                    r = rows(i)
                    pe.wait_ge(c_norm, i + 1)
                    for pair in range(2):
                        turn([((2 * e + b) * P, cp[0:r, 2 * pair + e, b * P:(b + 1) * P])
                              for e in range(2) for b in range(2)])

                def mem_out(i):
                    r, m = rows(i), 0 if i < TILE_P else 1
                    pe.wait_ge(t_kept, mem_turned[i])
                    if ou[0] >= 1:
                        pe.wait_ge(o_kept, ou[0])
                    for h in range(C_HEADS):
                        for b in range(2):
                            last = pe.matmul(g.ps[:, 4, h * r:(h + 1) * r], mval[:, m, b, h * HD:(h + 1) * HD],
                                             cpT[:, h, b, 0:r], start=(b == 0), stop=(b == 1))
                    last.then_inc(o_done, 1)
                    ou[0] += 1

                def recur_step(i, pos):
                    t, idx, kind = rows(i), STEP0[i] + pos, stages(i)[pos]
                    st, par = state[i // TILE_P], (STEP0[i] + pos) % 2
                    w = lambda h: wk[:, par, h * t:(h + 1) * t]
                    pe.wait_ge(w_done, idx + 1)
                    if kind == "q":
                        pe.wait_ge(hp_free, hu[0])
                        pe.wait_ge(s_cleared, 1)
                        def make(out, h):
                            last = pe.matmul(out[0:t], smat[0:t, h, 0:t], bv[0:t, i % 2, h * HD:(h + 1) * HD],
                                             start=True, stop=(i == 0))
                            if i:
                                last = pe.matmul(out[0:t], w(h), st[:, h, :], start=False, stop=True)
                            return last
                    elif kind == "k":
                        make = lambda out, h: pe.transpose(out[0:t], w(h), g.ident[:])
                    elif kind == 1:
                        make = lambda out, h: pe.matmul(out[0:t, 0:t], kp[:, h * t:(h + 1) * t], w(h), start=True, stop=True)
                    else:
                        make = lambda out, h: pe.matmul(out[0:t, 0:t], w(h), w(h), start=True, stop=True)
                    half_unit(make)
                    half_unit(make)

                def recur_state(i):
                    t = rows(i)
                    pe.wait_ge(hp_free, hu[0])
                    make = lambda out, h: pe.matmul(out, kdT[0:t, h * HD:(h + 1) * HD],
                                                    bv[0:t, i % 2, h * HD:(h + 1) * HD], start=True, stop=True)
                    half_unit(make)
                    half_unit(make)

                def recur_out(i):
                    t = rows(i)
                    pe.wait_ge(y_done, i + 1)
                    make = lambda out, h: pe.transpose(out[:, 0:t], osb[0:t, h * HD:(h + 1) * HD], g.ident[0:t, 0:t])
                    half_unit(make)
                    half_unit(make)

                pe.wait_ge(k_set, 16 * 3)
                for j, kb, _ in k_rows:
                    turn([(kv * P, k_nat[0:kb, j, kv * HD:(kv + 1) * HD]) for kv in range(A_KV)])
                q_turn(0)
                pe.wait_ge(mk_set, 16 * 2)
                for m in range(2):
                    for j in range(N_MEM // P):
                        turn([(h * P, m_nat[:, m, j, h * HD:(h + 1) * HD]) for h in range(C_HEADS)])
                for n in range(N_SLOT):
                    i, slot = divmod(n, A_HEADS)
                    if n < N_HEAD:
                        scores(n)
                    if slot == 0 and i >= 1:
                        recur_state(i - 1)
                    steps = due(i, slot - 1)
                    for pos in steps[:1]:
                        recur_step(i, pos)
                    if n == 3:
                        pe.wait_ge(s_set, N_SET)
                    if slot == 1 and i < N_TILE:
                        mem_scores(i)
                    if n >= 3:
                        prob_out(n - 3)
                    if slot == 4:
                        mem_out(i)
                    if 2 <= n < N_HEAD + 2:
                        prob_turn(n - 2)
                    if slot == 4 and i + 1 < N_TILE:
                        q_turn(i + 1)
                    if slot == 3:
                        mem_turn(i)
                    for pos in steps[1:]:
                        recur_step(i, pos)
                    if slot == 2 and i >= 1:
                        recur_out(i - 1)

            @block.scalar
            def _(act):
                tu = [0]

                def keep(copies):
                    act.wait_ge(t_done, tu[0] + 1)
                    for dst, src in copies(g.ps[:, 2 + tu[0] % 2, :]):
                        last = S.activation(dst, src, ACT.Copy)
                    last.then_inc(t_kept, 1)
                    tu[0] += 1

                def q_keep(i):
                    r = rows(i)
                    for h0, h1 in ((0, 4), (4, A_HEADS)):
                        keep(lambda b: [(qT[:, i % 2, h0:h1, 0:r],
                                         b.rearrange("p (h t) -> p h t", t=P)[:, 0:h1 - h0, 0:r])])

                def prob_keep(n):
                    i, h = divmod(n, A_HEADS)
                    r, vt, kv = rows(i), v_tiles(i), h // GROUP
                    if i >= 1:
                        act.wait_ge(o_done, 3 * (i - 1) + 2 + kv)
                    for b0 in range(0, len(vt), 4):
                        bl = range(b0, min(b0 + 4, len(vt)))
                        if all(vt[b][1] == P for b in bl):
                            keep(lambda bank: [(pT[:, b0:b0 + len(bl), h, 0:r],
                                                bank.rearrange("p (b t) -> p b t", t=P)[:, 0:len(bl), 0:r])])
                        else:
                            keep(lambda bank: [(pT[0:vt[b][1], b, h, 0:r],
                                                bank[0:vt[b][1], (b - b0) * P:(b - b0) * P + r]) for b in bl])

                def recur_exp(i, pos):
                    t, idx, kind = rows(i), STEP0[i] + pos, stages(i)[pos]
                    w = B_HEADS * t
                    if kind != "q":
                        act.wait_ge(d_done, dcount(i, pos))
                    if idx >= 2:
                        act.wait_ge(w_done, idx - 1)
                    dst = ex[:, idx % 2, 0:w]
                    if kind == "q":
                        b = cum[:, i % 2, 0:w]
                        c3 = b.rearrange("p (h t) -> p h t", h=B_HEADS)
                        if i >= 1:
                            act.wait_ge(hp_free, hu_st[i - 1])
                        S.activation(eb[:, :], c3[:, :, t - 1], ACT.Exp)
                        S.activation(dst, b, ACT.Exp).then_inc(x_done, 1)
                    elif kind == 1:
                        S.activation(exn[:, 0:w], dif[:, idx % 2, 0:w], ACT.Exp, scale=-1.0)
                        S.activation(dst, dif[:, idx % 2, 0:w], ACT.Exp).then_inc(x_done, 1)
                    else:
                        S.activation(dst, dif[:, idx % 2, 0:w], ACT.Exp).then_inc(x_done, 1)

                for j, kb, c0 in k_rows:
                    keep(lambda b: [(kT[:, :, c0:c0 + kb], b.rearrange("p (h t) -> p h t", t=P)[:, 0:A_KV, 0:kb])])
                q_keep(0)
                for m in range(2):
                    for j in range(N_MEM // P):
                        keep(lambda b: [(mkT[:, m, :, j * P:(j + 1) * P], b.rearrange("p (h t) -> p h t", t=P))])
                for n in range(N_SLOT):
                    i, slot = divmod(n, A_HEADS)
                    if n < N_HEAD:
                        r, w = rows(i), n_keys(i)
                        act.wait_ge(ntop_ok, n + 1)
                        if n >= 8:
                            act.wait_ge(p_done, n - 7)
                        S.activation(prob[0:r, n % 3, 0:w], prob[0:r, n % 3, 0:w], ACT.Exp, bias=ntop[0:r, n % 8:n % 8 + 1],
                                     scale=1.0, accum_out=den[0:r, n % 8:n % 8 + 1]).then_inc(e_done, 1)
                    if slot == 0 and i >= 1:
                        t = rows(i - 1)
                        act.wait_ge(hp_free, hu_idx[STEP0[i - 1] + stages(i - 1).index("q")])
                        if i >= 2:
                            act.wait_ge(ms_done, i - 1)
                        S.activation(sq[0:t, :], osb[0:t, :], ACT.Square, scale=float(HD) ** -0.5).then_inc(sq_done, 1)
                    if slot == 1 and i < N_TILE:
                        r = rows(i)
                        for pair in range(2):
                            act.wait_ge(c_top, 2 * i + pair + 1)
                            for h in (2 * pair, 2 * pair + 1):
                                last = S.activation(cp[0:r, h, :], g.ps[0:r, 7, (h % 2) * N_MEM:(h % 2 + 1) * N_MEM],
                                                    ACT.Exp, bias=ctop[0:r, h:h + 1], scale=SCALE,
                                                    accum_out=cden[0:r, h:h + 1])
                            last.then_inc(c_exp, 1)
                    for pos in due(i, slot):
                        recur_exp(i, pos)
                    if 2 <= n < N_HEAD + 2:
                        prob_keep(n - 2)
                    if slot == 4 and i + 1 < N_TILE:
                        q_keep(i + 1)
                    if slot == 3:
                        r = rows(i)
                        if i >= 1:
                            act.wait_ge(o_done, 3 * (i - 1) + 1)
                        for pair in range(2):
                            keep(lambda b: [(cpT[:, 2 * pair:2 * pair + 2, :, 0:r],
                                             b.rearrange("p (h b t) -> p h b t", h=2, b=2)[:, :, :, 0:r])])

            @block.gpsimd
            def _(pool):
                G.memset(expo[:], -0.5)
                G.memset(smat[:], 0.0).then_inc(s_cleared, 1)
                for n in range(N_SLOT):
                    i, slot = divmod(n, A_HEADS)
                    j = i % 2
                    if slot == 0 and i < N_TILE:
                        pool.wait_ge(s_in[j], N_IN * (i // 2 + 1))
                    for pos in due(i, slot):
                        w = B_HEADS * rows(i)
                        idx, kind = STEP0[i] + pos, stages(i)[pos]
                        e, o = ex[:, idx % 2, 0:w], wk[:, idx % 2, 0:w]
                        q, k_ = bq[:, j, 0:w], kk[:, j, 0:w]
                        pool.wait_ge(x_done, idx + 1)
                        if idx >= 2:
                            pool.wait_ge(hp_done, hu_idx[idx - 2])
                        if kind == 1:
                            G.tensor_tensor(kp[:, 0:w], k_, exn[:, 0:w], ALU.mult)
                            G.tensor_tensor(o, q, e, ALU.mult).then_inc(w_done, 1)
                        elif kind == "q":
                            G.tensor_tensor(o, q, e, ALU.mult).then_inc(w_done, 1)
                        elif kind == "k":
                            G.tensor_tensor(o, k_, e, ALU.mult).then_inc(w_done, 1)
                        else:
                            blk = lambda x: x.rearrange("p (b t) -> p b t", t=2 * kind)
                            G.tensor_tensor(blk(o)[:, :, 0:kind], blk(k_)[:, :, 0:kind],
                                            blk(e)[:, :, 0:kind], ALU.mult)
                            G.tensor_tensor(blk(o)[:, :, kind:], blk(q)[:, :, kind:],
                                            blk(e)[:, :, kind:], ALU.mult).then_inc(w_done, 1)
                    if slot == 4 and i < N_TILE:
                        t = rows(i)
                        if i == 0:
                            pool.wait_ge(s_set, N_SET)
                        G.tensor_tensor(bg[0:t, j, :], bg[0:t, j, :], grow[0:t, :], ALU.mult).then_inc(gg_done, 1)
                    if slot == 0 and i >= 1:
                        t = rows(i - 1)
                        pool.wait_ge(ms_done, i)
                        G.tensor_scalar(ms[0:t, :], ms[0:t, :], EPS, None, ALU.add).then_inc(rs_done, 1)
                        pool.wait_ge(rs_done, 2 * i - 1)
                        G.tensor_tensor(ms[0:t, :], ms[0:t, :], expo[0:t, :], ALU.pow).then_inc(rs_done, 1)
                        pool.wait_ge(rs_done, 2 * i)
                        pool.wait_ge(gg_done, i)
                        o3 = osb[0:t, :].rearrange("p (h d) -> p h d", h=B_HEADS)
                        G.tensor_tensor(o3, o3, bcast(ms[0:t, :], HD), ALU.mult).then_inc(y_part, 1)
                        pool.wait_ge(y_part, i)
                        G.tensor_tensor(osb[0:t, :], osb[0:t, :], bg[0:t, (i - 1) % 2, :], ALU.mult).then_inc(y_done, 1)

            @block.vector
            def _(dve):
                su, hu, ou = [0], [0], [0]
                steps = [0]

                def link(ins):
                    steps[0] += 1
                    ins.then_inc(s_step, 1)
                    dve.wait_ge(s_step, steps[0])

                def half_unit():
                    n = hu[0]
                    dve.wait_ge(hp_done, n + 1)
                    hu[0] += 1
                    return g.ps[:, 5 + n % 2, 0:H3 * P].rearrange("p (h t) -> p h t", h=H3), (n % 2) * H3

                def mask_scores(n):
                    i, h = divmod(n, A_HEADS)
                    r, w = rows(i), n_keys(i)
                    if n >= 3:
                        dve.wait_ge(t_done, prob_turned[n - 3])
                    if n >= 8:
                        dve.wait_ge(e_done, n - 7)
                    tp = top[0:r, n % 8:n % 8 + 1]
                    for c in range(0, w, 512):
                        cw = min(512, w - c)
                        dve.wait_ge(s_done, su[0] + 1)
                        acc = part[0:r, :] if c + cw < w else tp
                        ins = V.tensor_tensor_reduce(prob[0:r, n % 3, c:c + cw], g.ps[0:r, su[0] % 2, 0:cw],
                                                     g.bias[0:r, BIAS_OFF[i] + c:BIAS_OFF[i] + c + cw], SCALE,
                                                     NEG if c == 0 else part[0:r, :], ALU.add, ALU.max, acc)
                        ins.then_inc(s_masked, 1)
                        su[0] += 1
                        dve.wait_ge(s_masked, su[0])
                    V.tensor_scalar(ntop[0:r, n % 8:n % 8 + 1], tp, -1.0, None, ALU.mult).then_inc(ntop_ok, 1)

                def normalise(n):
                    i = n // A_HEADS
                    r, w, d = rows(i), n_keys(i), den[0:rows(i), n % 8:n % 8 + 1]
                    dve.wait_ge(e_done, n + 1)
                    link(V.reciprocal(d, d))
                    V.tensor_scalar(prob[0:r, n % 3, 0:w], prob[0:r, n % 3, 0:w], d, None, ALU.mult).then_inc(p_done, 1)

                def keep_out(w):
                    n = ou[0]
                    dve.wait_ge(o_done, n + 1)
                    if n >= 3:
                        dve.wait_ge(y_out[n % 3], 16 * (n // 3))
                    V.tensor_copy(ysb[:, n % 3, 0:w], g.ps[:, 4, 0:w]).then_inc(o_kept, 1)
                    ou[0] += 1

                def recur_diff(i, pos):
                    t, idx, kind = rows(i), STEP0[i] + pos, stages(i)[pos]
                    w = B_HEADS * t
                    if kind == "q":
                        return
                    if idx >= 2:
                        dve.wait_ge(x_done, idx - 1)
                    b, d = cum[:, i % 2, 0:w], dif[:, idx % 2, 0:w]
                    if kind == "k":
                        b3, d3 = (x.rearrange("p (h t) -> p h t", h=B_HEADS) for x in (b, d))
                        V.tensor_tensor(d3, b3[:, :, t - 1:t].to_broadcast([P, B_HEADS, t]), b3,
                                        ALU.subtract).then_inc(d_done, 1)
                        return
                    b3, d3 = (x.rearrange("p (b t) -> p b t", t=2 * kind) for x in (b, d))
                    nb = w // (2 * kind)
                    ref = b3[:, :, kind - 1:kind]
                    if kind == 1:
                        V.tensor_tensor(d3, b3, ref.to_broadcast([P, nb, 2]), ALU.subtract).then_inc(d_done, 1)
                    else:
                        ref = ref.to_broadcast([P, nb, kind])
                        V.tensor_tensor(d3[:, :, 0:kind], ref, b3[:, :, 0:kind], ALU.subtract)
                        V.tensor_tensor(d3[:, :, kind:], b3[:, :, kind:], ref, ALU.subtract).then_inc(d_done, 1)

                def recur_keep(i, pos):
                    t, kind = rows(i), stages(i)[pos]
                    if pos == 0:
                        dve.wait_ge(s_cleared, 1)
                        dve.wait_ge(s_set, N_SET)
                    if kind == "q" and i >= 1:
                        dve.wait_ge(y_done, i)
                        dve.wait_ge(hp_free, hu[0])
                    for _ in range(2):
                        bank, h0 = half_unit()
                        if kind == "q":
                            dst = osb[0:t, h0 * HD:(h0 + H3) * HD].rearrange("p (h d) -> p h d", h=H3)
                            last = V.tensor_copy(dst, bank[0:t])
                        elif kind == "k":
                            dst = kdT[0:t, h0 * HD:(h0 + H3) * HD].rearrange("p (h d) -> p h d", h=H3)
                            last = V.tensor_copy(dst, bank[0:t])
                        else:
                            m = bcast_mid(masks[0:t, LEVELS.index(kind), 0:t], H3)
                            last = V.copy_predicated(smat[0:t, h0:h0 + H3, 0:t], m, bank[0:t, :, 0:t])
                        last.then_inc(hp_free, 1)

                for n in range(N_SLOT):
                    i, slot = divmod(n, A_HEADS)
                    if n < N_HEAD:
                        mask_scores(n)
                    if slot == 0 and i >= 1:
                        st = state[(i - 1) // TILE_P]
                        for _ in range(2):
                            bank, h0 = half_unit()
                            for h in range(H3):
                                if i == 1:
                                    last = V.tensor_copy(st[:, h0 + h, :], bank[:, h, :])
                                else:
                                    last = V.scalar_tensor_tensor(
                                        out=st[:, h0 + h, :], in0=st[:, h0 + h, :], scalar=eb[:, h0 + h:h0 + h + 1],
                                        in1=bank[:, h, :], op0=ALU.mult, op1=ALU.add)
                            last.then_inc(hp_free, 1)
                    steps_now = due(i, slot - 1)
                    for pos in steps_now[:1]:
                        recur_keep(i, pos)
                    if slot == 1 and i < N_TILE:
                        r = rows(i)
                        for pair in range(2):
                            dve.wait_ge(c_done, 2 * i + pair + 1)
                            hs = slice(2 * pair, 2 * pair + 2)
                            link(V.tensor_reduce(ctop[0:r, hs], g.ps[0:r, 7, :].rearrange("p (h m) -> p h m", h=2),
                                                 AX.X, ALU.max))
                            V.tensor_scalar(ctop[0:r, hs], ctop[0:r, hs], -SCALE, None, ALU.mult).then_inc(c_top, 1)
                    if slot == 0 and i < N_TILE:
                        dve.wait_ge(s_in[i % 2], N_IN * (i // 2 + 1))
                    for pos in due(i, slot):
                        recur_diff(i, pos)
                    if 1 <= n <= N_HEAD:
                        normalise(n - 1)
                    if slot == 2 and i < N_TILE:
                        r = rows(i)
                        dve.wait_ge(c_exp, 2 * i + 2)
                        link(V.reciprocal(cden[0:r, :], cden[0:r, :]))
                        V.tensor_tensor(cp[0:r], cp[0:r], bcast(cden[0:r, :], N_MEM), ALU.mult).then_inc(c_norm, 1)
                    if n >= 3 and (n - 3) % GROUP == GROUP - 1:
                        keep_out(GROUP * rows((n - 3) // A_HEADS))
                    if slot == 4:
                        keep_out(C_HEADS * rows(i))
                    if slot == 0 and i >= 1:
                        t = rows(i - 1)
                        dve.wait_ge(sq_done, i)
                        V.tensor_reduce(ms[0:t, :], sq[0:t, :].rearrange("p (h d) -> p h d", h=B_HEADS),
                                        AX.X, ALU.add).then_inc(ms_done, 1)
                    for pos in steps_now[1:]:
                        recur_keep(i, pos)
                    if slot == 2 and i >= 1:
                        t = rows(i - 1)
                        if i >= 2:
                            dve.wait_ge(yb_out, 16 * (i - 1))
                        for _ in range(2):
                            bank, h0 = half_unit()
                            V.tensor_copy(ybT[:, h0:h0 + H3, 0:t], bank[:, :, 0:t]).then_inc(hp_free, 1)



BRANCHES = [("w_out_a", 0, A_HEADS), ("w_out_b", YB0, B_HEADS), ("w_out_c", YC0, C_HEADS)]


def block_gate_merge(g):
    nc, io = g.nc, g.io
    n0 = g.slab
    slabs = [(b, j) for b in range(3) for j in range(D_MODEL // 256)]
    g.slab += len(slabs)
    units = [(s, b, 2 * j + ft, c0, n) for s, (b, j) in enumerate(slabs) for ft in range(2) for c0, n in GROUPS]
    per_branch = len(units) // 3
    pieces = [(b, k) for b in range(3) for k in range(BRANCHES[b][2])]
    NB, NG = 4, 4
    with ExitStack() as ctx:
        sb = lambda name, shape, dt=F32: ctx.enter_context(nc.sbuf_tensor("gm_" + name, shape, dt))
        y_hi, y_lo = sb("y_hi", [P, 2, A_HEADS, T_ALL], F32R), sb("y_lo", [P, 2, A_HEADS, T_ALL], F32R)
        y_raw, gate, tmp = sb("y_raw", [P, 2, T_ALL]), sb("gate", [P, NG, 384]), sb("tmp", [P, 384])
        sem = lambda name: g.sem("gm_" + name)
        y_in, hi_done, lo_done = [sem("y_in0"), sem("y_in1")], sem("hi"), sem("lo")
        gate_in = [sem(f"gate_in{j}") for j in range(NG)]
        full, gated, summed = sem("full"), sem("gated"), sem("summed")

        with nc.Block() as block:
            @block.sync
            def _(sp):
                def load_piece(m):
                    b, k = pieces[m]
                    if m >= 2:
                        sp.wait_ge(lo_done, m - 1)
                    sp.dma_start(y_raw[:, m % 2, :], g.d_y[BRANCHES[b][1] + k * P:BRANCHES[b][1] + (k + 1) * P, :]
                                 ).then_inc(y_in[m % 2], 16)

                def load_weights(s):
                    b, j = slabs[s]
                    load_slab(g, sp, n0 + s, w_cols(io[BRANCHES[b][0]][0], j * 256, 256), BRANCHES[b][2])

                load_weights(0)
                load_weights(1)
                m = 0
                for b in range(3):
                    while m < len(pieces) and pieces[m][0] <= min(b + 1, 2) and (b > 0 or pieces[m][0] == 0):
                        load_piece(m)
                        m += 1
                        if b == 0:
                            continue
                        break
                    for u in range(b * per_branch, (b + 1) * per_branch):
                        s, _, f, c0, n = units[u]
                        if u >= NG:
                            sp.wait_ge(gated, u - NG + 1)
                        row = b * D_MODEL + f * P
                        sp.dma_start(gate[:, u % NG, 0:n], g.d_gate[row:row + P, c0:c0 + n]).then_inc(gate_in[u % NG], 16)
                        if u % 4 == 3 and m < len(pieces) and pieces[m][0] == b + 1:
                            load_piece(m)
                            m += 1
                        if u % 6 == 5 and s + 2 < len(slabs):
                            load_weights(s + 2)
                        elif u % 6 == 5:
                            load_out(g, sp, s + 2 - len(slabs), n0 + s + 2)
                assert m == len(pieces)

            @block.gpsimd
            def _(pool):
                for s, (b, j) in enumerate(slabs):
                    split_slab(g, pool, n0 + s, BRANCHES[b][2] * 256)
                split_slab(g, pool, n0 + len(slabs), SLAB)

            @block.scalar
            def _(act):
                def split(m):
                    b, k = pieces[m]
                    act.wait_ge(y_in[m % 2], 16 * (m // 2 + 1))
                    if b == 2:
                        act.wait_ge(full, per_branch)
                    nc.scalar.activation(y_hi[:, b % 2, k, :], y_raw[:, m % 2, :], ACT.Copy).then_inc(hi_done, 1)

                round_slab(g, act, n0, BRANCHES[0][2] * 256)
                m = 0
                while pieces[m][0] == 0:
                    split(m)
                    m += 1
                round_slab(g, act, n0 + 1, BRANCHES[0][2] * 256)
                for u, (s, b, f, c0, n) in enumerate(units):
                    if u % 6 == 1 and u > 6:
                        size = BRANCHES[slabs[s + 1][0]][2] * 256 if s + 1 < len(slabs) else SLAB
                        round_slab(g, act, n0 + s + 1, size)
                    if u % 4 == 3 and m < len(pieces) and pieces[m][0] == b + 1:
                        act.wait_ge(full, u + 1)
                        split(m)
                        m += 1

            @block.tensor
            def _(pe):
                for u, (s, b, f, c0, n) in enumerate(units):
                    kt = BRANCHES[b][2]
                    if u % per_branch == 0:
                        pe.wait_ge(lo_done, sum(BRANCHES[q][2] for q in range(b + 1)))
                    if u % 6 == 0:
                        pe.wait_ge(g.w_split, n0 + s + 1)
                    if u >= NB:
                        pe.wait_ge(gated, u - NB + 1)
                    w, y = slab_view(g, n0 + s, kt, 256), (y_hi, y_lo)
                    fs, cs = slice((f % 2) * P, (f % 2 + 1) * P), slice(c0, c0 + n)
                    three_products(pe, g.ps[:, u % NB, 0:n], lambda a, k: w[a][:, k, fs],
                                   lambda a, k: y[a][:, b % 2, k, cs], kt).then_inc(full, 1)
                    if u % 6 == 5:
                        pe.drain().then_inc(g.w_used, 1)

            @block.vector
            def _(dve):
                def split(m):
                    b, k = pieces[m]
                    dve.wait_ge(hi_done, m + 1)
                    nc.vector.tensor_tensor(y_lo[:, b % 2, k, :], y_raw[:, m % 2, :],
                                            y_hi[:, b % 2, k, :].bitcast(F32), ALU.subtract).then_inc(lo_done, 1)

                m = 0
                while pieces[m][0] == 0:
                    split(m)
                    m += 1
                for u, (s, b, f, c0, n) in enumerate(units):
                    dve.wait_ge(full, u + 1)
                    dve.wait_ge(gate_in[u % NG], 16 * (u // NG + 1))
                    dst, ps, gt = g.merged[:, f, c0:c0 + n], g.ps[:, u % NB, 0:n], gate[:, u % NG, 0:n]
                    if b == 0:
                        nc.vector.tensor_tensor(dst, ps, gt, ALU.mult).then_inc(gated, 1)
                    else:
                        if u > per_branch:
                            dve.wait_ge(summed, u - per_branch)
                        nc.vector.tensor_tensor(tmp[:, 0:n], ps, gt, ALU.mult).then_inc(gated, 1)
                        dve.wait_ge(gated, u + 1)
                        nc.vector.tensor_tensor(dst, dst, tmp[:, 0:n], ALU.add).then_inc(summed, 1)
                    if u % 4 == 3 and m < len(pieces) and pieces[m][0] == b + 1:
                        split(m)
                        m += 1



def token_srcs(io):
    return [io["x_prompt"][0, i * P:(i + 1) * P, :] for i in range(TILE_P)] + [io["x_sample"][0]]


def load_out(g, sp, s, n):
    load_slab(g, sp, n, w_cols(g.io["w_out"][0], s * 256, 256), KT)


def load_up(g, sp, s, n):
    load_slab(g, sp, n, w_cols(g.io["w_up"][0], s * 256, 256), KT)


def block_out(g):
    nc, io = g.nc, g.io
    n0 = g.slab
    NSL = D_MODEL // 256
    g.slab += NSL
    NB = 4
    units = [(s, i) for s in range(NSL) for i in range(N_TILE)]
    spare = lambda k: g.big[:, k * D_MODEL:(k + 1) * D_MODEL]
    gain, junk, xin, x2 = spare(0), spare(1), [spare(2), spare(3)], [spare(4), spare(5)]
    with ExitStack() as ctx:
        sb = lambda name, shape: ctx.enter_context(nc.sbuf_tensor("out_" + name, shape, F32))
        o_all = sb("o_all", [P, N_TILE, D_MODEL])
        ss, s2 = sb("ss", [P, N_TILE]), sb("s2", [P, N_TILE])
        sem = lambda name: g.sem("out_" + name)
        hi_done, lo_done, full, kept = sem("hi"), sem("lo"), sem("full"), sem("kept")
        gain_in, x_in, x2_out = sem("gain_in"), [sem("x_in0"), sem("x_in1")], [sem("x2_out0"), sem("x2_out1")]
        sq1, v1, r1, q1, n1, x2_done, sq2, v2, r2, q2, n2 = (sem(n) for n in (
            "sq1", "v1", "r1", "q1", "n1", "x2_done", "sq2", "v2", "r2", "q2", "n2"))
        t_done, t_hi, t_lo, zeroed = sem("t_done"), sem("t_hi"), sem("t_lo"), sem("zeroed")
        srcs = token_srcs(io)
        turns = [(k, c0, n) for k in range(KT) for c0, n in GROUPS]

        with nc.Block() as block:
            def store(sp, i):
                sp.wait_ge(x2_done, i + 1)
                sp.dma_start(g.d_x2[row_slice(i), :], x2[i % 2][0:rows(i), :]).then_inc(x2_out[i % 2], 16)

            @block.sync
            def _(sp):
                for s in range(2, NSL):
                    load_out(g, sp, s, n0 + s)
                sp.wait_ge(lo_done, KT)
                sp.dma_start(gain, io["post_mix_gain"][0].partition_broadcast(P)).then_inc(gain_in, 16)
                for i in range(N_TILE):
                    r = rows(i)
                    if i == 2:
                        for s in range(2):
                            load_up(g, sp, s, n0 + NSL + s)
                    if i >= 2:
                        sp.wait_ge(x2_done, i - 1)
                    sp.dma_start(xin[i % 2][0:r, :], srcs[i]).then_inc(x_in[i % 2], 16)
                    if i >= 1:
                        store(sp, i - 1)
                store(sp, N_TILE - 1)
                sp.wait_ge(x2_out[0], 16 * ((N_TILE + 1) // 2))
                sp.wait_ge(x2_out[1], 16 * (N_TILE // 2))

            @block.gpsimd
            def _(pool):
                for s in range(1, NSL + 1):
                    split_slab(g, pool, n0 + s, SLAB)

            @block.scalar
            def _(act):
                for k in range(KT):
                    nc.scalar.activation(g.h_hi[:, k, 0:T_ALL], g.merged[:, k, :], ACT.Copy).then_inc(hi_done, 1)
                for u, (s, i) in enumerate(units):
                    if i == (1 if s else 0):
                        round_slab(g, act, n0 + s + 1, SLAB)
                    act.wait_ge(full, u + 1)
                    nc.scalar.activation(o_all[0:rows(i), i, s * 256:(s + 1) * 256], g.ps[0:rows(i), u % NB, 0:256],
                                         ACT.Copy).then_inc(kept, 1)
                    if s == NSL - 1:
                        r = rows(i)
                        if i == 0:
                            act.wait_ge(lo_done, KT)
                        act.wait_ge(kept, u + 1)
                        if i:
                            act.wait_ge(sq2, i)
                        nc.scalar.activation(junk[0:r, :], o_all[0:r, i, :], ACT.Square,
                                             accum_out=ss[0:r, i:i + 1]).then_inc(sq1, 1)
                        act.wait_ge(v1, i + 1)
                        nc.scalar.activation(ss[0:r, i:i + 1], ss[0:r, i:i + 1], ACT.Sqrt).then_inc(r1, 1)
                        act.wait_ge(x2_done, i + 1)
                        nc.scalar.activation(junk[0:r, :], x2[i % 2][0:r, :], ACT.Square,
                                             accum_out=s2[0:r, i:i + 1]).then_inc(sq2, 1)
                        act.wait_ge(v2, i + 1)
                        nc.scalar.activation(s2[0:r, i:i + 1], s2[0:r, i:i + 1], ACT.Sqrt).then_inc(r2, 1)
                for u, (k, c0, n) in enumerate(turns):
                    act.wait_ge(t_done, u + 1)
                    nc.scalar.activation(g.h_hi[:, k, c0:c0 + n], g.ps[:, u % 8, 0:n], ACT.Copy,
                                         scale=g.gains[:, 2, k:k + 1]).then_inc(t_hi, 1)

            @block.tensor
            def _(pe):
                pe.wait_ge(lo_done, KT)
                pe.wait_ge(zeroed, 2)
                x = (g.h_hi, g.h_lo)
                for u, (s, i) in enumerate(units):
                    if i == 0:
                        pe.wait_ge(g.w_split, n0 + s + 1)
                    if u >= NB:
                        pe.wait_ge(kept, u - NB + 1)
                    w, c = slab_view(g, n0 + s, KT, 256), slice(i * P, (i + 1) * P)
                    three_products(pe, g.ps[:, u % NB, 0:256], lambda a, k: x[a][:, k, c],
                                   lambda b, k: w[b][:, k, :], KT).then_inc(full, 1)
                    if i == N_TILE - 1:
                        pe.drain().then_inc(g.w_used, 1)
                pe.wait_ge(n2, N_TILE)
                for u, (k, c0, n) in enumerate(turns):
                    if u >= 8:
                        pe.wait_ge(t_lo, u - 7)
                    for j in range(-(-n // P)):
                        i = c0 // P + j
                        r = rows(i)
                        last = pe.transpose(g.ps[:, u % 8, j * P:j * P + r], o_all[0:r, i, k * P:(k + 1) * P],
                                            g.ident[0:r, 0:r])
                    last.then_inc(t_done, 1)

            @block.vector
            def _(dve):
                V = nc.vector
                for t in (g.h_hi, g.h_lo):
                    V.memset(t[:, :, T_ALL:T_PAD].bitcast(F32), 0.0).then_inc(zeroed, 1)
                for k in range(KT):
                    dve.wait_ge(hi_done, k + 1)
                    V.tensor_tensor(g.h_lo[:, k, 0:T_ALL], g.merged[:, k, :], g.h_hi[:, k, 0:T_ALL].bitcast(F32),
                                    ALU.subtract).then_inc(lo_done, 1)
                dve.wait_ge(gain_in, 16)
                for i in range(N_TILE):
                    r = rows(i)
                    o, a, b = o_all[0:r, i, :], ss[0:r, i:i + 1], s2[0:r, i:i + 1]
                    x_new = x2[i % 2][0:r, :]
                    dve.wait_ge(sq1, i + 1)
                    V.tensor_scalar(a, a, 1.0 / D_MODEL, EPS, ALU.mult, ALU.add).then_inc(v1, 1)
                    dve.wait_ge(r1, i + 1)
                    V.reciprocal(a, a).then_inc(q1, 1)
                    dve.wait_ge(q1, i + 1)
                    V.scalar_tensor_tensor(out=o, in0=o, scalar=a, in1=gain[0:r, :],
                                           op0=ALU.mult, op1=ALU.mult).then_inc(n1, 1)
                    dve.wait_ge(n1, i + 1)
                    dve.wait_ge(x_in[i % 2], 16 * (i // 2 + 1))
                    if i >= 2:
                        dve.wait_ge(x2_out[i % 2], 16 * (i // 2))
                    V.tensor_tensor(x_new, o, xin[i % 2][0:r, :], ALU.add).then_inc(x2_done, 1)
                    dve.wait_ge(sq2, i + 1)
                    V.tensor_scalar(b, b, 1.0 / D_MODEL, EPS, ALU.mult, ALU.add).then_inc(v2, 1)
                    dve.wait_ge(r2, i + 1)
                    V.reciprocal(b, b).then_inc(q2, 1)
                    dve.wait_ge(q2, i + 1)
                    V.tensor_scalar(o, x_new, b, None, ALU.mult).then_inc(n2, 1)
                for u, (k, c0, n) in enumerate(turns):
                    dve.wait_ge(t_hi, u + 1)
                    V.scalar_tensor_tensor(out=g.h_lo[:, k, c0:c0 + n], in0=g.ps[:, u % 8, 0:n],
                                           scalar=g.gains[:, 2, k:k + 1], in1=g.h_hi[:, k, c0:c0 + n].bitcast(F32),
                                           op0=ALU.mult, op1=ALU.subtract).then_inc(t_lo, 1)



FF_G = 512
FK = FF_G // P


def block_ffn(g):
    nc, io = g.nc, g.io
    n0 = g.slab
    N_GRP = D_FF // FF_G
    g.slab += 4 * N_GRP
    assert n0 % 2 == 0
    w_up, w_down = io["w_up"][0], io["w_down"][0]
    acc = g.big[:].rearrange("p (i c) -> p i c", c=D_MODEL)
    ups = [(f, c0, n) for f in range(FK) for c0, n in GROUPS]
    downs = [(half, i) for half in range(2) for i in range(N_TILE)]
    NU, ND = len(ups), len(downs)
    B_UP, B_DN = 4, 3
    LEAD = 4
    with ExitStack() as ctx:
        sb = lambda name, shape, dt=F32: ctx.enter_context(nc.sbuf_tensor("ff_" + name, shape, dt))
        u_hi, u_lo = sb("u_hi", [P, FK, T_PAD], F32R), sb("u_lo", [P, FK, T_PAD], F32R)
        relu, sq = sb("relu", [P, 2, 384]), sb("sq", [P, 2, 384])
        sem = lambda name: g.sem("ff_" + name)
        (up_full, up_free, squared, sq_made, u_ready, dn_full, acc_done, group_done, zeroed) = (sem(n) for n in (
            "up_full", "up_free", "squared", "sq_made", "u_ready", "dn_full", "acc_done", "group_done", "zeroed"))

        with nc.Block() as block:
            @block.sync
            def _(sp):
                def load(i, s):
                    n, slot = n0 + 4 * i + s, s % 2
                    sp.wait_ge(g.w_split, n - 1)
                    if s < 2:
                        src = w_up[:, bass.ds(i * FF_G + s * 256, 256)].rearrange("(k p) c -> p k c", p=P)
                        k = KT
                    else:
                        src = w_down[bass.ds(i * FF_G, FF_G), (s - 2) * 512:(s - 1) * 512].rearrange(
                            "(k p) c -> p k c", p=P)
                        k = FK
                    sp.dma_start(g.w_raw[:, slot, :].rearrange("p (k c) -> p k c", k=k), src
                                 ).then_inc(g.w_loaded[slot], 16)

                with sp.Fori(0, N_GRP - 1) as i:
                    load(i, 2)
                    load(i, 3)
                    load(i + 1, 0)
                    load(i + 1, 1)
                load(N_GRP - 1, 2)
                load(N_GRP - 1, 3)

            @block.gpsimd
            def _(pool):
                G = nc.gpsimd
                G.memset(u_hi[:, :, T_ALL:T_PAD].bitcast(F32), 0.0).then_inc(zeroed, 1)
                G.memset(u_lo[:, :, T_ALL:T_PAD].bitcast(F32), 0.0).then_inc(zeroed, 1)

                def split(n, slot):
                    pool.wait_ge(g.w_rounded, n + 1)
                    G.tensor_tensor(g.w_lo[:, slot, :], g.w_raw[:, slot, :], g.w_hi[:, slot, :].bitcast(F32),
                                    ALU.subtract).then_inc(g.w_split, 1)

                with pool.Fori(0, N_GRP - 1) as i:
                    for s in range(1, 5):
                        split(n0 + 4 * i + s, s % 2)
                for s in range(1, 4):
                    split(n0 + 4 * (N_GRP - 1) + s, s % 2)

            @block.scalar
            def _(act):
                S = nc.scalar

                def rounded(i, s):
                    n, slot = n0 + 4 * i + s, s % 2
                    act.wait_ge(g.w_loaded[slot], 16 * (n0 // 2 + 2 * i + s // 2 + 1))
                    act.wait_ge(g.w_used, n - 1)
                    S.activation(g.w_hi[:, slot, :], g.w_raw[:, slot, :], ACT.Copy).then_inc(g.w_rounded, 1)

                def group(i, last):
                    rounded(i, 1)
                    for u, (f, c0, n) in enumerate(ups):
                        if u == 7:
                            rounded(i, 2)
                        act.wait_ge(up_full, i * NU + u + 1)
                        act.wait_ge(u_ready, i * NU + u - 1 + LEAD)
                        S.activation(relu[:, u % 2, 0:n], g.ps[:, u % B_UP, 0:n], ACT.Relu).then_inc(up_free, 1)
                        act.wait_ge(up_free, i * NU + u + 1 + LEAD)
                        if u == 0:
                            act.wait_ge(group_done, i + 1)
                        S.activation(u_hi[:, f, c0:c0 + n], relu[:, u % 2, 0:n], ACT.Square).then_inc(squared, 1)
                    rounded(i, 3)
                    if not last:
                        rounded(i + 1, 0)

                with act.Fori(0, N_GRP - 1) as i:
                    group(i, False)
                group(N_GRP - 1, True)

            @block.vector
            def _(dve):
                V = nc.vector
                for half, t in downs:
                    V.memset(acc[:, t, half * 512:(half + 1) * 512], 0.0).then_inc(acc_done, 1)
                V.memset(sq[:, 0, 0:1], 0.0).then_inc(u_ready, LEAD)
                V.memset(sq[:, 0, 1:2], 0.0).then_inc(up_free, LEAD)
                V.memset(sq[:, 0, 2:3], 0.0).then_inc(group_done, 1)
                dve.wait_ge(group_done, 1)
                with dve.Fori(0, N_GRP) as i:
                    for u, (f, c0, n) in enumerate(ups):
                        dve.wait_ge(up_free, i * NU + u + 1 + LEAD)
                        V.tensor_tensor(sq[:, u % 2, 0:n], relu[:, u % 2, 0:n], relu[:, u % 2, 0:n],
                                        ALU.mult).then_inc(sq_made, 1)
                        dve.wait_ge(sq_made, i * NU + u + 1)
                        dve.wait_ge(squared, i * NU + u + 1)
                        V.tensor_tensor(u_lo[:, f, c0:c0 + n], sq[:, u % 2, 0:n], u_hi[:, f, c0:c0 + n].bitcast(F32),
                                        ALU.subtract).then_inc(u_ready, 1)
                    for d, (half, t) in enumerate(downs):
                        dst = acc[:, t, half * 512:(half + 1) * 512]
                        dve.wait_ge(dn_full, i * ND + d + 1)
                        dve.wait_ge(acc_done, i * ND + d + 1)
                        V.tensor_tensor(dst, dst, g.ps[:, 4 + d % B_DN, :], ALU.add).then_inc(acc_done, 1)

            @block.tensor
            def _(pe):
                pe.wait_ge(zeroed, 2)
                x, uu = (g.h_hi, g.h_lo), (u_hi, u_lo)
                with pe.Fori(0, N_GRP) as i:
                    for u, (f, c0, n) in enumerate(ups):
                        if u % 6 == 0:
                            pe.wait_ge(g.w_split, n0 + 4 * i + u // 6 + 1)
                        pe.wait_ge(up_free, i * NU + u - B_UP + 1 + LEAD)
                        w = slab_view(g, u // 6, KT, 256)
                        fs, cs = slice((f % 2) * P, (f % 2 + 1) * P), slice(c0, c0 + n)
                        three_products(pe, g.ps[:, u % B_UP, 0:n], lambda a, k: w[a][:, k, fs],
                                       lambda b, k: x[b][:, k, cs], KT).then_inc(up_full, 1)
                        if u % 6 == 5:
                            pe.drain().then_inc(g.w_used, 1)
                    for d, (half, t) in enumerate(downs):
                        if half == 0 and t % 3 == 0:
                            pe.wait_ge(u_ready, i * NU + NU - 2 + t // 3 + LEAD)
                        if t == 0:
                            pe.wait_ge(g.w_split, n0 + 4 * i + 3 + half)
                        pe.wait_ge(acc_done, i * ND + d - B_DN + 1 + ND)
                        w, c = slab_view(g, half, FK, 512), slice(t * P, (t + 1) * P)
                        three_products(pe, g.ps[:, 4 + d % B_DN, :], lambda a, k: uu[a][:, k, c],
                                       lambda b, k: w[b][:, k, :], FK).then_inc(dn_full, 1)
                        if t == N_TILE - 1:
                            pe.drain().then_inc(g.w_used, 1)
                    pe.drain().then_inc(group_done, 1)



def block_final(g):
    nc, io = g.nc, g.io
    acc = g.big[:].rearrange("p (i c) -> p i c", c=D_MODEL)
    with ExitStack() as ctx:
        sb = lambda name, shape: ctx.enter_context(nc.sbuf_tensor("fin_" + name, shape, F32))
        gain, junk, x2, ss = sb("gain", [P, D_MODEL]), sb("junk", [P, D_MODEL]), sb("x2", [P, N_TILE, D_MODEL]), sb("ss", [P, N_TILE])
        sem = lambda name: g.sem("fin_" + name)
        gain_in, x_in = sem("gain_in"), g.arrived
        sq, v, r_, q, n_, done, out, zeroed = (sem(n) for n in ("sq", "v", "r", "q", "n", "done", "out", "zeroed"))
        outs = [io["y_prompt"][0, i * P:(i + 1) * P, :] for i in range(TILE_P)] + [io["y_sample"][0]]
        with nc.Block() as block:
            @block.sync
            def _(sp):
                sp.dma_start(gain[:], io["post_ffn_gain"][0].partition_broadcast(P)).then_inc(gain_in, 16)
                for i in range(N_TILE):
                    sp.dma_start(x2[0:rows(i), i, :], g.d_x2[row_slice(i), :]).then_inc(x_in[i], 16)
                for i in range(N_TILE):
                    sp.wait_ge(done, i + 1)
                    sp.dma_start(outs[i], x2[0:rows(i), i, :]).then_inc(out, 16)
                sp.wait_ge(out, 16 * N_TILE)

            @block.scalar
            def _(act):
                act.wait_ge(zeroed, 1)
                for i in range(N_TILE):
                    r = rows(i)
                    if i:
                        act.wait_ge(sq, i)
                    nc.scalar.activation(junk[0:r, :], acc[0:r, i, :], ACT.Square,
                                         accum_out=ss[0:r, i:i + 1]).then_inc(sq, 1)
                act.wait_ge(v, 1)
                nc.scalar.activation(ss[:], ss[:], ACT.Sqrt).then_inc(r_, 1)

            @block.vector
            def _(dve):
                V = nc.vector
                V.memset(ss[:], 1.0).then_inc(zeroed, 1)
                dve.wait_ge(sq, N_TILE)
                V.tensor_scalar(ss[:], ss[:], 1.0 / D_MODEL, EPS, ALU.mult, ALU.add).then_inc(v, 1)
                dve.wait_ge(r_, 1)
                V.reciprocal(ss[:], ss[:]).then_inc(q, 1)
                dve.wait_ge(q, 1)
                dve.wait_ge(gain_in, 16)
                for i in range(N_TILE):
                    r = rows(i)
                    a = acc[0:r, i, :]
                    V.scalar_tensor_tensor(out=a, in0=a, scalar=ss[0:r, i:i + 1], in1=gain[0:r, :],
                                           op0=ALU.mult, op1=ALU.mult).then_inc(n_, 1)
                    dve.wait_ge(n_, i + 1)
                    dve.wait_ge(x_in[i], 32)
                    V.tensor_tensor(x2[0:r, i, :], a, x2[0:r, i, :], ALU.add).then_inc(done, 1)



_INS = ["x_prompt", "x_sample", "cache_k", "cache_v", "cache_idx_k", "state_hgrn", "cache_mem_k", "cache_mem_v",
        "mem_prompt", "w_in", "w_mem_kv", "mem_norm_gain", "hgrn_lb_logits", "hgrn_norm_gain", "w_out_a", "w_out_b",
        "w_out_c", "w_out", "pre_mix_gain", "post_mix_gain", "pre_ffn_gain", "post_ffn_gain", "w_up", "w_down"]
_OUTS = [("y_prompt", (1, SEQ, D_MODEL)), ("y_sample", (1, DEC, D_MODEL)),
         ("new_k_prompt", (1, 1, SEQ, A_KV, HD)), ("new_v_prompt", (1, 1, SEQ, A_KV, HD)),
         ("new_idx_k_prompt", (1, 1, SEQ, IDX_D)), ("new_hgrn_prompt", (1, 1, B_HEADS, HD, HD)),
         ("new_mem_k_prompt", (1, 1, N_MEM, C_HEADS, HD)), ("new_mem_v_prompt", (1, 1, N_MEM, C_HEADS, HD)),
         ("new_k_sample", (1, 1, DEC, A_KV, HD)), ("new_v_sample", (1, 1, DEC, A_KV, HD)),
         ("new_idx_k_sample", (1, 1, DEC, IDX_D)), ("new_hgrn_sample", (1, 1, B_HEADS, HD, HD))]


def _constants():
    pos = np.concatenate([np.arange(SEQ), PAST + np.arange(DEC)]).astype(np.float32)
    rope = np.zeros((N_TILE * P, ROPE_W), np.float32)
    for half, c, s in ((HD // 8, OFF_COS, OFF_SIN), (IDX_D // 8, OFF_ICOS, OFF_ISIN)):
        freq = np.float32(500000.0) ** (-np.arange(half, dtype=np.float32) / np.float32(half))
        ang = pos[:, None] * freq[None, :].astype(np.float32)
        rope[:T_ALL, c:c + half], rope[:T_ALL, s:s + half] = np.cos(ang), np.sin(ang)
    s, t = np.arange(P)[:, None], np.arange(P)[None, :]
    masks = []
    for h in LEVELS:
        same = s // (2 * h) == t // (2 * h)
        masks.append(same & (s <= t) if h == 1 else same & (s % (2 * h) < h) & (t % (2 * h) >= h))
    return {"c_ident": np.eye(P, dtype=np.float32),
            "c_rope": np.ascontiguousarray(rope.reshape(N_TILE, P, ROPE_W).transpose(1, 0, 2)),
            "c_masks": np.ascontiguousarray(np.stack(masks, 1).astype(np.int32))}


def kernel(**inputs):
    import numpy as _np
    import concourse.bacc as _bacc
    from concourse import mybir as _mybir
    from concourse.bass_utils import run_bass_kernel_spmd as _run

    nc = _bacc.Bacc("TRN2", target_bir_lowering=False, num_devices=1)
    arrays = {f"in_{n}": _np.ascontiguousarray(inputs[n]) for n in _INS}
    arrays.update({f"in_{n}": a for n, a in _constants().items()})
    io = {n[3:]: nc.dram_tensor(n, a.shape, _mybir.dt.from_np(a.dtype), kind="ExternalInput").ap()
          for n, a in arrays.items()}
    for name, shape in _OUTS:
        io[name] = nc.dram_tensor(f"out_{name}", shape, _mybir.dt.float32, kind="ExternalOutput").ap()
    build(nc, io)
    r = _run(nc, [arrays], core_ids=[0])
    return tuple(r.results[0][f"out_{name}"] for name, _ in _OUTS)
```

```python
from contextlib import ExitStack

import numpy as np
import concourse.bass as bass
from concourse import mybir

P = 128
D_MODEL, SEQ, DEC, PAST, N_MEM = 1024, 1024, 64, 128, 256
HD, IDX_D = 128, 64
A_HEADS, A_KV, IDX_HEADS, B_HEADS, C_HEADS = 6, 2, 8, 6, 4
GROUP = A_HEADS // A_KV
A_W, KV_W, IDX_W = A_HEADS * HD, A_KV * HD, IDX_HEADS * IDX_D
B_W, C_W = B_HEADS * HD, C_HEADS * HD
D_FF = 4 * D_MODEL
EPS, NEG, MASKED = 1e-6, -3.0e38, 1.0e30
TOPK_P, TOPK_S = min(256, SEQ // 4), min(256, (PAST + DEC) // 4)

T_ALL = SEQ + DEC
T_PAD = -(-T_ALL // P) * P
N_TILE = T_PAD // P
TILE_P = SEQ // P
KT = D_MODEL // P
GROUPS = [(0, 384), (384, 384), (768, T_ALL - 768)]
SLAB = 2048
SCALE = float(HD) ** -0.5
IDX_SCALE = float(IDX_D) ** -0.5 * float(IDX_HEADS) ** -0.5

OFF_Q = 0
OFF_K = OFF_Q + A_W
OFF_V = OFF_K + KV_W
OFF_IQ = OFF_V + KV_W
OFF_IK = OFF_IQ + IDX_W
OFF_IW = OFF_IK + IDX_D
OFF_BQ = OFF_IW + IDX_HEADS
OFF_BF = OFF_BQ + B_W
OFF_BI = OFF_BF + B_W
OFF_BG = OFF_BI + B_W
OFF_CQ = OFF_BG + B_W
OFF_G = OFF_CQ + C_W
IDX_KW = IDX_D + IDX_HEADS

F32, F32R, I32 = mybir.dt.float32, mybir.dt.float32r, mybir.dt.int32
ALU, ACT, AX = mybir.AluOpType, mybir.ActivationFunctionType, mybir.AxisListType

LEVELS = [1, 2, 4, 8, 16, 32, 64]
OFF_COS, OFF_SIN = 0, 16
OFF_ICOS, OFF_ISIN = 32, 40
ROPE_W = 48


class Shared:
    pass


class IndexBuffers:
    pass


class ForgetBuffers:
    pass


class SlabPlan:

    def __init__(self, kind, w, cols, units, func, rope=None, mem=False, kept=None):
        self.kind, self.w, self.cols, self.units = kind, w, cols, units
        self.func, self.rope, self.mem = func, rope, mem
        self.kept = kept or cols


def rows(i):
    return P if i < TILE_P else DEC


def n_keys(i):
    return (i + 1) * P if i < TILE_P else PAST + DEC


BIAS_OFF = [sum(n_keys(j) for j in range(i)) for i in range(N_TILE + 1)]


def bcast(ap, n):
    return ap.unsqueeze(2).to_broadcast([ap.shape[0], ap.shape[1], n])


def bcast_mid(ap, n):
    return ap.unsqueeze(1).to_broadcast([ap.shape[0], n, ap.shape[1]])


def build(nc, io):
    with ExitStack() as ctx:
        g = Shared()
        g.nc, g.io = nc, io
        g.sb = lambda name, shape, dt=F32: ctx.enter_context(nc.sbuf_tensor(name, shape, dt))
        g.sem = lambda name: ctx.enter_context(nc.semaphore(name))
        g.ps = ctx.enter_context(nc.psum_tensor("ps", [P, 8, 512], F32))
        dram = lambda name, shape: nc.dram_tensor(name, shape, F32, kind="Internal").ap()
        g.d_q = dram("d_q", (T_ALL, A_W))
        g.d_iq = dram("d_iq", (T_ALL, IDX_W))
        g.d_ik = dram("d_ik", (T_ALL, IDX_KW))
        g.d_bq = dram("d_bq", (B_W, T_ALL))
        g.d_cum = dram("d_cum", (B_W, T_ALL))
        g.d_kk = dram("d_kk", (B_W, T_ALL))
        g.d_bi = dram("d_bi", (T_ALL, B_W))
        g.d_bg = dram("d_bg", (T_ALL, B_W))
        g.d_cq = dram("d_cq", (C_W, T_ALL))
        g.d_gate = dram("d_gate", (3 * D_MODEL, T_ALL))
        g.d_y = dram("d_y", (A_W + B_W + C_W, T_ALL))
        g.d_x2 = dram("d_x2", (T_ALL, D_MODEL))

        g.ident = g.sb("ident", [P, P])
        g.gains = g.sb("gains", [P, 3, KT])
        ring_semaphores(g)
        with ExitStack() as mid:
            g.bias = mid.enter_context(nc.sbuf_tensor("bias", [P, BIAS_OFF[N_TILE]], F32))
            with ExitStack() as first:
                weight_ring(g, first, "w1")
                g.h_hi = first.enter_context(nc.sbuf_tensor("h_hi", [P, KT, T_PAD], F32R))
                g.h_lo = first.enter_context(nc.sbuf_tensor("h_lo", [P, KT, T_PAD], F32R))
                with ExitStack() as c0:
                    g.m_hi = c0.enter_context(nc.sbuf_tensor("m_hi", [P, KT, N_MEM], F32R))
                    g.m_lo = c0.enter_context(nc.sbuf_tensor("m_lo", [P, KT, N_MEM], F32R))
                    plans = plan_first(g), plan_second(g)
                    block_norm(g, plans[0][:2])
                    block_project(g, "b1", plans[0], False, plans[1][:2])
                block_project(g, "b2", plans[1], True, [])
            block_branches(g)
        with ExitStack() as last:
            weight_ring(g, last, "w2")
            g.big = last.enter_context(nc.sbuf_tensor("big", [P, N_TILE * D_MODEL], F32))
            g.merged = g.big[:, 0:KT * T_ALL].rearrange("p (k t) -> p k t", k=KT)
            block_gate_merge(g)
            g.h_at = -(-nc.sbuf_base // 64) * 64
            g.h_hi = last.enter_context(nc.sbuf_tensor("f_hi", [P, KT, T_PAD], F32R))
            g.h_lo = last.enter_context(nc.sbuf_tensor("f_lo", [P, KT, T_PAD], F32R))
            block_out(g)
            block_ffn(g)



def weight_ring(g, ctx, tag):
    sb = lambda name, dt: ctx.enter_context(g.nc.sbuf_tensor(f"{tag}_{name}", [P, 2, SLAB], dt))
    g.w_raw, g.w_hi, g.w_lo = sb("raw", F32), sb("hi", F32R), sb("lo", F32R)


def ring_semaphores(g):
    g.slab = 0
    g.arrived = [g.sem(f"arrived{i}") for i in range(N_TILE + N_MEM // P)]
    g.w_loaded = [g.sem("w_loaded0"), g.sem("w_loaded1")]
    g.w_rounded = g.sem("w_rounded")
    g.w_split = g.sem("w_split")


def load_slab(g, sp, n, src, k):
    if n >= 2:
        sp.wait_ge(g.w_split, n - 1)
    cols = src.shape[2]
    dst = g.w_raw[:, n % 2, 0:k * cols].rearrange("p (k c) -> p k c", k=k)
    sp.dma_start(dst, src).then_inc(g.w_loaded[n % 2], 16)


def round_slab(g, act, n, size):
    s = n % 2
    act.wait_ge(g.w_loaded[s], 16 * (n // 2 + 1))
    g.nc.scalar.activation(g.w_hi[:, s, 0:size], g.w_raw[:, s, 0:size], ACT.Copy).then_inc(g.w_rounded, 1)


def split_slab(g, engine, n, size):
    s = n % 2
    engine.wait_ge(g.w_rounded, n + 1)
    engine.tensor_tensor(g.w_lo[:, s, 0:size], g.w_raw[:, s, 0:size], g.w_hi[:, s, 0:size].bitcast(F32),
                         ALU.subtract).then_inc(g.w_split, 1)


def slab_view(g, n, k, cols):
    s = n % 2
    return [w[:, s, 0:k * cols].rearrange("p (k c) -> p k c", k=k) for w in (g.w_hi, g.w_lo)]


def three_products(pe, out, left, right, k):
    for kk in range(k):
        for n, (a, b) in enumerate(((0, 0), (0, 1), (1, 0))):
            last = pe.matmul(out, left(a, kk), right(b, kk),
                             start=(kk == 0 and n == 0), stop=(kk == k - 1 and n == 2))
    return last


def w_cols(w, c0, n):
    return w[:, c0:c0 + n].rearrange("(k p) c -> p k c", p=P)



def block_norm(g, ahead):
    nc, io = g.nc, g.io
    NT = N_TILE + N_MEM // P
    with ExitStack() as ctx:
        xs = ctx.enter_context(nc.sbuf_tensor("n_x", [P, NT, D_MODEL], F32))
        junk = ctx.enter_context(nc.sbuf_tensor("n_junk", [P, D_MODEL], F32))
        ss = ctx.enter_context(nc.sbuf_tensor("n_ss", [P, NT], F32))
        expo = ctx.enter_context(nc.sbuf_tensor("n_expo", [P, NT], F32))
        x_in = g.arrived
        c_in, zeroed, squared, roots = g.sem("n_const"), g.sem("n_zero"), g.sem("n_sq"), g.sem("n_roots")
        scaled, turned, hi_done, lo_done = g.sem("n_scaled"), g.sem("n_turned"), g.sem("n_hi"), g.sem("n_lo")
        srcs = [io["x_prompt"][0, i * P:(i + 1) * P, :] for i in range(TILE_P)] + [io["x_sample"][0]]
        srcs += [io["mem_prompt"][0, i * P:(i + 1) * P, :] for i in range(N_MEM // P)]
        groups = [(0, c0, n, [c0 // P + j for j in range(-(-n // P))]) for c0, n in GROUPS]
        groups.append((1, 0, N_MEM, [N_TILE + j for j in range(N_MEM // P)]))
        units = [(k,) + gr for gr in groups for k in range(KT)]
        order = [("rows", 0), ("rows", 1), ("turned", 0), ("rows", 2), ("turned", 1), ("rows", 3), ("turned", 2), ("turned", 3)]

        with nc.Block() as block:
            @block.sync
            def _(sp):
                for i, src in enumerate(srcs):
                    sp.dma_start(xs[0:src.shape[0], i, :], src).then_inc(x_in[i], 16)
                    if i == 1:
                        sp.dma_start(g.ident[:], io["c_ident"]).then_inc(c_in, 16)
                        for j, name in enumerate(("pre_mix_gain", "mem_norm_gain", "pre_ffn_gain")):
                            sp.dma_start(g.gains[:, j, :], io[name][0].rearrange("(k p) -> p k", p=P),
                                         allow_slow_non_contiguous=True).then_inc(c_in, 16)
                for n in range(2):
                    load_slab(g, sp, n, ahead[n].w, KT)

            @block.gpsimd
            def _(pool):
                G = nc.gpsimd
                G.memset(expo[:], -0.5).then_inc(zeroed, 1)
                pool.wait_ge(zeroed, 2)
                for m, (_, _, _, tiles) in enumerate(groups):
                    v = ss[:, tiles[0]:tiles[-1] + 1]
                    pool.wait_ge(squared, tiles[-1] + 1)
                    G.tensor_scalar(v, v, 1.0 / D_MODEL, EPS, ALU.mult, ALU.add).then_inc(roots, 1)
                    pool.wait_ge(roots, 2 * m + 1)
                    G.tensor_tensor(v, v, expo[:, 0:len(tiles)], ALU.pow).then_inc(roots, 1)
                split_slab(g, pool, 0, KT * ahead[0].cols)

            @block.scalar
            def _(act):
                act.wait_ge(zeroed, 2)
                for what, m in order:
                    if what == "rows":
                        for i in groups[m][3]:
                            r = srcs[i].shape[0]
                            act.wait_ge(x_in[i], 16)
                            if i:
                                act.wait_ge(squared, i)
                            nc.scalar.activation(junk[0:r, :], xs[0:r, i, :], ACT.Square,
                                                 accum_out=ss[0:r, i:i + 1]).then_inc(squared, 1)
                        continue
                    act.wait_ge(c_in, 64)
                    if m == len(groups) - 1:
                        round_slab(g, act, 0, KT * ahead[0].cols)
                    for u in range(m * KT, (m + 1) * KT):
                        k, which, c0, n, _ = units[u]
                        act.wait_ge(turned, u + 1)
                        dst = (g.h_hi, g.m_hi)[which][:, k, c0:c0 + n]
                        nc.scalar.activation(dst, g.ps[:, u % 8, 0:n], ACT.Copy,
                                             scale=g.gains[:, which, k:k + 1]).then_inc(hi_done, 1)

            @block.vector
            def _(dve):
                nc.vector.memset(ss[:], 1.0).then_inc(zeroed, 1)
                for t in (g.h_hi, g.h_lo):
                    nc.vector.memset(t[:, :, T_ALL:T_PAD].bitcast(F32), 0.0)
                for what, m in order:
                    if what == "rows":
                        dve.wait_ge(roots, 2 * m + 2)
                        for i in groups[m][3]:
                            r = srcs[i].shape[0]
                            nc.vector.tensor_scalar(xs[0:r, i, :], xs[0:r, i, :], ss[0:r, i:i + 1], None,
                                                    ALU.mult).then_inc(scaled, 1)
                        continue
                    for u in range(m * KT, (m + 1) * KT):
                        k, which, c0, n, _ = units[u]
                        dve.wait_ge(hi_done, u + 1)
                        hi = (g.h_hi, g.m_hi)[which][:, k, c0:c0 + n]
                        lo = (g.h_lo, g.m_lo)[which][:, k, c0:c0 + n]
                        nc.vector.scalar_tensor_tensor(out=lo, in0=g.ps[:, u % 8, 0:n],
                                                       scalar=g.gains[:, which, k:k + 1], in1=hi.bitcast(F32),
                                                       op0=ALU.mult, op1=ALU.subtract).then_inc(lo_done, 1)

            @block.tensor
            def _(pe):
                pe.wait_ge(c_in, 64)
                for u, (k, which, c0, n, tiles) in enumerate(units):
                    if k == 0:
                        pe.wait_ge(scaled, tiles[-1] + 1)
                    if u >= 8:
                        pe.wait_ge(lo_done, u - 7)
                    for j, i in enumerate(tiles):
                        r = srcs[i].shape[0]
                        last = pe.transpose(g.ps[:, u % 8, j * P:j * P + r], xs[0:r, i, k * P:(k + 1) * P],
                                            g.ident[0:r, 0:r])
                    last.then_inc(turned, 1)



def token_units(dests):
    return [(i, rows(i), dests(i)) for i in range(N_TILE)]


def row_slice(i):
    return slice(i * P, i * P + rows(i))


def feature_units(d, f0):
    return [(ft, c0, n, d[f0 + ft * P:f0 + (ft + 1) * P, c0:c0 + n]) for ft in range(2) for c0, n in GROUPS]


def kv_dest(io, prompt, sample, i):
    return io[prompt][0, 0, i * P:(i + 1) * P] if i < TILE_P else io[sample][0, 0]


def plan_first(g):
    io, plan = g.io, []
    w = io["w_in"][0]

    def memory(j):
        out = io["new_mem_k_prompt"] if j < 2 else io["new_mem_v_prompt"]
        out = out[0, 0].rearrange("n h d -> n (h d)")
        c0 = (j % 2) * 256
        units = [(i, P, [(out[i * P:(i + 1) * P, c0:c0 + 256], 0, 256)]) for i in range(N_MEM // P)]
        plan.append(SlabPlan("t", w_cols(io["w_mem_kv"][0], j * 256, 256), 256, units, ACT.Copy, mem=True))

    for j in range(2):
        plan.append(SlabPlan("t", w_cols(w, OFF_IQ + j * 256, 256), 256,
                              token_units(lambda i: [(g.d_iq[row_slice(i), j * 256:(j + 1) * 256], 0, 256)]),
                              ACT.Copy, rope=(4, IDX_D, 8, OFF_ICOS, OFF_ISIN)))
        memory(j)
    plan.append(SlabPlan("t", w_cols(w, OFF_IK, 256), 256,
                          token_units(lambda i: [(g.d_ik[row_slice(i), :], 0, IDX_KW),
                                                 (kv_dest(io, "new_idx_k_prompt", "new_idx_k_sample", i), 0, IDX_D)]),
                          ACT.Copy, rope=(1, IDX_D, 8, OFF_ICOS, OFF_ISIN), kept=IDX_KW))
    memory(2)
    memory(3)
    return plan


def plan_second(g):
    io, plan = g.io, []
    w = io["w_in"][0]
    rope = (2, HD, 16, OFF_COS, OFF_SIN)

    def flat(name_p, name_s, i):
        return kv_dest(io, name_p, name_s, i).rearrange("t h d -> t (h d)")

    plan.append(SlabPlan("t", w_cols(w, OFF_K, 256), 256,
                          token_units(lambda i: [(flat("new_k_prompt", "new_k_sample", i), 0, 256)]),
                          ACT.Copy, rope=rope))
    plan.append(SlabPlan("t", w_cols(w, OFF_V, 256), 256,
                          token_units(lambda i: [(flat("new_v_prompt", "new_v_sample", i), 0, 256)]), ACT.Copy))

    def to_rows(d, off, n, func, rope=None):
        for j in range(n):
            plan.append(SlabPlan("t", w_cols(w, off + j * 256, 256), 256,
                                  token_units(lambda i: [(d[row_slice(i), j * 256:(j + 1) * 256], 0, 256)]),
                                  func, rope=rope))

    def to_features(d, off, n, func):
        for j in range(n):
            plan.append(SlabPlan("f", w_cols(w, off + j * 256, 256), 256, feature_units(d, j * 256), func))

    to_rows(g.d_q, OFF_Q, 3, ACT.Copy, rope=rope)
    to_rows(g.d_bi, OFF_BI, 3, ACT.Copy)
    to_features(g.d_cq, OFF_CQ, 2, ACT.Copy)
    to_rows(g.d_bg, OFF_BG, 3, ACT.Silu)
    to_features(g.d_bq, OFF_BQ, 3, ACT.Silu)
    n_late = 3
    gates = [(g.d_gate[j * 256:], OFF_G + j * 256) for j in range(3 * D_MODEL // 256)]
    for d, off in gates[:-n_late]:
        to_features(d, off, 1, ACT.Sigmoid)
    for j in range(3):
        plan.append(SlabPlan("decay", w_cols(w, OFF_BF + j * 256, 256), 256,
                             [(ft, c0, n, 2 * j + ft) for ft in range(2) for c0, n in GROUPS], ACT.Sigmoid))
    for d, off in gates[-n_late:]:
        to_features(d, off, 1, ACT.Sigmoid)
    return plan


def block_project(g, tag, plan, with_index, ahead):
    nc, io = g.nc, g.io
    n0 = g.slab
    g.slab += len(plan)
    NB, NS = 4, 8
    coming = plan + ahead
    order = []
    for s, sl in enumerate(plan):
        order += [(s, u) for u in sl.units]
    first = [sum(len(q.units) for q in plan[:s]) for s in range(len(plan) + 1)]
    roped = []
    for s, u in order:
        roped.append((roped[-1] if roped else 0) + (plan[s].rope is not None))
    n_out = []
    per = [0] * NS
    for n, (s, u) in enumerate(order):
        per[n % NS] += {"t": lambda: len(u[2]), "f": lambda: 1, "decay": lambda: 2}[plan[s].kind]()
        n_out.append(per[n % NS])
    with ExitStack() as ctx:
        stage = ctx.enter_context(nc.sbuf_tensor(f"{tag}_stage", [P, NS, 384], F32))
        cs = ctx.enter_context(nc.sbuf_tensor(f"{tag}_cs", [P, N_TILE, ROPE_W], F32))
        rt = ctx.enter_context(nc.sbuf_tensor(f"{tag}_rt", [P, 4, 32], F32))
        cs_in, full, staged = g.sem(f"{tag}_cs_in"), g.sem(f"{tag}_full"), g.sem(f"{tag}_staged")
        rope_part, rope_done = g.sem(f"{tag}_rope_part"), g.sem(f"{tag}_roped")
        stored = [g.sem(f"{tag}_stored{j}") for j in range(NS)]
        ix = index_setup(g, ctx) if with_index else None
        fg = forget_setup(g, ctx, ix) if with_index else None
        decays = [n for n, (s, u) in enumerate(order) if plan[s].kind == "decay"]

        with nc.Block() as block:
            @block.sync
            def _(sp):
                sp.dma_start(cs[:], io["c_rope"]).then_inc(cs_in, 16)
                if ix:
                    sp.dma_start(fg.lgt[:], io["hgrn_lb_logits"].rearrange("r (h p) -> p r h", p=P),
                                 allow_slow_non_contiguous=True).then_inc(fg.set_, 16)
                    index_loads(g, ix, sp)
                for s, sl in enumerate(plan):
                    if s + 2 < len(coming):
                        load_slab(g, sp, n0 + s + 2, coming[s + 2].w, KT)
                    for n in range(first[s], first[s + 1]):
                        u = order[n][1]
                        if sl.kind == "decay":
                            ft, c0, w, h = u
                            sp.wait_ge(fg.summed, n - decays[0] + 1)
                            for dst, src in ((g.d_kk, fg.kk), (g.d_cum, fg.cum)):
                                sp.dma_start(dst[h * P:(h + 1) * P, c0:c0 + w],
                                             src[:, n % NS, 0:w]).then_inc(stored[n % NS], 16)
                            continue
                        if sl.rope:
                            sp.wait_ge(rope_done, roped[n])
                        else:
                            sp.wait_ge(staged, n + 1)
                        if sl.kind == "t":
                            for dst, c0, c in u[2]:
                                sp.dma_start(dst, stage[0:u[1], n % NS, c0:c0 + c]).then_inc(stored[n % NS], 16)
                        else:
                            sp.dma_start(u[3], stage[:, n % NS, 0:u[2]]).then_inc(stored[n % NS], 16)
                for j in range(NS):
                    sp.wait_ge(stored[j], 16 * per[j])

            @block.gpsimd
            def _(pool):
                pool.wait_ge(cs_in, 16)
                parts = 0
                for s, sl in enumerate(plan):
                    if ix and s + 1 < len(coming):
                        split_slab(g, pool, n0 + s + 1, KT * coming[s + 1].cols)
                    if not sl.rope:
                        continue
                    heads, width, half, co, so = sl.rope
                    for n in range(first[s], first[s + 1]):
                        i, r, _ = order[n][1]
                        x = stage[0:r, n % NS, 0:heads * width].rearrange("p (h d) -> p h d", h=heads)
                        x1, x2 = x[:, :, 0:half], x[:, :, half:2 * half]
                        cos = bcast_mid(cs[0:r, i, co:co + half], heads)
                        sin = bcast_mid(cs[0:r, i, so:so + half], heads)
                        t = [rt[0:r, j, 0:heads * half].rearrange("p (h d) -> p h d", h=heads) for j in range(4)]
                        pool.wait_ge(staged, n + 1)
                        if parts:
                            pool.wait_ge(rope_done, parts)
                        for j, (a, b) in enumerate(((x1, cos), (x2, sin), (x2, cos), (x1, sin))):
                            last = nc.gpsimd.tensor_tensor(t[j], a, b, ALU.mult)
                        parts += 1
                        last.then_inc(rope_part, 1)
                        pool.wait_ge(rope_part, parts)
                        nc.gpsimd.tensor_tensor(x1, t[0], t[1], ALU.subtract)
                        nc.gpsimd.tensor_tensor(x2, t[2], t[3], ALU.add).then_inc(rope_done, 1)

            @block.scalar
            def _(act):
                if ix:
                    act.wait_ge(fg.lb_step, 1)
                    nc.scalar.activation(fg.lgt[:], fg.lgt[:], ACT.Exp).then_inc(fg.lb_exp, 1)
                for s, sl in enumerate(plan):
                    for n in range(first[s], first[s + 1]):
                        u = order[n][1]
                        if n == first[s] and s + 1 < len(coming):
                            if s:
                                act.wait_ge(full, n)
                            round_slab(g, act, n0 + s + 1, KT * coming[s + 1].cols)
                        act.wait_ge(full, n + 1)
                        if n >= NS:
                            act.wait_ge(stored[n % NS], 16 * n_out[n - NS])
                        r, c = (u[1], sl.kept) if sl.kind == "t" else (P, u[2])
                        nc.scalar.activation(stage[0:r, n % NS, 0:c], g.ps[0:r, n % NB, 0:c],
                                             sl.func).then_inc(staged, 1)
                    if sl.kind == "decay":
                        for n in range(first[s], first[s + 1]):
                            x = stage[:, n % NS, 0:order[n][1][2]]
                            act.wait_ge(fg.made, n - decays[0] + 1)
                            nc.scalar.activation(x, x, ACT.Ln).then_inc(fg.logged, 1)
                    if ix:
                        index_act(g, ix, act, s)

            @block.tensor
            def _(pe):
                for s, sl in enumerate(plan):
                    w = slab_view(g, n0 + s, KT, sl.cols)
                    x = (g.m_hi, g.m_lo) if sl.mem else (g.h_hi, g.h_lo)
                    pe.wait_ge(g.w_split, n0 + s + 1)
                    for n in range(first[s], first[s + 1]):
                        u = order[n][1]
                        if n >= NB:
                            pe.wait_ge(staged, n - NB + 1)
                        if sl.kind == "t":
                            c = slice(u[0] * P, (u[0] + 1) * P)
                            last = three_products(pe, g.ps[:, n % NB, 0:sl.cols],
                                                  lambda a, k: x[a][:, k, c], lambda b, k: w[b][:, k, :], KT)
                        else:
                            f, c = slice(u[0] * P, (u[0] + 1) * P), slice(u[1], u[1] + u[2])
                            last = three_products(pe, g.ps[:, n % NB, 0:u[2]],
                                                  lambda a, k: w[a][:, k, f], lambda b, k: x[b][:, k, c], KT)
                        last.then_inc(full, 1)
                    if ix and s == 0:
                        index_turn(g, ix, pe)
                    if ix:
                        index_scores(g, ix, pe, s)

            if not ix:
                @block.vector
                def _(dve):
                    for s in range(1, len(coming) - 1):
                        split_slab(g, dve, n0 + s, KT * coming[s].cols)
            if ix:
                @block.vector
                def _(dve):
                    forget_bounds(g, fg, dve)
                    index_select(g, ix, dve)
                    for s, sl in enumerate(plan):
                        if sl.kind != "decay":
                            continue
                        for n in range(first[s], first[s + 1]):
                            ft, c0, w, h = order[n][1]
                            x = stage[:, n % NS, 0:w]
                            dve.wait_ge(staged, n + 1)
                            nc.vector.tensor_scalar(x, x, fg.oml[:, h:h + 1], fg.lb[:, h:h + 1],
                                                    ALU.mult, ALU.add).then_inc(fg.f_made, 1)
                            dve.wait_ge(fg.f_made, n - decays[0] + 2)
                            nc.vector.tensor_scalar(fg.kk[:, n % NS, 0:w], x, -1.0, 1.0,
                                                    ALU.mult, ALU.add).then_inc(fg.made, 1)
                        for n in range(first[s], first[s + 1]):
                            w = order[n][1][2]
                            dve.wait_ge(fg.logged, n - decays[0] + 1)
                            for c in range(0, w, P):
                                e = min(c + P, w)
                                last = nc.vector.tensor_tensor_scan(fg.cum[:, n % NS, c:e], stage[:, n % NS, c:e],
                                                                    fg.zero[:, 0:e - c], 0.0, ALU.add, ALU.add)
                            last.then_inc(fg.summed, 1)



def forget_setup(g, ctx, ix):
    sb = lambda name, shape: ctx.enter_context(g.nc.sbuf_tensor("fg_" + name, shape, F32))
    fg = ForgetBuffers()
    fg.lgt, fg.lb, fg.oml = sb("lgt", [P, 2, B_HEADS]), sb("lb", [P, B_HEADS]), sb("oml", [P, B_HEADS])
    fg.lmx, fg.zero = sb("lmx", [P, B_HEADS]), sb("zero", [P, P])
    fg.kk = ix.work[:].rearrange("p a b -> p (a b)").rearrange("p (j c) -> p j c", c=384)
    fg.cum = ix.qT[:].rearrange("p a b -> p (a b)")[:, 0:8 * 384].rearrange("p (j c) -> p j c", c=384)
    fg.set_, fg.lb_step, fg.lb_exp = g.sem("fg_set"), g.sem("fg_lb_step"), g.sem("fg_lb_exp")
    fg.f_made, fg.made, fg.logged, fg.summed = (g.sem("fg_f_made"), g.sem("fg_made"), g.sem("fg_logged"),
                                                g.sem("fg_summed"))
    return fg


def forget_bounds(g, fg, dve):
    V = g.nc.vector
    dve.wait_ge(fg.set_, 16)
    V.memset(fg.zero[:], 0.0)
    V.tensor_tensor(fg.lmx[:], fg.lgt[:, 0, :], fg.lgt[:, 1, :], ALU.max).then_inc(fg.f_made, 1)
    dve.wait_ge(fg.f_made, 1)
    for r in range(2):
        last = V.tensor_tensor(fg.lgt[:, r, :], fg.lgt[:, r, :], fg.lmx[:], ALU.subtract)
    last.then_inc(fg.lb_step, 1)
    dve.wait_ge(fg.lb_exp, 1)
    V.tensor_tensor(fg.lmx[:], fg.lgt[:, 0, :], fg.lgt[:, 1, :], ALU.add).then_inc(fg.lb_step, 1)
    dve.wait_ge(fg.lb_step, 2)
    V.reciprocal(fg.lmx[:], fg.lmx[:]).then_inc(fg.lb_step, 1)
    dve.wait_ge(fg.lb_step, 3)
    V.tensor_tensor(fg.lb[:], fg.lgt[:, 0, :], fg.lmx[:], ALU.mult).then_inc(fg.lb_step, 1)
    dve.wait_ge(fg.lb_step, 4)
    V.tensor_scalar(fg.oml[:], fg.lb[:], -1.0, 1.0, ALU.mult, ALU.add).then_inc(fg.lb_step, 1)
    dve.wait_ge(fg.lb_step, 5)



SCORED = list(range(2, N_TILE))
SCORED_AFTER = {1: [2, 3], 2: [4, 5], 3: [6, 7], 4: [8]}
IX_BANKS = 4


def index_setup(g, ctx):
    nc = g.nc
    sb = lambda name, shape: ctx.enter_context(nc.sbuf_tensor(name, shape, F32))
    ix = IndexBuffers()
    ix.qT = sb("ix_qT", [P, IDX_W // P, T_ALL])
    ix.kT = sb("ix_kT", [P, SEQ + PAST + DEC])
    ix.w = sb("ix_w", [P, N_TILE, IDX_HEADS])
    ix.relu = sb("ix_relu", [P, 3, 512])
    ix.work = sb("ix_work", [P, 3, 1024])
    ix.m8 = sb("ix_m8", [P, 8])
    ix.cnt = sb("ix_cnt", [P, 1])
    ix.in_, ix.turned, ix.kept, ix.scored = g.sem("ix_in"), g.sem("ix_turned"), g.sem("ix_kept"), g.sem("ix_scored")
    ix.relued, ix.added, ix.step = g.sem("ix_relued"), g.sem("ix_added"), g.sem("ix_step")
    ix.q_rows = g.bias[:, 0:N_TILE * IDX_W].rearrange("p (i c) -> p i c", i=N_TILE)
    ix.k_rows = ix.work[:].rearrange("p a b -> p (a b)")[:, 0:(N_TILE + 1) * P].rearrange("p (i c) -> p i c", c=P)
    ix.k_tiles = [(j, P, j * P) for j in range(TILE_P)] + [(N_TILE, P, SEQ), (TILE_P, DEC, SEQ + PAST)]
    ix.units = [(i, h, c, min(512, n_keys(i) - c)) for i in SCORED
                for c in range(0, n_keys(i), 512) for h in range(IDX_HEADS)]
    ix.turns = [("q", i) for i in range(N_TILE)] + [("k", j) for j in range(len(ix.k_tiles))]
    ix.n_in = 0
    return ix


def index_loads(g, ix, sp):
    def load(dst, src):
        sp.dma_start(dst, src, allow_slow_non_contiguous=True).then_inc(ix.in_, 16)
        ix.n_in += 16
    for i in range(N_TILE):
        r = rows(i)
        load(ix.q_rows[0:r, i, :], g.d_iq[row_slice(i), :])
        load(ix.w[0:r, i, :], g.d_ik[row_slice(i), IDX_D:IDX_KW])
        for c in range(0, P, IDX_D):
            load(ix.k_rows[0:r, i, c:c + IDX_D], g.d_ik[row_slice(i), 0:IDX_D])
    for c in range(0, P, IDX_D):
        load(ix.k_rows[:, N_TILE, c:c + IDX_D], g.io["cache_idx_k"][0, 0])


def index_turn(g, ix, pe):
    pe.wait_ge(ix.in_, ix.n_in)
    for n, (kind, j) in enumerate(ix.turns):
        bank = g.ps[:, 4 + n % IX_BANKS, :]
        if n >= IX_BANKS:
            pe.wait_ge(ix.kept, n - IX_BANKS + 1)
        if kind == "q":
            r = rows(j)
            for f in range(IDX_W // P):
                last = pe.transpose(bank[:, f * P:f * P + r], ix.q_rows[0:r, j, f * P:(f + 1) * P],
                                    g.ident[0:r, 0:r])
        else:
            src, r, _ = ix.k_tiles[j]
            last = pe.transpose(bank[:, 0:r], ix.k_rows[0:r, src, :], g.ident[0:r, 0:r])
        last.then_inc(ix.turned, 1)


def index_scores(g, ix, pe, s):
    for n, (i, h, c, w) in enumerate(ix.units):
        if i not in SCORED_AFTER.get(s, []):
            continue
        if n == 0:
            pe.wait_ge(ix.kept, len(ix.turns))
        if n >= IX_BANKS:
            pe.wait_ge(ix.relued, n - IX_BANKS + 1)
        half = slice((h % 2) * IDX_D, (h % 2) * IDX_D + IDX_D)
        k0 = (0 if i < TILE_P else SEQ) + c
        pe.matmul(g.ps[0:rows(i), 4 + n % IX_BANKS, 0:w], ix.qT[half, h // 2, row_slice(i)],
                  ix.kT[half, k0:k0 + w], start=True, stop=True).then_inc(ix.scored, 1)


def index_act(g, ix, act, s):
    for n, (i, h, c, w) in enumerate(ix.units):
        if i not in SCORED_AFTER.get(s, []):
            continue
        act.wait_ge(ix.scored, n + 1)
        if n >= 3:
            act.wait_ge(ix.added, n - 2)
        g.nc.scalar.activation(ix.relu[0:rows(i), n % 3, 0:w], g.ps[0:rows(i), 4 + n % IX_BANKS, 0:w],
                               ACT.Relu, scale=IDX_SCALE).then_inc(ix.relued, 1)


def index_select(g, ix, dve):
    v = g.nc.vector
    for n, (kind, j) in enumerate(ix.turns):
        bank = g.ps[:, 4 + n % IX_BANKS, :]
        dve.wait_ge(ix.turned, n + 1)
        if kind == "q":
            r = rows(j)
            src = bank.rearrange("p (f t) -> p f t", t=P)[:, :, 0:r]
            v.tensor_copy(ix.qT[:, :, j * P:j * P + r], src).then_inc(ix.kept, 1)
        else:
            _, r, c0 = ix.k_tiles[j]
            v.tensor_copy(ix.kT[:, c0:c0 + r], bank[:, 0:r]).then_inc(ix.kept, 1)
    for n, (i, h, c, w) in enumerate(ix.units):
        r, sc = rows(i), g.bias[0:rows(i), BIAS_OFF[i] + c:BIAS_OFF[i] + c + w]
        dve.wait_ge(ix.relued, n + 1)
        relu, weight = ix.relu[0:r, n % 3, 0:w], ix.w[0:r, i, h:h + 1]
        if h == 0:
            v.tensor_scalar(sc, relu, weight, None, ALU.mult).then_inc(ix.added, 1)
        else:
            dve.wait_ge(ix.added, n)
            v.scalar_tensor_tensor(out=sc, in0=relu, scalar=weight, in1=sc,
                                   op0=ALU.mult, op1=ALU.add).then_inc(ix.added, 1)
    dve.wait_ge(ix.added, len(ix.units))

    steps = [0]

    def link(ins):
        steps[0] += 1
        ins.then_inc(ix.step, 1)
        dve.wait_ge(ix.step, steps[0])

    for i in range(N_TILE):
        n, r = n_keys(i), rows(i)
        sc = g.bias[0:r, BIAS_OFF[i]:BIAS_OFF[i + 1]]
        if i < 2:
            link(v.memset(sc, 0.0))
            link(v.memset(sc[0:64, n - 64:n], -MASKED))
            continue
        if i < TILE_P:
            link(v.memset(sc[0:64, n - 64:n], NEG))
        topk = TOPK_P if i < TILE_P else TOPK_S
        left, eq, cum = (ix.work[0:r, j, 0:n] for j in range(3))
        m8, cnt = ix.m8[0:r, :], ix.cnt[0:r, :]
        for it in range(topk // 8):
            link(v.max(m8, sc if it == 0 else left))
            if it < topk // 8 - 1:
                link(v.match_replace(left, m8, sc if it == 0 else left, NEG))
        bar = m8[:, 7:8]
        link(v.tensor_scalar(left, sc, bar, 0.0, ALU.is_gt, ALU.add, accum_out=cnt))
        link(v.tensor_scalar(cnt, cnt, -1.0, float(topk), ALU.mult, ALU.add))
        link(v.tensor_scalar(eq, sc, bar, None, ALU.is_equal))
        link(v.tensor_tensor_scan(cum, eq, eq, 0.0, ALU.add, ALU.max))
        link(v.scalar_tensor_tensor(out=eq, in0=cum, scalar=cnt, in1=eq, op0=ALU.is_le, op1=ALU.mult))
        link(v.tensor_tensor(left, left, eq, ALU.add))
        link(v.tensor_scalar(sc, left, -1.0, MASKED, ALU.add, ALU.mult))



N_HEAD = N_TILE * A_HEADS
N_SLOT = N_HEAD + 4
H3 = B_HEADS // 2
YB0, YC0 = A_W, A_W + B_W


def stages(i):
    return [h for h in LEVELS if 2 * h <= rows(i)] + ["q", "k"]


STEP0 = [sum(len(stages(j)) for j in range(i)) for i in range(N_TILE + 1)]


def v_tiles(i):
    if i < TILE_P:
        return [(j, P) for j in range(i + 1)]
    return [(TILE_P, P), (TILE_P + 1, DEC)]


def block_branches(g):
    nc, io = g.nc, g.io
    V, S, G = nc.vector, nc.scalar, nc.gpsimd
    with ExitStack() as ctx:
        sb = lambda name, shape, dt=F32: ctx.enter_context(nc.sbuf_tensor("br_" + name, shape, dt))
        kT = sb("kT", [P, A_KV, SEQ + PAST + DEC])
        val = sb("val", [P, N_TILE + 1, KV_W])
        mkT = sb("mkT", [P, 2, C_HEADS, N_MEM])
        mval = sb("mval", [P, 2, N_MEM // P, C_W])
        pT = sb("pT", [P, TILE_P, A_HEADS, P])
        nat = pT[:].rearrange("p a b c -> p (a b c)")
        k_nat = nat[:, 0:(N_TILE + 1) * KV_W].rearrange("p (j c) -> p j c", c=KV_W)
        m_nat = nat[:, (N_TILE + 1) * KV_W:(N_TILE + 1) * KV_W + 4 * C_W].rearrange("p (m j c) -> p m j c", m=2, j=2)
        q_nat, qT = sb("q_nat", [P, 2, A_W]), sb("qT", [P, 2, A_HEADS, P])
        prob = sb("prob", [P, 3, 1024])
        top, ntop, den = sb("top", [P, 8]), sb("ntop", [P, 8]), sb("den", [P, 8])
        part = sb("part", [P, 1])
        cq = sb("cq", [P, 2, C_HEADS, P])
        cp, cpT = sb("cp", [P, C_HEADS, N_MEM]), sb("cpT", [P, C_HEADS, 2, P])
        ctop, cden = sb("ctop", [P, C_HEADS]), sb("cden", [P, C_HEADS])
        ysb = sb("ysb", [P, 3, 512])
        cum, bq = sb("cum", [P, 2, B_W]), sb("bq", [P, 2, B_W])
        bv, bg = sb("bv", [P, 2, B_W]), sb("bg", [P, 2, B_W])
        kk = sb("kk", [P, 2, B_W])
        dif, ex, wk = sb("dif", [P, 2, B_W]), sb("ex", [P, 2, B_W]), sb("wk", [P, 2, B_W])
        exn, kp = sb("exn", [P, B_W]), sb("kp", [P, B_W])
        smat, kdT = sb("smat", [P, B_HEADS, P]), sb("kdT", [P, B_W])
        osb, sq = sb("osb", [P, B_W]), sb("sq", [P, B_W])
        ybT = sb("ybT", [P, B_HEADS, P])
        ms, expo = sb("ms", [P, B_HEADS]), sb("expo", [P, B_HEADS])
        eb = sb("eb", [P, B_HEADS])
        state = [sb("stateP", [P, B_HEADS, HD]), sb("stateS", [P, B_HEADS, HD])]
        masks, grow = sb("masks", [P, len(LEVELS), P], I32), sb("grow", [P, B_W])

        sem = lambda name: g.sem("br_" + name)
        k_set, mk_set, s_set, s_step = sem("k_set"), sem("mk_set"), sem("set"), sem("step")
        s_in, q_in = [sem("in0"), sem("in1")], [sem("q_in0"), sem("q_in1")]
        t_done, t_kept = sem("t_done"), sem("t_kept")
        s_done, s_masked, ntop_ok, e_done, p_done = (sem("s_done"), sem("s_masked"), sem("ntop"), sem("exp"),
                                                     sem("p_done"))
        c_done, c_top, c_exp, c_norm = sem("c_done"), sem("c_top"), sem("c_exp"), sem("c_norm")
        o_done, o_kept = sem("o_done"), sem("o_kept")
        y_out = [sem(f"y_out{j}") for j in range(3)]
        yb_out, st_out = sem("yb_out"), sem("st_out")
        d_done, x_done, w_done = sem("d_done"), sem("x_done"), sem("w_done")
        hp_done, hp_free, s_cleared = sem("hp_done"), sem("hp_free"), sem("s_cleared")
        sq_done, ms_done, rs_done, o_normed, y_done, gg_done = (sem("sq"), sem("ms"), sem("rs"), sem("o_normed"),
                                                              sem("y_done"), sem("gg"))

        k_rows = [(j, P, j * P) for j in range(TILE_P)] + [(TILE_P, P, SEQ), (TILE_P + 1, DEC, SEQ + PAST)]
        N_SET = 16 * (3 + 2 + 2)

        def due(n):
            i, slot = divmod(n, A_HEADS)
            if slot == A_HEADS - 1:
                return [(i + 1, 0)] if i + 1 < N_TILE else []
            return [(i, p) for p in (2 * slot + 1, 2 * slot + 2) if i < N_TILE and p < len(stages(i))]

        def halves(n):
            steps = due(n)
            return steps[:len(steps) // 2], steps[len(steps) // 2:]

        qturned, prob_turned, mem_turned, tc = {0: len(k_rows) + 4 + 2}, {}, {}, len(k_rows) + 4 + 2
        hu_idx, hu_st, hu_y, hc = {}, {}, {}, 0
        for n in range(N_SLOT):
            i, slot = divmod(n, A_HEADS)
            if slot == 3 and i < N_TILE:
                tc += 2
                mem_turned[i] = tc
            if slot == 5 and i + 1 < N_TILE:
                tc += 2
                qturned[i + 1] = tc
            if 2 <= n < N_HEAD + 2:
                tc += -(-len(v_tiles((n - 2) // A_HEADS)) // 4)
                prob_turned[n - 2] = tc
            if slot == 5 and i < N_TILE:
                hc += 2
                hu_st[i] = hc
            if slot == 3 and i >= 1:
                hc += 2
                hu_y[i - 1] = hc
            for j, pos in due(n - 1):
                hc += 2
                hu_idx[STEP0[j] + pos] = hc

        N_IN = 16 * 6

        def dcount(i, pos):
            st = stages(i)
            return STEP0[i] - i + pos + 1 - (1 if pos >= st.index("q") else 0)

        with nc.Block() as block:
            @block.sync
            def _(sp):
                def setup(dst, src, s=s_set):
                    sp.dma_start(dst, src, allow_slow_non_contiguous=True).then_inc(s, 16)

                kp_, vp_ = (io[n][0, 0].rearrange("(j p) h d -> p j (h d)", p=P)
                            for n in ("new_k_prompt", "new_v_prompt"))
                setup(k_nat[:, 0:TILE_P, :], kp_, k_set)
                setup(k_nat[:, TILE_P, :], io["cache_k"][0, 0].rearrange("t h d -> t (h d)"), k_set)
                setup(k_nat[0:DEC, TILE_P + 1, :], io["new_k_sample"][0, 0].rearrange("t h d -> t (h d)"), k_set)

                def setup_rest():
                    mems = ("new_mem_k_prompt", "new_mem_v_prompt"), ("cache_mem_k", "cache_mem_v")
                    of_mem = lambda name: io[name][0, 0].rearrange("(j p) h d -> p j (h d)", p=P)
                    for m in range(2):
                        setup(m_nat[:, m, :, :], of_mem(mems[m][0]), mk_set)
                    setup(masks[:], io["c_masks"], mk_set)
                    setup(val[:, 0:TILE_P, :], vp_)
                    setup(val[:, TILE_P, :], io["cache_v"][0, 0].rearrange("t h d -> t (h d)"))
                    setup(val[0:DEC, TILE_P + 1, :], io["new_v_sample"][0, 0].rearrange("t h d -> t (h d)"))
                    for m in range(2):
                        setup(mval[:, m, :, :], of_mem(mems[m][1]))
                    setup(grow[:], io["hgrn_norm_gain"][0].rearrange("h d -> (h d)").partition_broadcast(P))
                    setup(state[1][:], io["state_hgrn"][0, 0].rearrange("h d v -> d h v"))

                def heads_of(t, i):
                    return t[:, i % 2, 0:B_HEADS * rows(i)].rearrange("p (h t) -> p h t", h=B_HEADS)

                def features(d, i):
                    return d[:, row_slice(i)].rearrange("(h p) t -> p h t", p=P)

                def load_q(i):
                    sp.dma_start(q_nat[0:rows(i), i % 2, :], g.d_q[row_slice(i), :]).then_inc(q_in[i % 2], 16)

                def load_first(i):
                    for dst, src in ((heads_of(cum, i), features(g.d_cum, i)), (heads_of(kk, i), features(g.d_kk, i)),
                                     (heads_of(bq, i), features(g.d_bq, i)),
                                     (cq[:, i % 2, :, 0:rows(i)], features(g.d_cq, i))):
                        sp.dma_start(dst, src).then_inc(s_in[i % 2], 16)

                def load_second(i):
                    for dst, src in ((bv, g.d_bi), (bg, g.d_bg)):
                        sp.dma_start(dst[0:rows(i), i % 2, :], src[row_slice(i), :]).then_inc(s_in[i % 2], 16)

                def store_y(n, i, row0, heads):
                    r = rows(i)
                    sp.wait_ge(o_kept, n + 1)
                    src = ysb[:, n % 3, 0:heads * r].rearrange("p (h t) -> p h t", h=heads)
                    dst = g.d_y[row0:row0 + heads * HD, row_slice(i)].rearrange("(h p) t -> p h t", p=P)
                    sp.dma_start(dst, src).then_inc(y_out[n % 3], 16)

                load_q(0)
                load_first(0)
                load_second(0)
                setup_rest()
                load_q(1)
                load_first(1)
                load_second(1)
                for i in range(N_TILE):
                    r = rows(i)
                    if i + 2 < N_TILE:
                        sp.wait_ge(t_kept, qturned[i])
                        load_q(i + 2)
                    store_y(3 * i, i, YC0, C_HEADS)
                    store_y(3 * i + 1, i, 0, GROUP)
                    if i + 2 < N_TILE:
                        sp.wait_ge(w_done, STEP0[i + 1])
                        load_first(i + 2)
                    store_y(3 * i + 2, i, GROUP * HD, GROUP)
                    sp.wait_ge(hp_free, hu_y[i])
                    sp.dma_start(g.d_y[YB0:YC0, row_slice(i)].rearrange("(h p) t -> p h t", p=P),
                                 ybT[:, :, 0:r]).then_inc(yb_out, 16)
                    if i + 2 < N_TILE:
                        load_second(i + 2)
                for j, (name, i) in enumerate((("new_hgrn_prompt", TILE_P - 1), ("new_hgrn_sample", N_TILE - 1))):
                    sp.wait_ge(hp_free, hu_st[i])
                    sp.dma_start(io[name][0, 0].rearrange("h d v -> d h v"), state[j][:]).then_inc(st_out, 16)
                for j in range(3):
                    sp.wait_ge(y_out[j], 16 * N_TILE)
                sp.wait_ge(yb_out, 16 * N_TILE)
                sp.wait_ge(st_out, 32)

            @block.tensor
            def _(pe):
                tu, su, hu, ou = [0], [0], [0], [0]

                def turn(parts):
                    n = tu[0]
                    if n >= 2:
                        pe.wait_ge(t_kept, n - 1)
                    for c, x in parts:
                        kb, m = x.shape
                        last = pe.transpose(g.ps[0:m, 2 + n % 2, c:c + kb], x, g.ident[0:kb, 0:kb])
                    last.then_inc(t_done, 1)
                    tu[0] += 1
                    return last

                def half_unit(make):
                    n = hu[0]
                    if n >= 2:
                        pe.wait_ge(hp_free, n - 1)
                    for h in range(H3):
                        last = make(g.ps[:, 5 + n % 2, h * P:(h + 1) * P], (n % 2) * H3 + h)
                    last.then_inc(hp_done, 1)
                    hu[0] += 1
                    return last

                def q_turn(i):
                    r = rows(i)
                    pe.wait_ge(q_in[i % 2], 16 * (i // 2 + 1))
                    for h0, h1 in ((0, 4), (4, A_HEADS)):
                        turn([((h - h0) * P, q_nat[0:r, i % 2, h * HD:(h + 1) * HD]) for h in range(h0, h1)])

                def scores(n):
                    i, h = divmod(n, A_HEADS)
                    r, k0 = rows(i), 0 if i < TILE_P else SEQ
                    if h == 0:
                        pe.wait_ge(t_kept, qturned[i])
                    for c in range(0, n_keys(i), 512):
                        w = min(512, n_keys(i) - c)
                        if su[0] >= 2:
                            pe.wait_ge(s_masked, su[0] - 1)
                        pe.matmul(g.ps[0:r, su[0] % 2, 0:w], qT[:, i % 2, h, 0:r],
                                  kT[:, h // GROUP, k0 + c:k0 + c + w], start=True, stop=True).then_inc(s_done, 1)
                        su[0] += 1

                def prob_turn(n):
                    i, h = divmod(n, A_HEADS)
                    r, vt = rows(i), v_tiles(i)
                    pe.wait_ge(p_done, n + 1)
                    for b0 in range(0, len(vt), 4):
                        turn([((b - b0) * P, prob[0:r, n % 3, b * P:b * P + vt[b][1]])
                              for b in range(b0, min(b0 + 4, len(vt)))])

                def prob_out(n):
                    i, h = divmod(n, A_HEADS)
                    r, vt = rows(i), v_tiles(i)
                    if h % GROUP == GROUP - 1:
                        kv = h // GROUP
                        pe.wait_ge(t_kept, prob_turned[n])
                        out = g.ps[:, 4, 0:GROUP * r]
                        if ou[0] >= 1:
                            pe.wait_ge(o_kept, ou[0])
                        for b, (vj, kb) in enumerate(vt):
                            last = pe.matmul(out, val[0:kb, vj, kv * HD:(kv + 1) * HD],
                                             pT[0:kb, b, kv * GROUP:(kv + 1) * GROUP, 0:r],
                                             start=(b == 0), stop=(b == len(vt) - 1))
                        last.then_inc(o_done, 1)
                        ou[0] += 1

                def mem_scores(i, pair):
                    r, m = rows(i), 0 if i < TILE_P else 1
                    pe.wait_ge(s_in[i % 2], N_IN * (i // 2 + 1))
                    if 2 * i + pair >= 1:
                        pe.wait_ge(c_exp, 2 * i + pair)
                    for e in range(2):
                        last = pe.matmul(g.ps[0:r, 7, e * N_MEM:(e + 1) * N_MEM], cq[:, i % 2, 2 * pair + e, 0:r],
                                         mkT[:, m, 2 * pair + e, :], start=True, stop=True)
                    last.then_inc(c_done, 1)

                def mem_turn(i):
                    r = rows(i)
                    pe.wait_ge(c_norm, i + 1)
                    for pair in range(2):
                        turn([((2 * e + b) * P, cp[0:r, 2 * pair + e, b * P:(b + 1) * P])
                              for e in range(2) for b in range(2)])

                def mem_out(i):
                    r, m = rows(i), 0 if i < TILE_P else 1
                    pe.wait_ge(t_kept, mem_turned[i])
                    if ou[0] >= 1:
                        pe.wait_ge(o_kept, ou[0])
                    for h in range(C_HEADS):
                        for b in range(2):
                            last = pe.matmul(g.ps[:, 4, h * r:(h + 1) * r], mval[:, m, b, h * HD:(h + 1) * HD],
                                             cpT[:, h, b, 0:r], start=(b == 0), stop=(b == 1))
                    last.then_inc(o_done, 1)
                    ou[0] += 1

                def recur_step(i, pos):
                    t, idx, kind = rows(i), STEP0[i] + pos, stages(i)[pos]
                    st, par = state[i // TILE_P], (STEP0[i] + pos) % 2
                    w = lambda h: wk[:, par, h * t:(h + 1) * t]
                    pe.wait_ge(w_done, idx + 1)
                    if kind == "q":
                        pe.wait_ge(hp_free, hu[0])
                        pe.wait_ge(s_cleared, 1)
                        def make(out, h):
                            last = pe.matmul(out[0:t], smat[0:t, h, 0:t], bv[0:t, i % 2, h * HD:(h + 1) * HD],
                                             start=True, stop=(i == 0))
                            if i:
                                last = pe.matmul(out[0:t], w(h), st[:, h, :], start=False, stop=True)
                            return last
                    elif kind == "k":
                        make = lambda out, h: pe.transpose(out[0:t], w(h), g.ident[:])
                    elif kind == 1:
                        make = lambda out, h: pe.matmul(out[0:t, 0:t], kp[:, h * t:(h + 1) * t], w(h), start=True, stop=True)
                    else:
                        make = lambda out, h: pe.matmul(out[0:t, 0:t], w(h), w(h), start=True, stop=True)
                    half_unit(make)
                    half_unit(make)

                def recur_state(i):
                    t = rows(i)
                    pe.wait_ge(hp_free, hu[0])
                    make = lambda out, h: pe.matmul(out, kdT[0:t, h * HD:(h + 1) * HD],
                                                    bv[0:t, i % 2, h * HD:(h + 1) * HD], start=True, stop=True)
                    half_unit(make)
                    half_unit(make)

                def recur_out(i):
                    t = rows(i)
                    pe.wait_ge(y_done, i + 1)
                    make = lambda out, h: pe.transpose(out[:, 0:t], osb[0:t, h * HD:(h + 1) * HD], g.ident[0:t, 0:t])
                    half_unit(make)
                    half_unit(make)

                pe.wait_ge(k_set, 16 * 3)
                for j, kb, _ in k_rows:
                    turn([(kv * P, k_nat[0:kb, j, kv * HD:(kv + 1) * HD]) for kv in range(A_KV)])
                q_turn(0)
                pe.wait_ge(mk_set, 16 * 3)
                for m in range(2):
                    for j in range(N_MEM // P):
                        turn([(h * P, m_nat[:, m, j, h * HD:(h + 1) * HD]) for h in range(C_HEADS)])
                for n in range(N_SLOT):
                    i, slot = divmod(n, A_HEADS)
                    if n < N_HEAD:
                        scores(n)
                    if slot == 5 and i < N_TILE:
                        recur_state(i)
                    if slot == 3 and i >= 1:
                        recur_out(i - 1)
                    early, late = halves(n - 1)
                    if n == 3:
                        pe.wait_ge(s_set, N_SET)
                    if slot == 1 and i < N_TILE:
                        mem_scores(i, 0)
                    if slot == 2 and i < N_TILE:
                        mem_scores(i, 1)
                    if 3 <= n < N_HEAD + 3:
                        prob_out(n - 3)
                    if slot == 4 and i < N_TILE:
                        mem_out(i)
                    for j, pos in early:
                        recur_step(j, pos)
                    if slot == 3 and i < N_TILE:
                        mem_turn(i)
                    if slot == 5 and i + 1 < N_TILE:
                        q_turn(i + 1)
                    if 2 <= n < N_HEAD + 2:
                        prob_turn(n - 2)
                    for j, pos in late:
                        recur_step(j, pos)

            @block.scalar
            def _(act):
                tu = [0]

                def keep(copies):
                    act.wait_ge(t_done, tu[0] + 1)
                    for dst, src in copies(g.ps[:, 2 + tu[0] % 2, :]):
                        last = S.activation(dst, src, ACT.Copy)
                    last.then_inc(t_kept, 1)
                    tu[0] += 1

                def q_keep(i):
                    r = rows(i)
                    for h0, h1 in ((0, 4), (4, A_HEADS)):
                        keep(lambda b: [(qT[:, i % 2, h0:h1, 0:r],
                                         b.rearrange("p (h t) -> p h t", t=P)[:, 0:h1 - h0, 0:r])])

                def prob_keep(n):
                    i, h = divmod(n, A_HEADS)
                    r, vt, kv = rows(i), v_tiles(i), h // GROUP
                    if i >= 1:
                        act.wait_ge(o_done, 3 * (i - 1) + 2 + kv)
                    for b0 in range(0, len(vt), 4):
                        bl = range(b0, min(b0 + 4, len(vt)))
                        if all(vt[b][1] == P for b in bl):
                            keep(lambda bank: [(pT[:, b0:b0 + len(bl), h, 0:r],
                                                bank.rearrange("p (b t) -> p b t", t=P)[:, 0:len(bl), 0:r])])
                        else:
                            keep(lambda bank: [(pT[0:vt[b][1], b, h, 0:r],
                                                bank[0:vt[b][1], (b - b0) * P:(b - b0) * P + r]) for b in bl])

                def mem_exp(i, pair):
                    r = rows(i)
                    act.wait_ge(c_top, 2 * i + pair + 1)
                    for h in (2 * pair, 2 * pair + 1):
                        last = S.activation(cp[0:r, h, :], g.ps[0:r, 7, (h % 2) * N_MEM:(h % 2 + 1) * N_MEM],
                                            ACT.Exp, bias=ctop[0:r, h:h + 1], scale=SCALE,
                                            accum_out=cden[0:r, h:h + 1])
                    last.then_inc(c_exp, 1)

                def recur_exp(i, pos):
                    t, idx, kind = rows(i), STEP0[i] + pos, stages(i)[pos]
                    w = B_HEADS * t
                    if kind != "q":
                        act.wait_ge(d_done, dcount(i, pos))
                    if idx >= 2:
                        act.wait_ge(w_done, idx - 1)
                    dst = ex[:, idx % 2, 0:w]
                    if kind == "q":
                        b = cum[:, i % 2, 0:w]
                        c3 = b.rearrange("p (h t) -> p h t", h=B_HEADS)
                        if i >= 1:
                            act.wait_ge(hp_free, hu_st[i - 1])
                        S.activation(eb[:, :], c3[:, :, t - 1], ACT.Exp)
                        S.activation(dst, b, ACT.Exp).then_inc(x_done, 1)
                    elif kind == 1:
                        S.activation(exn[:, 0:w], dif[:, idx % 2, 0:w], ACT.Exp, scale=-1.0)
                        S.activation(dst, dif[:, idx % 2, 0:w], ACT.Exp).then_inc(x_done, 1)
                    else:
                        S.activation(dst, dif[:, idx % 2, 0:w], ACT.Exp).then_inc(x_done, 1)

                for j, kb, c0 in k_rows:
                    keep(lambda b: [(kT[:, :, c0:c0 + kb], b.rearrange("p (h t) -> p h t", t=P)[:, 0:A_KV, 0:kb])])
                q_keep(0)
                for m in range(2):
                    for j in range(N_MEM // P):
                        keep(lambda b: [(mkT[:, m, :, j * P:(j + 1) * P], b.rearrange("p (h t) -> p h t", t=P))])
                recur_exp(0, 0)
                for n in range(N_SLOT):
                    i, slot = divmod(n, A_HEADS)
                    if n < N_HEAD:
                        r, w = rows(i), n_keys(i)
                        act.wait_ge(ntop_ok, n + 1)
                        if n >= 8:
                            act.wait_ge(p_done, n - 7)
                        S.activation(prob[0:r, n % 3, 0:w], prob[0:r, n % 3, 0:w], ACT.Exp, bias=ntop[0:r, n % 8:n % 8 + 1],
                                     scale=1.0, accum_out=den[0:r, n % 8:n % 8 + 1]).then_inc(e_done, 1)
                    if slot in (1, 2) and i < N_TILE:
                        mem_exp(i, slot - 1)
                    for j, pos in due(n):
                        recur_exp(j, pos)
                    if slot == 5 and i < N_TILE:
                        t = rows(i)
                        act.wait_ge(hp_free, hu_idx[STEP0[i] + stages(i).index("q")])
                        if i >= 1:
                            act.wait_ge(ms_done, i)
                        S.activation(sq[0:t, :], osb[0:t, :], ACT.Square, scale=float(HD) ** -0.5).then_inc(sq_done, 1)
                    if slot == 3 and i < N_TILE:
                        r = rows(i)
                        if i >= 1:
                            act.wait_ge(o_done, 3 * (i - 1) + 1)
                        for pair in range(2):
                            keep(lambda b: [(cpT[:, 2 * pair:2 * pair + 2, :, 0:r],
                                             b.rearrange("p (h b t) -> p h b t", h=2, b=2)[:, :, :, 0:r])])
                    if slot == 5 and i + 1 < N_TILE:
                        q_keep(i + 1)
                    if 2 <= n < N_HEAD + 2:
                        prob_keep(n - 2)
                    if slot == 0 and i >= 1:
                        act.wait_ge(rs_done, 2 * i)
                        for h in range(B_HEADS):
                            o = osb[0:rows(i - 1), h * HD:(h + 1) * HD]
                            last = S.activation(o, o, ACT.Copy, scale=ms[0:rows(i - 1), h:h + 1])
                        last.then_inc(o_normed, 1)
            @block.gpsimd
            def _(pool):
                G.memset(expo[:], -0.5)
                G.memset(smat[:], 0.0).then_inc(s_cleared, 1)
                def recur_scale(i, pos):
                    w, j = B_HEADS * rows(i), i % 2
                    idx, kind = STEP0[i] + pos, stages(i)[pos]
                    e, o = ex[:, idx % 2, 0:w], wk[:, idx % 2, 0:w]
                    q, k_ = bq[:, j, 0:w], kk[:, j, 0:w]
                    pool.wait_ge(s_in[j], N_IN * (i // 2 + 1))
                    pool.wait_ge(x_done, idx + 1)
                    if idx >= 2:
                        pool.wait_ge(hp_done, hu_idx[idx - 2])
                    if kind == 1:
                        G.tensor_tensor(kp[:, 0:w], k_, exn[:, 0:w], ALU.mult)
                        G.tensor_tensor(o, q, e, ALU.mult).then_inc(w_done, 1)
                    elif kind == "q":
                        G.tensor_tensor(o, q, e, ALU.mult).then_inc(w_done, 1)
                    elif kind == "k":
                        G.tensor_tensor(o, k_, e, ALU.mult).then_inc(w_done, 1)
                    else:
                        blk = lambda x: x.rearrange("p (b t) -> p b t", t=2 * kind)
                        G.tensor_tensor(blk(o)[:, :, 0:kind], blk(k_)[:, :, 0:kind], blk(e)[:, :, 0:kind], ALU.mult)
                        G.tensor_tensor(blk(o)[:, :, kind:], blk(q)[:, :, kind:],
                                        blk(e)[:, :, kind:], ALU.mult).then_inc(w_done, 1)

                recur_scale(0, 0)
                for n in range(N_SLOT):
                    i, slot = divmod(n, A_HEADS)
                    j = i % 2
                    for step in due(n):
                        recur_scale(*step)
                    if slot == 4 and i < N_TILE:
                        t = rows(i)
                        if i == 0:
                            pool.wait_ge(s_set, N_SET)
                        G.tensor_tensor(bg[0:t, j, :], bg[0:t, j, :], grow[0:t, :], ALU.mult).then_inc(gg_done, 1)
                    if slot == 0 and i >= 1:
                        m = ms[0:rows(i - 1), :]
                        pool.wait_ge(ms_done, i)
                        G.tensor_scalar(m, m, EPS, None, ALU.add).then_inc(rs_done, 1)
                        pool.wait_ge(rs_done, 2 * i - 1)
                        G.tensor_tensor(m, m, expo[0:rows(i - 1), :], ALU.pow).then_inc(rs_done, 1)
                    if slot == 1 and i >= 1:
                        o = osb[0:rows(i - 1), :]
                        pool.wait_ge(o_normed, i)
                        pool.wait_ge(gg_done, i)
                        G.tensor_tensor(o, o, bg[0:rows(i - 1), (i - 1) % 2, :], ALU.mult).then_inc(y_done, 1)

            @block.vector
            def _(dve):
                su, hu, ou = [0], [0], [0]
                steps = [0]

                def link(ins):
                    steps[0] += 1
                    ins.then_inc(s_step, 1)
                    dve.wait_ge(s_step, steps[0])

                def half_unit():
                    n = hu[0]
                    dve.wait_ge(hp_done, n + 1)
                    hu[0] += 1
                    return g.ps[:, 5 + n % 2, 0:H3 * P].rearrange("p (h t) -> p h t", h=H3), (n % 2) * H3

                def mask_scores(n):
                    i, h = divmod(n, A_HEADS)
                    r, w = rows(i), n_keys(i)
                    if n >= 3:
                        dve.wait_ge(t_done, prob_turned[n - 3])
                    if n >= 8:
                        dve.wait_ge(e_done, n - 7)
                    tp = top[0:r, n % 8:n % 8 + 1]
                    for c in range(0, w, 512):
                        cw = min(512, w - c)
                        dve.wait_ge(s_done, su[0] + 1)
                        acc = part[0:r, :] if c + cw < w else tp
                        ins = V.tensor_tensor_reduce(prob[0:r, n % 3, c:c + cw], g.ps[0:r, su[0] % 2, 0:cw],
                                                     g.bias[0:r, BIAS_OFF[i] + c:BIAS_OFF[i] + c + cw], SCALE,
                                                     NEG if c == 0 else part[0:r, :], ALU.add, ALU.max, acc)
                        ins.then_inc(s_masked, 1)
                        su[0] += 1
                        dve.wait_ge(s_masked, su[0])
                    V.tensor_scalar(ntop[0:r, n % 8:n % 8 + 1], tp, -1.0, None, ALU.mult).then_inc(ntop_ok, 1)

                def normalise(n):
                    i = n // A_HEADS
                    r, w, d = rows(i), n_keys(i), den[0:rows(i), n % 8:n % 8 + 1]
                    dve.wait_ge(e_done, n + 1)
                    link(V.reciprocal(d, d))
                    V.tensor_scalar(prob[0:r, n % 3, 0:w], prob[0:r, n % 3, 0:w], d, None, ALU.mult).then_inc(p_done, 1)

                def keep_out(w):
                    n = ou[0]
                    dve.wait_ge(o_done, n + 1)
                    if n >= 3:
                        dve.wait_ge(y_out[n % 3], 16 * (n // 3))
                    V.tensor_copy(ysb[:, n % 3, 0:w], g.ps[:, 4, 0:w]).then_inc(o_kept, 1)
                    ou[0] += 1

                def mem_top(i, pair):
                    r, hs = rows(i), slice(2 * pair, 2 * pair + 2)
                    dve.wait_ge(c_done, 2 * i + pair + 1)
                    link(V.tensor_reduce(ctop[0:r, hs], g.ps[0:r, 7, :].rearrange("p (h m) -> p h m", h=2),
                                         AX.X, ALU.max))
                    V.tensor_scalar(ctop[0:r, hs], ctop[0:r, hs], -SCALE, None, ALU.mult).then_inc(c_top, 1)

                def recur_diff(i, pos):
                    t, idx, kind = rows(i), STEP0[i] + pos, stages(i)[pos]
                    w = B_HEADS * t
                    if kind == "q":
                        return
                    if pos == 0:
                        dve.wait_ge(s_in[i % 2], N_IN * (i // 2 + 1))
                    if idx >= 2:
                        dve.wait_ge(x_done, idx - 1)
                    b, d = cum[:, i % 2, 0:w], dif[:, idx % 2, 0:w]
                    if kind == "k":
                        b3, d3 = (x.rearrange("p (h t) -> p h t", h=B_HEADS) for x in (b, d))
                        V.tensor_tensor(d3, b3[:, :, t - 1:t].to_broadcast([P, B_HEADS, t]), b3,
                                        ALU.subtract).then_inc(d_done, 1)
                        return
                    b3, d3 = (x.rearrange("p (b t) -> p b t", t=2 * kind) for x in (b, d))
                    nb = w // (2 * kind)
                    ref = b3[:, :, kind - 1:kind]
                    if kind == 1:
                        V.tensor_tensor(d3, b3, ref.to_broadcast([P, nb, 2]), ALU.subtract).then_inc(d_done, 1)
                    else:
                        ref = ref.to_broadcast([P, nb, kind])
                        V.tensor_tensor(d3[:, :, 0:kind], ref, b3[:, :, 0:kind], ALU.subtract)
                        V.tensor_tensor(d3[:, :, kind:], b3[:, :, kind:], ref, ALU.subtract).then_inc(d_done, 1)

                def recur_keep(i, pos):
                    t, kind = rows(i), stages(i)[pos]
                    if pos == 0:
                        dve.wait_ge(s_cleared, 1)
                        dve.wait_ge(mk_set, 16 * 3)
                    if kind == "q" and i >= 1:
                        dve.wait_ge(y_done, i)
                        dve.wait_ge(hp_free, hu[0])
                    for _ in range(2):
                        bank, h0 = half_unit()
                        if kind == "q":
                            dst = osb[0:t, h0 * HD:(h0 + H3) * HD].rearrange("p (h d) -> p h d", h=H3)
                            last = V.tensor_copy(dst, bank[0:t])
                        elif kind == "k":
                            dst = kdT[0:t, h0 * HD:(h0 + H3) * HD].rearrange("p (h d) -> p h d", h=H3)
                            last = V.tensor_copy(dst, bank[0:t])
                        else:
                            m = bcast_mid(masks[0:t, LEVELS.index(kind), 0:t], H3)
                            last = V.copy_predicated(smat[0:t, h0:h0 + H3, 0:t], m, bank[0:t, :, 0:t])
                        last.then_inc(hp_free, 1)

                recur_diff(0, 0)
                for n in range(N_SLOT):
                    i, slot = divmod(n, A_HEADS)
                    if n < N_HEAD:
                        mask_scores(n)
                    if slot == 3 and i >= 1:
                        t = rows(i - 1)
                        if i >= 2:
                            dve.wait_ge(yb_out, 16 * (i - 1))
                        for _ in range(2):
                            bank, h0 = half_unit()
                            V.tensor_copy(ybT[:, h0:h0 + H3, 0:t], bank[:, :, 0:t]).then_inc(hp_free, 1)
                    early, late = halves(n - 1)
                    if slot in (1, 2) and i < N_TILE:
                        mem_top(i, slot - 1)
                    for j, pos in due(n):
                        recur_diff(j, pos)
                    if slot == 5 and i < N_TILE:
                        st = state[i // TILE_P]
                        for _ in range(2):
                            bank, h0 = half_unit()
                            for h in range(H3):
                                if i == 0:
                                    last = V.tensor_copy(st[:, h0 + h, :], bank[:, h, :])
                                else:
                                    last = V.scalar_tensor_tensor(
                                        out=st[:, h0 + h, :], in0=st[:, h0 + h, :], scalar=eb[:, h0 + h:h0 + h + 1],
                                        in1=bank[:, h, :], op0=ALU.mult, op1=ALU.add)
                            last.then_inc(hp_free, 1)
                    if 1 <= n <= N_HEAD:
                        normalise(n - 1)
                    if 3 <= n < N_HEAD + 3 and (n - 3) % GROUP == GROUP - 1:
                        keep_out(GROUP * rows((n - 3) // A_HEADS))
                    if slot == 4 and i < N_TILE:
                        keep_out(C_HEADS * rows(i))
                    for j, pos in early:
                        recur_keep(j, pos)
                    if slot == 2 and i < N_TILE:
                        r = rows(i)
                        dve.wait_ge(c_exp, 2 * i + 2)
                        link(V.reciprocal(cden[0:r, :], cden[0:r, :]))
                        V.tensor_tensor(cp[0:r], cp[0:r], bcast(cden[0:r, :], N_MEM), ALU.mult).then_inc(c_norm, 1)
                    if slot == 5 and i < N_TILE:
                        t = rows(i)
                        dve.wait_ge(sq_done, i + 1)
                        V.tensor_reduce(ms[0:t, :], sq[0:t, :].rearrange("p (h d) -> p h d", h=B_HEADS),
                                        AX.X, ALU.add).then_inc(ms_done, 1)
                    for j, pos in late:
                        recur_keep(j, pos)



BRANCHES = [("w_out_c", YC0, C_HEADS, 2), ("w_out_a", 0, A_HEADS, 0), ("w_out_b", YB0, B_HEADS, 1)]


def block_gate_merge(g):
    nc, io = g.nc, g.io
    n0 = g.slab
    slabs = [(b, j) for b in range(3) for j in range(D_MODEL // 256)]
    g.slab += len(slabs)
    units = [(s, b, 2 * j + ft, c0, n) for s, (b, j) in enumerate(slabs) for c0, n in GROUPS for ft in range(2)]
    per_branch = len(units) // 3
    pieces = [(b, half * (BRANCHES[b][2] // 2), c0, n) for b in range(3) for c0, n in GROUPS for half in range(2)]
    per_pieces = len(pieces) // 3
    NB, NG = 4, 4
    early = {0: (0, 4), 2: (4, 6)}
    with ExitStack() as ctx:
        sb = lambda name, shape, dt=F32: ctx.enter_context(nc.sbuf_tensor("gm_" + name, shape, dt))
        y_hi, y_lo = sb("y_hi", [P, 2, A_HEADS, T_ALL], F32R), sb("y_lo", [P, 2, A_HEADS, T_ALL], F32R)
        y_raw, gate, tmp = sb("y_raw", [P, 2, A_HEADS // 2 * 384]), sb("gate", [P, NG, 384]), sb("tmp", [P, 384])
        sem = lambda name: g.sem("gm_" + name)
        y_in, hi_done, lo_done = [sem("y_in0"), sem("y_in1")], sem("hi"), sem("lo")
        gate_in = [sem(f"gate_in{j}") for j in range(NG)]
        full, gated, summed = sem("full"), sem("gated"), sem("summed")

        def piece(m):
            b, k0, c0, n = pieces[m]
            nk = BRANCHES[b][2] // 2
            raw = y_raw[:, m % 2, 0:nk * n].rearrange("p (k t) -> p k t", k=nk)
            return raw, y_hi[:, b % 2, k0:k0 + nk, c0:c0 + n], y_lo[:, b % 2, k0:k0 + nk, c0:c0 + n]

        def after(u):
            b = u // per_branch
            return per_pieces * (b + 1) + u % per_branch // 4 if u % 4 == 3 and b < 2 else None

        with nc.Block() as block:
            @block.sync
            def _(sp):
                def load_piece(m):
                    b, k0, c0, n = pieces[m]
                    nk, row = BRANCHES[b][2] // 2, BRANCHES[b][1] + k0 * P
                    if m >= 2:
                        sp.wait_ge(lo_done, m - 1)
                    sp.dma_start(piece(m)[0], g.d_y[row:row + nk * P, c0:c0 + n].rearrange("(k p) t -> p k t", p=P)
                                 ).then_inc(y_in[m % 2], 16)

                def load_weights(s):
                    b, j = slabs[s]
                    load_slab(g, sp, n0 + s, w_cols(io[BRANCHES[b][0]][0], j * 256, 256), BRANCHES[b][2])

                def load_gate(u):
                    s, b, f, c0, n = units[u]
                    if u >= NG:
                        sp.wait_ge(gated, u - NG + 1)
                    row = BRANCHES[b][3] * D_MODEL + f * P
                    sp.dma_start(gate[:, u % NG, 0:n], g.d_gate[row:row + P, c0:c0 + n]).then_inc(gate_in[u % NG], 16)

                load_weights(0)
                load_piece(0)
                load_piece(1)
                load_gate(0)
                load_gate(1)
                load_piece(2)
                load_weights(1)
                for m in range(3, per_pieces):
                    load_piece(m)
                for u in range(2, len(units)):
                    load_gate(u)
                    if after(u) is not None:
                        load_piece(after(u))
                    s = u // 6
                    if u % 6 == 2 and s + 2 < len(slabs):
                        load_weights(s + 2)
                    elif u % 6 == 2:
                        load_out(g, sp, s + 2 - len(slabs), n0 + s + 2)

            @block.gpsimd
            def _(pool):
                for s, (b, j) in enumerate(slabs):
                    split_slab(g, pool, n0 + s, BRANCHES[b][2] * 256)
                split_slab(g, pool, n0 + len(slabs), SLAB)

            @block.scalar
            def _(act):
                def split(m):
                    raw, hi, _ = piece(m)
                    act.wait_ge(y_in[m % 2], 16 * (m // 2 + 1))
                    nc.scalar.activation(hi, raw, ACT.Copy).then_inc(hi_done, 1)

                round_slab(g, act, n0, BRANCHES[0][2] * 256)
                for m in range(per_pieces):
                    split(m)
                    if m == 2:
                        round_slab(g, act, n0 + 1, BRANCHES[0][2] * 256)
                for u, (s, b, f, c0, n) in enumerate(units):
                    if u % 6 == 0 and u >= 6:
                        act.wait_ge(full, u)
                        size = BRANCHES[slabs[s + 1][0]][2] * 256 if s + 1 < len(slabs) else SLAB
                        round_slab(g, act, n0 + s + 1, size)
                    if after(u) is not None:
                        act.wait_ge(full, u + 1)
                        split(after(u))

            @block.tensor
            def _(pe):
                for u, (s, b, f, c0, n) in enumerate(units):
                    kt = BRANCHES[b][2]
                    if b == 0:
                        pe.wait_ge(lo_done, min(per_pieces, u % 6 // 2 * 2 + 2) if u < 6 else per_pieces)
                    elif u % per_branch == 0:
                        pe.wait_ge(lo_done, (b + 1) * per_pieces)
                    if u % 6 == 0:
                        pe.wait_ge(g.w_split, n0 + s + 1)
                    if u >= NB:
                        pe.wait_ge(gated, u - NB + 1)
                    w, y = slab_view(g, n0 + s, kt, 256), (y_hi, y_lo)
                    fs, cs = slice((f % 2) * P, (f % 2 + 1) * P), slice(c0, c0 + n)
                    three_products(pe, g.ps[:, u % NB, 0:n], lambda a, k: w[a][:, k, fs],
                                   lambda a, k: y[a][:, b % 2, k, cs], kt).then_inc(full, 1)

            @block.vector
            def _(dve):
                def split(m):
                    raw, hi, lo = piece(m)
                    dve.wait_ge(hi_done, m + 1)
                    nc.vector.tensor_tensor(lo, raw, hi.bitcast(F32), ALU.subtract).then_inc(lo_done, 1)

                for u, (s, b, f, c0, n) in enumerate(units):
                    for m in range(*early.get(u, (0, 0))):
                        split(m)
                    dve.wait_ge(full, u + 1)
                    dve.wait_ge(gate_in[u % NG], 16 * (u // NG + 1))
                    dst, ps, gt = g.merged[:, f, c0:c0 + n], g.ps[:, u % NB, 0:n], gate[:, u % NG, 0:n]
                    if b == 0:
                        nc.vector.tensor_tensor(dst, ps, gt, ALU.mult).then_inc(gated, 1)
                    else:
                        if u > per_branch:
                            dve.wait_ge(summed, u - per_branch)
                        nc.vector.tensor_tensor(tmp[:, 0:n], ps, gt, ALU.mult).then_inc(gated, 1)
                        dve.wait_ge(gated, u + 1)
                        nc.vector.tensor_tensor(dst, dst, tmp[:, 0:n], ALU.add).then_inc(summed, 1)
                    if after(u) is not None:
                        split(after(u))



def token_srcs(io):
    return [io["x_prompt"][0, i * P:(i + 1) * P, :] for i in range(TILE_P)] + [io["x_sample"][0]]


def load_out(g, sp, s, n):
    load_slab(g, sp, n, w_cols(g.io["w_out"][0], s * 256, 256), KT)


def load_up(g, sp, s, n):
    load_slab(g, sp, n, w_cols(g.io["w_up"][0], s * 256, 256), KT)


def block_out(g):
    nc, io = g.nc, g.io
    n0 = g.slab
    NSL = D_MODEL // 256
    g.slab += NSL
    NB = 4
    units = [(s, i) for s in range(NSL) for i in range(N_TILE)]
    spare = lambda k: g.big[:, k * D_MODEL:(k + 1) * D_MODEL]
    NX = 3
    xin, x2, junk, junk2 = [spare(j) for j in range(NX)], [spare(NX + j) for j in range(NX)], spare(6), spare(7)
    turns = [(gr, k) for gr in range(len(GROUPS)) for k in range(KT)]
    turn_after = {7: [0], N_TILE - 1: [1, 2]}
    split_parts = [(slice(k0, k0 + KT // 2), slice(c0, c0 + n)) for c0, n in GROUPS for k0 in (0, KT // 2)]
    N_PARTS = len(split_parts)
    with ExitStack() as ctx:
        sb = lambda name, shape: ctx.enter_context(nc.sbuf_tensor("out_" + name, shape, F32))
        o_all, gain = sb("o_all", [P, N_TILE, D_MODEL]), sb("gain", [P, D_MODEL])
        parts, ss, s2, expo = sb("parts", [P, N_TILE, NSL]), sb("ss", [P, N_TILE]), sb("s2", [P, N_TILE]), sb("expo", [P, 1])
        sem = lambda name: g.sem("out_" + name)
        hi_done, lo_done, full, kept, squared = sem("hi"), sem("lo"), sem("full"), sem("kept"), sem("squared")
        gain_in, x_in, x2_out = sem("gain_in"), [sem(f"x_in{j}") for j in range(NX)], [sem(f"x2_out{j}") for j in range(NX)]
        sum1, r1, x2_done, sq2, r2, n2 = (sem(n) for n in ("sum1", "r1", "x2_done", "sq2", "r2", "n2"))
        t_done, t_hi, t_lo, zeroed = sem("t_done"), sem("t_hi"), sem("t_lo"), sem("zeroed")
        srcs = token_srcs(io)

        def group_turns(i):
            return [v for v, (gr, _) in enumerate(turns) if gr in turn_after.get(i, [])]

        def turned(v):
            gr, k = turns[v]
            c0, n = GROUPS[gr]
            return k, c0, n, g.ps[:, 4 + v % 4, 0:n]

        with nc.Block() as block:
            def store(sp, i):
                sp.wait_ge(x2_done, i + 1)
                sp.dma_start(g.d_x2[row_slice(i), :], x2[i % NX][0:rows(i), :]).then_inc(x2_out[i % NX], 16)

            @block.sync
            def _(sp):
                sp.dma_start(gain[:], io["post_mix_gain"][0].partition_broadcast(P)).then_inc(gain_in, 16)
                for s in range(2, NSL):
                    load_out(g, sp, s, n0 + s)
                sp.wait_ge(lo_done, N_PARTS)
                for i in range(N_TILE):
                    r = rows(i)
                    if i == NX:
                        for s in range(2):
                            load_up(g, sp, s, n0 + NSL + s)
                    if i >= NX:
                        store(sp, i - NX)
                    sp.dma_start(xin[i % NX][0:r, :], srcs[i]).then_inc(x_in[i % NX], 16)
                for i in range(N_TILE - NX, N_TILE):
                    store(sp, i)
                for j in range(NX):
                    sp.wait_ge(x2_out[j], 16 * len(range(j, N_TILE, NX)))

            @block.gpsimd
            def _(pool):
                G = nc.gpsimd
                G.memset(expo[:], -0.5).then_inc(zeroed, 1)
                pool.wait_ge(zeroed, 3)
                for s in range(1, NSL + 1):
                    split_slab(g, pool, n0 + s, SLAB)

                def inverse_root(v, counter, done):
                    G.tensor_scalar(v, v, 1.0 / D_MODEL, EPS, ALU.mult, ALU.add).then_inc(counter, 1)
                    pool.wait_ge(counter, 2 * done + 1)
                    G.tensor_tensor(v, v, expo[0:v.shape[0], :], ALU.pow).then_inc(counter, 1)

                for j in range(N_TILE + 2):
                    if j < N_TILE:
                        pool.wait_ge(sum1, j + 1)
                        inverse_root(ss[0:rows(j), j:j + 1], r1, j)
                    if j >= 2:
                        i, r = j - 2, rows(j - 2)
                        pool.wait_ge(sq2, i + 1)
                        inverse_root(s2[0:r, i:i + 1], r2, i)

            @block.scalar
            def _(act):
                def second_square(i):
                    r = rows(i)
                    act.wait_ge(x2_done, i + 1)
                    if i:
                        act.wait_ge(sq2, i)
                    nc.scalar.activation(junk2[0:r, :], x2[i % NX][0:r, :], ACT.Square,
                                         accum_out=s2[0:r, i:i + 1]).then_inc(sq2, 1)

                for ks, cs in split_parts:
                    nc.scalar.activation(g.h_hi[:, ks, cs], g.merged[:, ks, cs], ACT.Copy).then_inc(hi_done, 1)
                act.wait_ge(lo_done, N_PARTS)
                for u, (s, i) in enumerate(units):
                    r = rows(i)
                    if i == 0:
                        if s:
                            act.wait_ge(full, u)
                        round_slab(g, act, n0 + s + 1, SLAB)
                    act.wait_ge(full, u + 1)
                    if u >= 4:
                        act.wait_ge(squared, u - 3)
                    nc.scalar.activation(junk[0:r, u % 4 * 256:(u % 4 + 1) * 256], g.ps[0:r, u % NB, 0:256], ACT.Square,
                                         accum_out=parts[0:r, i, s:s + 1]).then_inc(squared, 1)
                    if s < NSL - 1:
                        continue
                    for j in [i - 2] if i < N_TILE - 1 else [i - 2, i - 1, i]:
                        if j >= 0:
                            second_square(j)
                    for v in group_turns(i):
                        k, c0, n, bank = turned(v)
                        act.wait_ge(t_done, v + 1)
                        nc.scalar.activation(g.h_hi[:, k, c0:c0 + n], bank, ACT.Copy,
                                             scale=g.gains[:, 2, k:k + 1]).then_inc(t_hi, 1)

            @block.tensor
            def _(pe):
                pe.wait_ge(zeroed, 3)
                x = (g.h_hi, g.h_lo)
                for u, (s, i) in enumerate(units):
                    if s == 0 and i * P in [c0 for c0, _ in GROUPS]:
                        pe.wait_ge(lo_done, 2 * (i * P // GROUPS[0][1] + 1))
                    if i == 0:
                        pe.wait_ge(g.w_split, n0 + s + 1)
                    if u >= NB:
                        pe.wait_ge(kept, u - NB + 1)
                    w, c = slab_view(g, n0 + s, KT, 256), slice(i * P, (i + 1) * P)
                    three_products(pe, g.ps[:, u % NB, 0:256], lambda a, k: x[a][:, k, c],
                                   lambda b, k: w[b][:, k, :], KT).then_inc(full, 1)
                    if s < NSL - 1:
                        continue
                    for v in group_turns(i):
                        k, c0, n, bank = turned(v)
                        if k == 0:
                            pe.wait_ge(n2, -(-(c0 + n) // P))
                        if v >= 4:
                            pe.wait_ge(t_lo, v - 3)
                        for j in range(-(-n // P)):
                            q = c0 // P + j
                            last = pe.transpose(bank[:, j * P:j * P + rows(q)], o_all[0:rows(q), q, k * P:(k + 1) * P],
                                                g.ident[0:rows(q), 0:rows(q)])
                        last.then_inc(t_done, 1)

            @block.vector
            def _(dve):
                V = nc.vector

                def new_x(i):
                    r = rows(i)
                    dve.wait_ge(r1, 2 * i + 2)
                    dve.wait_ge(x_in[i % NX], 16 * (i // NX + 1))
                    if i >= NX:
                        dve.wait_ge(x2_out[i % NX], 16 * (i // NX))
                        dve.wait_ge(n2, i - NX + 1)
                    V.scalar_tensor_tensor(out=x2[i % NX][0:r, :], in0=o_all[0:r, i, :], scalar=ss[0:r, i:i + 1],
                                           in1=xin[i % NX][0:r, :], op0=ALU.mult, op1=ALU.add).then_inc(x2_done, 1)

                def second_norm(i):
                    r = rows(i)
                    dve.wait_ge(r2, 2 * i + 2)
                    V.tensor_scalar(o_all[0:r, i, :], x2[i % NX][0:r, :], s2[0:r, i:i + 1], None, ALU.mult).then_inc(n2, 1)

                for t in (g.h_hi, g.h_lo):
                    V.memset(t[:, :, T_ALL:T_PAD].bitcast(F32), 0.0).then_inc(zeroed, 1)
                for m, (ks, cs) in enumerate(split_parts):
                    dve.wait_ge(hi_done, m + 1)
                    V.tensor_tensor(g.h_lo[:, ks, cs], g.merged[:, ks, cs], g.h_hi[:, ks, cs].bitcast(F32),
                                    ALU.subtract).then_inc(lo_done, 1)
                dve.wait_ge(gain_in, 16)
                for u, (s, i) in enumerate(units):
                    r, c = rows(i), slice(s * 256, (s + 1) * 256)
                    dve.wait_ge(squared, u + 1)
                    V.tensor_tensor(o_all[0:r, i, c], g.ps[0:r, u % NB, 0:256], gain[0:r, c], ALU.mult).then_inc(kept, 1)
                    if s < NSL - 1:
                        continue
                    V.tensor_reduce(ss[0:r, i:i + 1], parts[0:r, i, :], AX.X, ALU.add).then_inc(sum1, 1)
                    if i >= 3:
                        second_norm(i - 3)
                    if i >= 1:
                        new_x(i - 1)
                    if i == N_TILE - 1:
                        second_norm(i - 2)
                        new_x(i)
                        second_norm(i - 1)
                        second_norm(i)
                    for v in group_turns(i):
                        k, c0, n, bank = turned(v)
                        dve.wait_ge(t_hi, v + 1)
                        V.scalar_tensor_tensor(out=g.h_lo[:, k, c0:c0 + n], in0=bank, scalar=g.gains[:, 2, k:k + 1],
                                               in1=g.h_hi[:, k, c0:c0 + n].bitcast(F32),
                                               op0=ALU.mult, op1=ALU.subtract).then_inc(t_lo, 1)



FF_G = 512
FK = FF_G // P


def block_ffn(g):
    nc, io = g.nc, g.io
    n0 = g.slab
    N_GRP = D_FF // FF_G
    g.slab += 4 * N_GRP
    assert n0 % 2 == 0
    w_up, w_down = io["w_up"][0], io["w_down"][0]
    acc = g.big[:].rearrange("p (i c) -> p i c", c=D_MODEL)
    ups = [(f, c0, n) for f in range(FK) for c0, n in GROUPS]
    downs = [(half, i) for half in range(2) for i in range(N_TILE)]
    NU, ND = len(ups), len(downs)
    B_UP, B_DN = 4, 3
    LEAD = 4
    with ExitStack() as ctx:
        sb = lambda name, shape, dt=F32: ctx.enter_context(nc.sbuf_tensor("ff_" + name, shape, dt))
        u_hi, u_lo = sb("u_hi", [P, FK, T_PAD], F32R), sb("u_lo", [P, FK, T_PAD], F32R)
        both = sb("relu_sq", [P, 4, 384])
        relu, sq = both[:, 0:2, :], both[:, 2:4, :]
        ss, expo = sb("ss", [P, N_TILE]), sb("expo", [P, 1])
        x2 = nc.alloc_sbuf_tensor_at("ff_x2", [P, N_TILE, D_MODEL], F32, offset=g.h_at)
        gain = nc.alloc_sbuf_tensor_at("ff_gain", [P, D_MODEL], F32, offset=g.h_at + 4 * N_TILE * D_MODEL)
        junk = both[:].rearrange("p a b -> p (a b)")[:, 0:D_MODEL]
        outs = [io["y_prompt"][0, i * P:(i + 1) * P, :] for i in range(TILE_P)] + [io["y_sample"][0]]
        sem = lambda name: g.sem("ff_" + name)
        gain_in, y_squared, roots, normed, y_done, y_out = (sem(n) for n in (
            "gain_in", "y_squared", "roots", "normed", "y_done", "y_out"))
        (up_full, up_free, squared, sq_made, u_ready, dn_full, acc_done, zeroed) = (sem(n) for n in (
            "up_full", "up_free", "squared", "sq_made", "u_ready", "dn_full", "acc_done", "zeroed"))

        with nc.Block() as block:
            @block.sync
            def _(sp):
                def load(i, s):
                    n, slot = n0 + 4 * i + s, s % 2
                    sp.wait_ge(g.w_split, n - 1)
                    if s < 2:
                        src = w_up[:, bass.ds(i * FF_G + s * 256, 256)].rearrange("(k p) c -> p k c", p=P)
                        k = KT
                    else:
                        src = w_down[bass.ds(i * FF_G, FF_G), (s - 2) * 512:(s - 1) * 512].rearrange(
                            "(k p) c -> p k c", p=P)
                        k = FK
                    sp.dma_start(g.w_raw[:, slot, :].rearrange("p (k c) -> p k c", k=k), src
                                 ).then_inc(g.w_loaded[slot], 16)

                with sp.Fori(0, N_GRP - 1) as i:
                    load(i, 2)
                    load(i, 3)
                    load(i + 1, 0)
                    load(i + 1, 1)
                load(N_GRP - 1, 2)
                load(N_GRP - 1, 3)
                sp.wait_ge(up_full, N_GRP * NU)
                sp.dma_start(gain[:], io["post_ffn_gain"][0].partition_broadcast(P)).then_inc(gain_in, 16)
                for t in range(N_TILE):
                    sp.dma_start(x2[0:rows(t), t, :], g.d_x2[row_slice(t), :]).then_inc(g.arrived[t], 16)
                for t in range(N_TILE):
                    sp.wait_ge(y_done, t + 1)
                    sp.dma_start(outs[t], acc[0:rows(t), t, :]).then_inc(y_out, 16)
                sp.wait_ge(y_out, 16 * N_TILE)

            @block.gpsimd
            def _(pool):
                G = nc.gpsimd
                G.memset(expo[:], -0.5)
                G.memset(u_hi[:, :, T_ALL:T_PAD].bitcast(F32), 0.0).then_inc(zeroed, 1)
                G.memset(u_lo[:, :, T_ALL:T_PAD].bitcast(F32), 0.0).then_inc(zeroed, 1)

                def split(n, slot):
                    pool.wait_ge(g.w_rounded, n + 1)
                    G.tensor_tensor(g.w_lo[:, slot, :], g.w_raw[:, slot, :], g.w_hi[:, slot, :].bitcast(F32),
                                    ALU.subtract).then_inc(g.w_split, 1)

                with pool.Fori(0, N_GRP - 1) as i:
                    for s in range(1, 5):
                        split(n0 + 4 * i + s, s % 2)
                for s in range(1, 4):
                    split(n0 + 4 * (N_GRP - 1) + s, s % 2)
                for t in range(N_TILE):
                    v = ss[0:rows(t), t:t + 1]
                    pool.wait_ge(y_squared, t + 1)
                    G.tensor_scalar(v, v, 1.0 / D_MODEL, EPS, ALU.mult, ALU.add).then_inc(roots, 1)
                    pool.wait_ge(roots, 2 * t + 1)
                    G.tensor_tensor(v, v, expo[0:rows(t), :], ALU.pow).then_inc(roots, 1)

            @block.scalar
            def _(act):
                S = nc.scalar

                def rounded(i, s):
                    slot = s % 2
                    act.wait_ge(g.w_loaded[slot], 16 * (n0 // 2 + 2 * i + s // 2 + 1))
                    S.activation(g.w_hi[:, slot, :], g.w_raw[:, slot, :], ACT.Copy).then_inc(g.w_rounded, 1)

                def group(i, last):
                    for u, (f, c0, n) in enumerate(ups):
                        if u == 6:
                            act.wait_ge(up_full, i * NU + 6)
                            rounded(i, 2)
                        act.wait_ge(up_full, i * NU + u + 1)
                        act.wait_ge(u_ready, i * NU + u - 1 + LEAD)
                        S.activation(relu[:, u % 2, 0:n], g.ps[:, u % B_UP, 0:n], ACT.Relu).then_inc(up_free, 1)
                        act.wait_ge(up_free, i * NU + u + 1 + LEAD)
                        S.activation(u_hi[:, f, c0:c0 + n], relu[:, u % 2, 0:n], ACT.Square).then_inc(squared, 1)
                    rounded(i, 3)
                    if not last:
                        act.wait_ge(dn_full, i * ND + N_TILE)
                        rounded(i + 1, 0)
                        act.wait_ge(dn_full, i * ND + ND)
                        rounded(i + 1, 1)

                rounded(0, 1)
                with act.Fori(0, N_GRP - 1) as i:
                    group(i, False)
                group(N_GRP - 1, True)
                act.wait_ge(u_ready, N_GRP * NU + LEAD)
                for t in range(N_TILE):
                    r = rows(t)
                    act.wait_ge(acc_done, N_GRP * ND + N_TILE + t + 1)
                    if t:
                        act.wait_ge(y_squared, t)
                    S.activation(junk[0:r, :], acc[0:r, t, :], ACT.Square, accum_out=ss[0:r, t:t + 1]).then_inc(y_squared, 1)

            @block.vector
            def _(dve):
                V = nc.vector
                V.memset(sq[:, 0, 0:1], 0.0).then_inc(u_ready, LEAD)
                V.memset(sq[:, 0, 1:2], 0.0).then_inc(up_free, LEAD)
                for half, t in downs:
                    V.memset(acc[:, t, half * 512:(half + 1) * 512], 0.0).then_inc(acc_done, 1)
                dve.wait_ge(acc_done, ND)

                def group(i, after_down):
                    for u, (f, c0, n) in enumerate(ups):
                        dve.wait_ge(up_free, i * NU + u + 1 + LEAD)
                        V.tensor_tensor(sq[:, u % 2, 0:n], relu[:, u % 2, 0:n], relu[:, u % 2, 0:n],
                                        ALU.mult).then_inc(sq_made, 1)
                        dve.wait_ge(sq_made, i * NU + u + 1)
                        dve.wait_ge(squared, i * NU + u + 1)
                        V.tensor_tensor(u_lo[:, f, c0:c0 + n], sq[:, u % 2, 0:n], u_hi[:, f, c0:c0 + n].bitcast(F32),
                                        ALU.subtract).then_inc(u_ready, 1)
                    for d, (half, t) in enumerate(downs):
                        dst = acc[:, t, half * 512:(half + 1) * 512]
                        dve.wait_ge(dn_full, i * ND + d + 1)
                        dve.wait_ge(acc_done, i * ND + d + 1)
                        V.tensor_tensor(dst, dst, g.ps[:, 4 + d % B_DN, :], ALU.add).then_inc(acc_done, 1)
                        after_down(d)

                def last_norm(t):
                    r = rows(t)
                    a = acc[0:r, t, :]
                    dve.wait_ge(roots, 2 * t + 2)
                    V.scalar_tensor_tensor(out=a, in0=a, scalar=ss[0:r, t:t + 1], in1=gain[0:r, :],
                                           op0=ALU.mult, op1=ALU.mult).then_inc(normed, 1)
                    dve.wait_ge(normed, t + 1)
                    dve.wait_ge(g.arrived[t], 32)
                    V.tensor_tensor(a, a, x2[0:r, t, :], ALU.add).then_inc(y_done, 1)

                def of_last_group(d):
                    if d == N_TILE:
                        dve.wait_ge(gain_in, 16)
                    if d > N_TILE:
                        last_norm(d - N_TILE - 1)
                    if d == ND - 1:
                        last_norm(N_TILE - 1)

                with dve.Fori(0, N_GRP - 1) as i:
                    group(i, lambda d: None)
                group(N_GRP - 1, of_last_group)

            @block.tensor
            def _(pe):
                pe.wait_ge(zeroed, 2)
                x, uu = (g.h_hi, g.h_lo), (u_hi, u_lo)
                with pe.Fori(0, N_GRP) as i:
                    for u, (f, c0, n) in enumerate(ups):
                        if u % 6 == 0:
                            pe.wait_ge(g.w_split, n0 + 4 * i + u // 6 + 1)
                        pe.wait_ge(up_free, i * NU + u - B_UP + 1 + LEAD)
                        w = slab_view(g, u // 6, KT, 256)
                        fs, cs = slice((f % 2) * P, (f % 2 + 1) * P), slice(c0, c0 + n)
                        three_products(pe, g.ps[:, u % B_UP, 0:n], lambda a, k: w[a][:, k, fs],
                                       lambda b, k: x[b][:, k, cs], KT).then_inc(up_full, 1)
                    for d, (half, t) in enumerate(downs):
                        if half == 0 and t % 3 == 0:
                            pe.wait_ge(u_ready, i * NU + NU - 2 + t // 3 + LEAD)
                        if t == 0:
                            pe.wait_ge(g.w_split, n0 + 4 * i + 3 + half)
                        pe.wait_ge(acc_done, i * ND + d - B_DN + 1 + ND)
                        w, c = slab_view(g, half, FK, 512), slice(t * P, (t + 1) * P)
                        three_products(pe, g.ps[:, 4 + d % B_DN, :], lambda a, k: uu[a][:, k, c],
                                       lambda b, k: w[b][:, k, :], FK).then_inc(dn_full, 1)



_INS = ["x_prompt", "x_sample", "cache_k", "cache_v", "cache_idx_k", "state_hgrn", "cache_mem_k", "cache_mem_v",
        "mem_prompt", "w_in", "w_mem_kv", "mem_norm_gain", "hgrn_lb_logits", "hgrn_norm_gain", "w_out_a", "w_out_b",
        "w_out_c", "w_out", "pre_mix_gain", "post_mix_gain", "pre_ffn_gain", "post_ffn_gain", "w_up", "w_down"]
_OUTS = [("y_prompt", (1, SEQ, D_MODEL)), ("y_sample", (1, DEC, D_MODEL)),
         ("new_k_prompt", (1, 1, SEQ, A_KV, HD)), ("new_v_prompt", (1, 1, SEQ, A_KV, HD)),
         ("new_idx_k_prompt", (1, 1, SEQ, IDX_D)), ("new_hgrn_prompt", (1, 1, B_HEADS, HD, HD)),
         ("new_mem_k_prompt", (1, 1, N_MEM, C_HEADS, HD)), ("new_mem_v_prompt", (1, 1, N_MEM, C_HEADS, HD)),
         ("new_k_sample", (1, 1, DEC, A_KV, HD)), ("new_v_sample", (1, 1, DEC, A_KV, HD)),
         ("new_idx_k_sample", (1, 1, DEC, IDX_D)), ("new_hgrn_sample", (1, 1, B_HEADS, HD, HD))]


def _constants():
    pos = np.concatenate([np.arange(SEQ), PAST + np.arange(DEC)]).astype(np.float32)
    rope = np.zeros((N_TILE * P, ROPE_W), np.float32)
    for half, c, s in ((HD // 8, OFF_COS, OFF_SIN), (IDX_D // 8, OFF_ICOS, OFF_ISIN)):
        freq = np.float32(500000.0) ** (-np.arange(half, dtype=np.float32) / np.float32(half))
        ang = pos[:, None] * freq[None, :].astype(np.float32)
        rope[:T_ALL, c:c + half], rope[:T_ALL, s:s + half] = np.cos(ang), np.sin(ang)
    s, t = np.arange(P)[:, None], np.arange(P)[None, :]
    masks = []
    for h in LEVELS:
        same = s // (2 * h) == t // (2 * h)
        masks.append(same & (s <= t) if h == 1 else same & (s % (2 * h) < h) & (t % (2 * h) >= h))
    return {"c_ident": np.eye(P, dtype=np.float32),
            "c_rope": np.ascontiguousarray(rope.reshape(N_TILE, P, ROPE_W).transpose(1, 0, 2)),
            "c_masks": np.ascontiguousarray(np.stack(masks, 1).astype(np.int32))}


def kernel(**inputs):
    import numpy as _np
    import concourse.bacc as _bacc
    from concourse import mybir as _mybir
    from concourse.bass_utils import run_bass_kernel_spmd as _run

    nc = _bacc.Bacc("TRN2", target_bir_lowering=False, num_devices=1)
    arrays = {f"in_{n}": _np.ascontiguousarray(inputs[n]) for n in _INS}
    arrays.update({f"in_{n}": a for n, a in _constants().items()})
    io = {n[3:]: nc.dram_tensor(n, a.shape, _mybir.dt.from_np(a.dtype), kind="ExternalInput").ap()
          for n, a in arrays.items()}
    for name, shape in _OUTS:
        io[name] = nc.dram_tensor(f"out_{name}", shape, _mybir.dt.float32, kind="ExternalOutput").ap()
    build(nc, io)
    r = _run(nc, [arrays], core_ids=[0])
    return tuple(r.results[0][f"out_{name}"] for name, _ in _OUTS)
```
